# Optimizing a Trainium2 kernel written in Bass

```python
import jax, jax.numpy as jnp
from jax import lax
import numpy as np

D_MODEL = 2048
BATCH = 1
SEQ = 256
DEPTH = 2

HG_WIDTH = D_MODEL // 4
MLA_WIDTH = D_MODEL // 2
RW_WIDTH = D_MODEL // 4
MIX_WIDTH = HG_WIDTH + MLA_WIDTH + RW_WIDTH

HG_HEAD_DIM = 128
HG_HEADS = HG_WIDTH // HG_HEAD_DIM
HG_CHUNK = 64

MLA_NOPE = 128
MLA_ROPE = 64
MLA_V = 128
MLA_HEADS = MLA_WIDTH // MLA_V
MLA_Q_RANK = 512
MLA_KV_RANK = 256
MLA_QK_DIM = MLA_NOPE + MLA_ROPE
ROPE_THETA = 10000.0
Q_BLOCK = 128
MASK_VALUE = -1e30

RW_HEAD = 64
RW_HEADS = RW_WIDTH // RW_HEAD
RW_W_RANK = 64
RW_A_RANK = 64
RW_V_RANK = 32
RW_G_RANK = 128
RW_GN_EPS = 64e-5
RW_SIZES = (RW_WIDTH, RW_WIDTH, RW_WIDTH, RW_W_RANK, RW_A_RANK, RW_G_RANK)
RW_IN = sum(RW_SIZES)

IN_SIZES = (HG_WIDTH, HG_WIDTH, HG_WIDTH, HG_WIDTH, MLA_Q_RANK, MLA_KV_RANK, MLA_ROPE, RW_IN)
IN_WIDTH = sum(IN_SIZES)

D_FF = ((8 * D_MODEL + 3 * 256 - 1) // (3 * 256)) * 256
RMS_EPS = 1e-6

kernel_name = "hymba_style_hgrn2_mla_rwkv7_hybrid"

def split_cols(t, sizes):
    out, start = [], 0
    for s in sizes:
        out.append(t[..., start:start + s])
        start += s
    return out

def rms_norm(x, gain):
    xf = x.astype(jnp.float32)
    y = xf * lax.rsqrt(jnp.mean(xf * xf, axis=-1, keepdims=True) + RMS_EPS)
    return (y * gain.astype(jnp.float32)).astype(x.dtype)

def rope_tables(positions):
    half = MLA_ROPE // 2
    inv_freq = ROPE_THETA ** (-jnp.arange(half, dtype=jnp.float32) / half)
    ang = positions.astype(jnp.float32)[..., None] * inv_freq
    return jnp.cos(ang), jnp.sin(ang)

def apply_rope(x, cos, sin):
    x1, x2 = jnp.split(x.astype(jnp.float32), 2, axis=-1)
    return jnp.concatenate([x1 * cos - x2 * sin, x2 * cos + x1 * sin], axis=-1).astype(x.dtype)

def hgrn2_chunkwise(q, log_f, k, v):
    B, S, H, DK = q.shape
    DV = v.shape[-1]
    nc = S // HG_CHUNK
    to_chunks = lambda t: t.reshape(B, nc, HG_CHUNK, H, t.shape[-1]).transpose(1, 0, 3, 2, 4)
    causal = jnp.tril(jnp.ones((HG_CHUNK, HG_CHUNK), dtype=bool))[:, :, None]

    def step(state, inp):
        q_c, lf_c, k_c, v_c = inp
        b = jnp.cumsum(lf_c, axis=2)
        o_inter = jnp.einsum('bhtk,bhkv->bhtv', q_c * jnp.exp(b), state)
        diff = b[:, :, :, None, :] - b[:, :, None, :, :]
        decay = jnp.where(causal, jnp.exp(jnp.where(causal, diff, 0.0)), 0.0)
        scores = jnp.einsum('bhtk,bhsk,bhtsk->bhts', q_c, k_c, decay)
        o = o_inter + jnp.einsum('bhts,bhsv->bhtv', scores, v_c)
        b_last = b[:, :, -1:, :]
        state = state * jnp.exp(b_last[:, :, 0, :, None]) + jnp.einsum(
            'bhsk,bhsv->bhkv', k_c * jnp.exp(b_last - b), v_c)
        return state, o

    s0 = jnp.zeros((B, H, DK, DV), jnp.float32)
    _, o = lax.scan(step, s0, (to_chunks(q), to_chunks(log_f), to_chunks(k), to_chunks(v)))
    return o.transpose(1, 0, 3, 2, 4).reshape(B, S, H, DV)

def hgrn2_mixer(q_raw, f_raw, i_raw, g_raw, lower_bound, out_gain):
    B, S, _ = q_raw.shape
    shp = (B, S, HG_HEADS, HG_HEAD_DIM)
    q = jax.nn.silu(q_raw.astype(jnp.float32)).reshape(shp)
    z = f_raw.astype(jnp.float32).reshape(shp)
    lb = lower_bound.astype(jnp.float32).reshape(HG_HEADS, HG_HEAD_DIM)
    log_f = jnp.log(lb + (1.0 - lb) * jax.nn.sigmoid(z))
    k = (1.0 - lb) * jax.nn.sigmoid(-z)
    v = i_raw.astype(jnp.float32).reshape(shp)
    o = hgrn2_chunkwise(q, log_f, k, v)
    o = rms_norm(o, out_gain) * jax.nn.silu(g_raw.astype(jnp.float32)).reshape(shp)
    return o.reshape(B, S, HG_WIDTH).astype(q_raw.dtype)

def causal_block_attention(q_nope, q_rope, k_nope, k_rope, v):
    B, S, H, _ = q_nope.shape
    nb = S // Q_BLOCK
    blocks = lambda t: jnp.moveaxis(t.reshape(B, nb, Q_BLOCK, *t.shape[2:]), 1, 0)
    k_idx = jnp.arange(S)
    scale = MLA_QK_DIM ** -0.5

    def one_block(args):
        qn, qr, blk = args
        s = (jnp.einsum('bqhd,bkhd->bhqk', qn, k_nope)
             + jnp.einsum('bqhd,bkd->bhqk', qr, k_rope))
        q_idx = blk * Q_BLOCK + jnp.arange(Q_BLOCK)
        s = jnp.where(k_idx[None, :] <= q_idx[:, None], s.astype(jnp.float32) * scale, MASK_VALUE)
        p = jax.nn.softmax(s, axis=-1)
        return jnp.einsum('bhqk,bkhd->bqhd', p.astype(v.dtype), v)

    out = lax.map(one_block, (blocks(q_nope), blocks(q_rope), jnp.arange(nb)))
    return jnp.moveaxis(out, 0, 1).reshape(B, S, H * v.shape[-1])

def mla_mixer(q_a, kv_a, k_rope_raw, cos, sin, q_a_gain, w_qb, kv_a_gain, w_kvb, q_gain, k_gain):
    B, S, _ = q_a.shape
    q = (rms_norm(q_a, q_a_gain) @ w_qb).reshape(B, S, MLA_HEADS, MLA_QK_DIM)
    kv = (rms_norm(kv_a, kv_a_gain) @ w_kvb).reshape(B, S, MLA_HEADS, MLA_NOPE + MLA_V)
    q_nope, q_rope = q[..., :MLA_NOPE], q[..., MLA_NOPE:]
    k_nope, v = kv[..., :MLA_NOPE], kv[..., MLA_NOPE:]
    q_nope = rms_norm(q_nope, q_gain[:MLA_NOPE])
    q_rope = rms_norm(q_rope, q_gain[MLA_NOPE:])
    k_nope = rms_norm(k_nope, k_gain[:MLA_NOPE])
    k_rope = rms_norm(k_rope_raw, k_gain[MLA_NOPE:])
    q_rope = apply_rope(q_rope, cos[:, :, None, :], sin[:, :, None, :])
    k_rope = apply_rope(k_rope, cos, sin)
    o = causal_block_attention(q_nope, q_rope, k_nope, k_rope, v)
    return o.astype(q_a.dtype)

def rwkv7_mixer(proj, mu, w0, w2, a0, a2, g2, k_k, k_a, r_k, ln_w, ln_b, v_first, v_res):
    B, S, _ = proj.shape
    p = proj.astype(jnp.float32)
    prev = jnp.pad(p, ((0, 0), (1, 0), (0, 0)))[:, :S]
    p = p + (prev - p) * mu
    r, k, v, wd, ad, gd = split_cols(p, RW_SIZES)
    w_log = -jax.nn.softplus(-(w0 + jnp.tanh(wd) @ w2)) - 0.5
    a = jax.nn.sigmoid(a0 + ad @ a2)
    g = jax.nn.sigmoid(gd) @ g2
    if v_res is None:
        v_first = v
    else:
        v0, v1, v2 = v_res
        v = v + (v_first - v) * jax.nn.sigmoid(v0 + (v @ v1) @ v2)
    heads = lambda t: t.reshape(B, S, RW_HEADS, RW_HEAD)
    kk = heads(k * k_k)
    kk = kk / jnp.maximum(jnp.sqrt(jnp.sum(kk * kk, axis=-1, keepdims=True)), 1e-12)
    k = heads(k * (1.0 + (a - 1.0) * k_a))
    r, v, a = heads(r), heads(v), heads(a)
    decay = jnp.exp(-jnp.exp(heads(w_log)))
    time_major = lambda t: jnp.moveaxis(t, 1, 0)

    def step(state, inp):
        r_t, w_t, k_t, v_t, kk_t, a_t = inp
        sa = jnp.einsum('bhvk,bhk->bhv', state, -kk_t)
        state = (state * w_t[:, :, None, :]
                 + sa[..., :, None] * (kk_t * a_t)[..., None, :]
                 + v_t[..., :, None] * k_t[..., None, :])
        return state, jnp.einsum('bhvk,bhk->bhv', state, r_t)

    s0 = jnp.zeros((B, RW_HEADS, RW_HEAD, RW_HEAD), jnp.float32)
    _, y = lax.scan(step, s0, (time_major(r), time_major(decay), time_major(k),
                               time_major(v), time_major(kk), time_major(a)))
    y = jnp.moveaxis(y, 0, 1)
    mean = jnp.mean(y, axis=-1, keepdims=True)
    var = jnp.mean(jnp.square(y - mean), axis=-1, keepdims=True)
    y = ((y - mean) * lax.rsqrt(var + RW_GN_EPS)).reshape(B, S, RW_WIDTH) * ln_w + ln_b
    bonus = (jnp.sum(r * k * r_k, axis=-1, keepdims=True) * v).reshape(B, S, RW_WIDTH)
    out = (y + bonus) * g
    return out.astype(proj.dtype), v_first

def setup_inputs(seed: int = 0) -> dict:
    key = jax.random.key(seed)
    ks = iter(jax.random.split(key, 40))
    nrm = lambda shape, scale: jax.random.normal(next(ks), shape, jnp.float32) * scale
    gain = lambda shape: 1.0 + nrm(shape, 0.02)
    L = DEPTH
    return {
        "x": nrm((BATCH, SEQ, D_MODEL), 1.0),
        "positions": jnp.arange(SEQ, dtype=jnp.int32)[None, :]
                     + jax.random.randint(next(ks), (BATCH, 1), 0, 64, dtype=jnp.int32),
        "attn_norm": gain((L, D_MODEL)),
        "w_in": nrm((L, D_MODEL, IN_WIDTH), D_MODEL ** -0.5),
        "hg_lower_bounds": nrm((L, HG_WIDTH), 0.1),
        "hg_out_norm": gain((L, HG_HEAD_DIM)),
        "mla_q_a_norm": gain((L, MLA_Q_RANK)),
        "mla_w_qb": nrm((L, MLA_Q_RANK, MLA_HEADS * MLA_QK_DIM), MLA_Q_RANK ** -0.5),
        "mla_kv_a_norm": gain((L, MLA_KV_RANK)),
        "mla_w_kvb": nrm((L, MLA_KV_RANK, MLA_HEADS * (MLA_NOPE + MLA_V)), MLA_KV_RANK ** -0.5),
        "mla_q_norm": gain((L, MLA_QK_DIM)),
        "mla_k_norm": gain((L, MLA_QK_DIM)),
        "rw_mu": jax.random.uniform(next(ks), (L, RW_IN), jnp.float32),
        "rw_w0": jax.random.uniform(next(ks), (L, RW_WIDTH), jnp.float32, -5.0, 1.0),
        "rw_w2": nrm((L, RW_W_RANK, RW_WIDTH), RW_W_RANK ** -0.5),
        "rw_a0": nrm((L, RW_WIDTH), 0.1),
        "rw_a2": nrm((L, RW_A_RANK, RW_WIDTH), RW_A_RANK ** -0.5),
        "rw_g2": nrm((L, RW_G_RANK, RW_WIDTH), RW_G_RANK ** -0.5),
        "rw_v0": nrm((L - 1, RW_WIDTH), 0.1),
        "rw_v1": nrm((L - 1, RW_WIDTH, RW_V_RANK), RW_WIDTH ** -0.5),
        "rw_v2": nrm((L - 1, RW_V_RANK, RW_WIDTH), RW_V_RANK ** -0.5),
        "rw_k_k": 0.85 + nrm((L, RW_WIDTH), 0.02),
        "rw_k_a": gain((L, RW_WIDTH)),
        "rw_r_k": nrm((L, RW_HEADS, RW_HEAD), 0.1),
        "rw_ln_w": gain((L, RW_WIDTH)),
        "rw_ln_b": nrm((L, RW_WIDTH), 0.02),
        "w_o": nrm((L, MIX_WIDTH, D_MODEL), MIX_WIDTH ** -0.5),
        "ffn_norm": gain((L, D_MODEL)),
        "w_gate_up": nrm((L, D_MODEL, 2 * D_FF), D_MODEL ** -0.5),
        "w_down": nrm((L, D_FF, D_MODEL), D_FF ** -0.5),
    }

def reference(x, positions, attn_norm, w_in, hg_lower_bounds, hg_out_norm,
              mla_q_a_norm, mla_w_qb, mla_kv_a_norm, mla_w_kvb, mla_q_norm, mla_k_norm,
              rw_mu, rw_w0, rw_w2, rw_a0, rw_a2, rw_g2, rw_v0, rw_v1, rw_v2,
              rw_k_k, rw_k_a, rw_r_k, rw_ln_w, rw_ln_b,
              w_o, ffn_norm, w_gate_up, w_down):
    lb_sm = jax.nn.softmax(hg_lower_bounds.astype(jnp.float32), axis=0)
    lower_bounds = jnp.cumsum(lb_sm, axis=0) - lb_sm[0]
    cos, sin = rope_tables(positions)
    v_first = None
    for l in range(DEPTH):
        h = rms_norm(x, attn_norm[l])
        p = h @ w_in[l]
        hq, hf, hi, hg, mq, mkv, mkr, rw = split_cols(p, IN_SIZES)
        o_hg = hgrn2_mixer(hq, hf, hi, hg, lower_bounds[l], hg_out_norm[l])
        o_mla = mla_mixer(mq, mkv, mkr, cos, sin, mla_q_a_norm[l], mla_w_qb[l],
                          mla_kv_a_norm[l], mla_w_kvb[l], mla_q_norm[l], mla_k_norm[l])
        v_res = None if l == 0 else (rw_v0[l - 1], rw_v1[l - 1], rw_v2[l - 1])
        o_rw, v_first = rwkv7_mixer(rw, rw_mu[l], rw_w0[l], rw_w2[l], rw_a0[l], rw_a2[l], rw_g2[l],
                                    rw_k_k[l], rw_k_a[l], rw_r_k[l], rw_ln_w[l], rw_ln_b[l],
                                    v_first, v_res)
        mixed = jnp.concatenate([o_hg, o_mla, o_rw], axis=-1)
        x = x + (mixed @ w_o[l]).astype(x.dtype)
        h = rms_norm(x, ffn_norm[l])
        gate, up = jnp.split(h @ w_gate_up[l], 2, axis=-1)
        x = x + ((jax.nn.silu(gate) * up) @ w_down[l]).astype(x.dtype)
    return x


_drawn_inputs = setup_inputs


def setup_inputs(seed=0):
    import zlib

    import numpy as np

    out = dict(_drawn_inputs(seed))
    spreads = {}
    factors = {'attn_norm': 2.686,
     'hg_lower_bounds': 21.516,
     'hg_out_norm': 6.288,
     'mla_q_a_norm': 8.0,
     'mla_kv_a_norm': 8.0,
     'mla_q_norm': 8.0,
     'mla_k_norm': 8.0,
     'rw_a0': 3.535,
     'rw_v0': 5.968,
     'rw_k_k': 150.203,
     'rw_k_a': 6.69,
     'rw_ln_w': 24.424,
     'rw_ln_b': 25.649,
     'ffn_norm': 2.826}
    for name, (base, spread) in spreads.items():
        noise = np.random.default_rng([zlib.crc32(name.encode()), seed]).standard_normal(out[name].shape)
        drawn = base * np.exp(spread * noise) if base else spread * noise
        out[name] = __import__('jax').numpy.asarray(drawn.astype(out[name].dtype))
    for name, factor in factors.items():
        out[name] = (out[name] * factor).astype(out[name].dtype)
    return out
```

```python
from contextlib import ExitStack

import numpy as np

import concourse.bass as bass
from concourse import mybir

F32 = mybir.dt.float32
F32R = mybir.dt.float32r
U32 = mybir.dt.uint32
I32 = mybir.dt.int32
ALU = mybir.AluOpType
ACT = mybir.ActivationFunctionType
AX = mybir.AxisListType

P = 128
D = 2048
SEQ = 256
TT = SEQ // P
DEPTH = 2
KT = D // P
CH = 512

HG_H = 4
MLA_H = 8
NOPE = 128
ROPE = 64
QK = NOPE + ROPE
Q_RANK = 512
KV_RANK = 256
D_FF = 5632
RW_IN = 1792
RW_F = RW_IN // P
RC = 64
NC = SEQ // RC
JC = 4 * NC
IN_W = 4672
EPS = 1e-6
GN_EPS = 64e-5
C0 = float(np.exp(np.float32(-0.5)))
MAGIC = 12582912.0
TINY = float(2.0 ** -63)

IN_CHUNKS = [(c * CH, CH) for c in range(5)] + [(2880 + c * CH, CH) for c in range(3)] + [(2560, 320), (4416, 256)]
PAIRS = [6, 5]
RAW_SLOTS = 4
HALF_RING = 4
N_IN = len(IN_CHUNKS) * 4
N_PLAIN = 8
N_O = 16
N_FFN = sum(8 * p + 4 * p for p in PAIRS)
SPLIT_PER_LAYER = N_IN + N_O + N_FFN
SLOTS_PER_LAYER = SPLIT_PER_LAYER + N_PLAIN
FFN_AT = N_IN + N_PLAIN + N_O
assert N_IN % 4 == N_PLAIN % 4 == N_O % 4 == N_FFN % 4 == 0

PARAM_COLS = dict(hg_lb=4, q_a=4, kv_a=2, gq=1, gk=1, mu=14, w0=4, a0=4, v0=4, k_k=4, k_a=4, r_k=4, ln_w=4, ln_b=4)
CONST_COLS = dict(ident=128, hg_masks=8 * 128, attn=384, reset=1024, ones2=128, idst=64, strict_lo=64,
                  strict_up=64, incl_up=64, pair_lo=64, pair_up=64, lev_lo=5 * 64, inv_freq=32)
LORA_COLS = dict(wa=512, g2=512, v1=128, v2=512)
HG_LEVELS = [0, 64, 32, 16, 8, 4, 2, 1]
RW_LEVELS = [2, 4, 8, 16, 32]


def offsets(cols):
    at, out = 0, {}
    for name, n in cols.items():
        out[name] = (at, at + n)
        at += n
    return out, at


PAR, N_PAR = offsets(PARAM_COLS)
CON, N_CON = offsets(CONST_COLS)
LOR, N_LOR = offsets(LORA_COLS)


def build(nc, stream, x_in, positions, params, consts, lora, gains, rows, out):
    with ExitStack() as ctx:
        def sb(name, shape, dt=F32, on=ctx):
            return on.enter_context(nc.sbuf_tensor(name, shape, dt))

        def sem(name):
            return ctx.enter_context(nc.semaphore(name))

        x = sb("x", [P, TT, D])
        hT_hi = sb("hT_hi", [P, KT, SEQ], F32R)
        hT_lo = sb("hT_lo", [P, KT, SEQ], F32R)
        raw = sb("raw", [P, RAW_SLOTS, 4 * CH])
        v_first = sb("v_first", [P, 4, SEQ])
        gain = sb("gain", [P, D])
        con = sb("con", [P, N_CON])
        par = sb("par", [P, DEPTH, N_PAR])
        lor = sb("lor", [P, N_LOR])
        row = sb("row", [P, 128 + 9 * ROPE])
        derived = sb("derived", [P, DEPTH, 12])
        rkb = sb("rkb", [P, 4, P])
        cs = sb("cs", [P, 2, TT, 32])
        small = sb("small", [P, 256])

        with ExitStack() as on:
            w_hi = sb("w_hi", [P, HALF_RING, 2 * CH], F32R, on)
            w_lo = sb("w_lo", [P, HALF_RING, 2 * CH], F32R, on)
            act_hi = sb("act_hi", [P, 4 * PAIRS[0], SEQ], F32R, on)
            act_lo = sb("act_lo", [P, 4 * PAIRS[0], SEQ], F32R, on)
            silu = sb("silu", [P, TT, CH], F32, on)
            act_row = sb("act_row", [P, TT, CH], F32, on)
        ARENA = 22528
        arena = sb("arena", [P, ARENA])

        def at(off, *shape):
            n = int(np.prod(shape))
            assert off + n <= ARENA
            v = arena[:, off:off + n]
            if len(shape) == 2:
                return v.rearrange("p (a b) -> p a b", b=shape[1])
            if len(shape) == 3:
                return v.rearrange("p (a b c) -> p a b c", b=shape[1], c=shape[2])
            return v

        RING_END = 8192
        hrow = at(RING_END, TT, D)
        p_rw = at(RING_END, TT, RW_IN)
        p_mla = at(RING_END + 3584, TT, 832)
        p_hg = at(RING_END + 5248, TT, 2048)
        HG_AT = RING_END + 5248 + 4096

        hg_q = at(0, 4, SEQ)
        hg_k = at(1024, 4, SEQ)
        hg_sig = at(2048, 4, SEQ)
        hg_b = at(3072, 4, SEQ)
        hg_e = [at(4096, 4, SEQ), at(5120, 4, SEQ)]
        hg_kend = at(6144, 4, SEQ)
        hg_qbeg = at(7168, 4, SEQ)
        hg_gate = at(HG_AT, TT, CH)
        hg_diag = at(HG_AT + 1024, 8, P)
        hg_cross = at(HG_AT + 2048, 4, P)
        hg_k128 = at(HG_AT + 2560, 4, P)
        hg_q128 = at(HG_AT + 3072, 4, P)
        hg_o = at(HG_AT + 3584, TT, CH)
        hg_sq = hg_sig

        qrow = at(0, TT, MLA_H * QK)
        kvrow = at(3072, TT, MLA_H * 2 * NOPE)
        qaT = at(7168, 4, SEQ)
        MB = RING_END + 5248
        kvaT = at(MB, 2, SEQ)
        mla_sq = at(MB + 512, 3072)
        scores = at(MB + 512, MLA_H, 384)
        qnT = at(MB + 3584, MLA_H, SEQ)
        knT = at(MB + 5632, MLA_H, SEQ)
        k_sq = at(MB + 5632, TT * MLA_H, NOPE)
        ro = at(MB + 7680, TT, 640)
        probsT = at(0, MLA_H, 384)
        rT = at(7168, 4, SEQ)
        rkT = kvaT[:, 0, :]
        rb = gain[:, 0:1280].rearrange("p (t n) -> p t n", t=TT)
        rtmp = gain[:, 1280:1280 + 576].rearrange("p (t h n) -> p t h n", t=TT, h=9)

        pT = at(0, RW_F, SEQ + 1)
        v_st = at(0, JC, RC)
        b_st = at(1024, JC, RC)
        k_st = at(2048, JC, RC)
        pm = at(3600, RW_F, SEQ)
        rw_r, rw_k, rw_v = pm[:, 0:4, :], pm[:, 4:8, :], pm[:, 8:12, :]
        rw_sig = at(7184, 256)
        mab = at(8192, JC, RC)
        mab_t = at(9216, JC, RC)
        mak_t = at(10240, JC, RC)
        RB = 11776
        rw_w = at(RB, 4, SEQ)
        rw_a = at(RB + 1024, 4, SEQ)
        rw_g = at(RB + 2048, 4, SEQ)
        rw_kk = at(RB + 3072, 4, SEQ)
        rw_b = at(RB + 4096, 4, SEQ)
        rw_e = [at(RB + 5120, 4, SEQ), at(RB + 6144, 4, SEQ), at(RB + 7168, 4, SEQ)]
        rw_bonus = at(RB + 8192, 4, SEQ)
        rw_tmp = at(RB + 9216, 4, SEQ)
        mrb_t = at(RB, JC, RC)
        inv = at(RB + 4096, JC, RC)
        inv_t = at(RB + 5120, JC, RC)
        g_t = at(RB + 6144, JC, RC)
        b_lev = at(RB + 7168, JC, RC)
        mrk_t = at(RB + 9216, JC, RC)
        rhs = at(8192, 4, RC)
        sa = at(8192 + 256, 4, RC)
        state = [at(8192 + 512, 4, RC), at(8192 + 768, 4, RC)]
        yc = at(9216, JC, RC)
        ysq = at(RB + 6144, JC, RC)

        psum = ctx.enter_context(nc.psum_tensor("psum", [P, 8, CH], F32))

        def bank(b, n=1):
            return psum[:, b:b + n, :].rearrange("p a b -> p (a b)")

        def C(name):
            return con[:, CON[name][0]:CON[name][1]]

        ident = C("ident")
        idst = C("idst")
        hg_masks = C("hg_masks").rearrange("p (l t) -> p l t", t=P)
        lev_lo = C("lev_lo").rearrange("p (l t) -> p l t", t=RC)

        def par_of(l, name):
            return par[:, l, PAR[name][0]:PAR[name][1]]

        def lora_of(name):
            return lor[:, LOR[name][0]:LOR[name][1]]

        def over(v, n, m):
            return v.unsqueeze(1).broadcast_to([P, n, m])

        def along(v, m):
            return v.unsqueeze(2).broadcast_to([P, v.shape[1], m])

        raw_in = [sem(f"raw_in{s}") for s in range(RAW_SLOTS)]
        x_in_sem, con_in, par_in, row_in, lora_in, pos_in = (sem(n) for n in (
            "x_loaded", "consts_loaded", "params_loaded", "rows_loaded", "lora_loaded", "positions_loaded"))
        gain_in = sem("gain_loaded")
        out_done = sem("out_stored")
        hi_done, lo_done = sem("w_hi_written"), sem("w_lo_written")
        half_used = sem("half_used")
        plain_used = sem("plain_slot_used")
        acc_free = [sem("acc_even_free"), sem("acc_odd_free")]
        x_updated = sem("x_updated")
        names = {}

        def S(name):
            if name not in names:
                names[name] = sem(name)
            return names[name]

        block = ctx.enter_context(nc.Block())

        def chunk_ends(s4, j):
            return s4 * 8 + (2 * j + HALF_RING)

        @block.sync
        def _(sp):
            sp.dma_start(x[:, :, :], x_in.rearrange("(t p) d -> p t d", p=P)).then_inc(x_in_sem, 16)
            for l in range(DEPTH):
                g0, s0 = l * SLOTS_PER_LAYER, l * SPLIT_PER_LAYER
                for j in range(FFN_AT):
                    if j < N_IN + 4:
                        if l or j >= 4:
                            sp.wait_ge(lo_done, 2 * (s0 + j - 3))
                    elif j < N_IN + N_PLAIN + 4:
                        sp.wait_ge(plain_used, N_PLAIN * l + j - N_IN - 3)
                    else:
                        sp.wait_ge(lo_done, 2 * (s0 + j - N_PLAIN - 3))
                    n = 4 * (IN_CHUNKS[j // 4][1] if j < N_IN else 384 if j < N_IN + 4
                             else 256 if j < N_IN + N_PLAIN else CH)
                    sp.dma_start(raw[:, j % 4, 0:n], stream[g0 + j, :, 0:n]).then_inc(raw_in[j % 4], 16)
                with sp.Fori(0, N_FFN // 4) as i:
                    for j in range(4):
                        sp.wait_ge(lo_done, i * 8 + 2 * (s0 + N_IN + N_O + j - 3))
                        sp.dma_start(raw[:, j, :],
                                     stream[bass.ds(i * 4 + (g0 + FFN_AT + j), 1), :, :].rearrange(
                                         "o p n -> (o p) n")).then_inc(raw_in[j], 16)
            sp.wait_ge(x_updated, 2 * DEPTH)
            sp.dma_start(out.rearrange("(t p) d -> p t d", p=P), x[:, :, :]).then_inc(out_done, 16)
            sp.wait_ge(out_done, 16)

        @block.gpsimd
        def _(pool):
            pool.dma_start(con[:, :], consts).then_inc(con_in, 16)
            pool.dma_start(gain[:, :], gains[0:1, :].broadcast_to([P, D])).then_inc(gain_in, 16)
            pool.dma_start(par[:, :, :], params.rearrange("p (l n) -> p l n", l=DEPTH)).then_inc(par_in, 16)
            pool.dma_start(small[:, 200:202].bitcast(I32), positions).then_inc(pos_in, 16)
            for l in range(DEPTH):
                if l:
                    pool.wait_ge(S("hg_gate_ready"), l)
                    pool.wait_ge(S("rw_mix_lo"), l)
                    pool.wait_ge(S("hrow_ready"), 4 * l)
                    pool.dma_start(gain[:, :], gains[2 * l:2 * l + 1, :].broadcast_to([P, D])).then_inc(gain_in, 16)
                pool.dma_start(row[:, :], rows[l:l + 1, :].broadcast_to([P, 128 + 9 * ROPE])).then_inc(row_in, 16)
                pool.dma_start(lor[:, :], lora[l, :, :]).then_inc(lora_in, 16)
                pool.wait_ge(S("mla_rope_done"), l + 1)
                pool.dma_start(gain[:, :], gains[2 * l + 1:2 * l + 2, :].broadcast_to([P, D])).then_inc(gain_in, 16)

        @block.scalar
        def _(act):
            def chained(ins, s, value):
                ins.then_inc(s, 1)
                act.wait_ge(s, value)

            def split_hi(g4, s4, j, w=CH):
                act.wait_ge(raw_in[j % 4], g4 * 16 + 16 * (j // 4 + 1))
                for hf in range(2):
                    q = 2 * j + hf
                    act.wait_ge(half_used, s4 * 8 + (q + 1))
                    nc.scalar.activation(w_hi[:, q % HALF_RING, 0:2 * w], raw[:, j % 4, hf * 2 * w:(hf + 1) * 2 * w],
                                         ACT.Copy).then_inc(hi_done, 1)

            def norm(n):
                act.wait_ge(x_in_sem, 16)
                if n:
                    act.wait_ge(x_updated, n)
                for t in range(TT):
                    nc.scalar.activation(hrow[:, t, :], x[:, t, :], ACT.Square,
                                         accum_out=small[:, t:t + 1]).then_inc(S("x_squares"), 1)
                act.wait_ge(S("x_var"), n + 1)
                nc.scalar.activation(small[:, 4:6], small[:, 2:4], ACT.Sqrt).then_inc(S("x_std"), 1)
                for g in range(8):
                    act.wait_ge(S("norm_turned"), 8 * n + g + 1)
                    nc.scalar.activation(hT_hi[:, 2 * g:2 * g + 2, :], bank(g).rearrange("p (k t) -> p k t", k=2),
                                         ACT.Copy).then_inc(S("hT_hi_ready"), 1)

            for k in range(2):
                act.wait_ge(S("angle_ready"), k + 1)
                nc.scalar.activation(cs[:, k, :, :], small[:, 64 * k + 8:64 * k + 72].rearrange(
                    "p (t n) -> p t n", t=TT), ACT.Sin).then_inc(S("cs_ready"), 1)
            act.wait_ge(S("lb_shifted"), 1)
            nc.scalar.activation(small[:, 144:152], small[:, 144:152], ACT.Exp).then_inc(S("lb_exp"), 1)

            for l in range(DEPTH):
                ev = l + 1
                g4, s4 = l * SLOTS_PER_LAYER // 4, l * SPLIT_PER_LAYER // 4
                norm(2 * l)
                for j in range(N_IN):
                    split_hi(g4, s4, j, IN_CHUNKS[j // 4][1])

                act.wait_ge(S("p_ready"), len(IN_CHUNKS) * ev)
                nc.scalar.activation(hg_gate[:, :, :], p_hg[:, :, 1536:2048], ACT.Silu).then_inc(S("hg_gate_silu"), 1)
                act.wait_ge(S("hg_turned"), 2 * l + 1)
                nc.scalar.activation(hg_q.rearrange("p h t -> p (h t)"), bank(0, 2), ACT.Silu).then_inc(S("hg_q_ready"), 1)
                act.wait_ge(S("hg_turned"), 2 * l + 2)
                nc.scalar.activation(hg_sig.rearrange("p h t -> p (h t)"), bank(2, 2), ACT.Sigmoid).then_inc(S("hg_sig_ready"), 1)
                nc.scalar.activation(hg_k.rearrange("p h t -> p (h t)"), bank(2, 2), ACT.Sigmoid,
                                     scale=-1.0).then_inc(S("hg_sig_ready"), 1)
                act.wait_ge(S("hg_sig_floor"), ev)
                act.wait_ge(S("derived_ready"), 1)
                for h in range(HG_H):
                    nc.scalar.activation(hg_b[:, h, :], hg_sig[:, h, :], ACT.Ln, bias=derived[:, l, h:h + 1],
                                         scale=derived[:, l, 4 + h:5 + h]).then_inc(S("hg_logf"), 1)
                for k in range(8):
                    act.wait_ge(S("hg_exponent"), 8 * l + k + 1)
                    if k < 2:
                        dst = (hg_kend, hg_qbeg)[k]
                    else:
                        dst = hg_e[k % 2]
                    src = hg_b if k == 1 else dst
                    nc.scalar.activation(dst, src, ACT.Exp).then_inc(S("hg_exp"), 1)
                    if k == 0:
                        nc.scalar.activation(small[:, 160:176].rearrange("p (h c) -> p h c", h=4),
                                             hg_b.rearrange("p h (c i) -> p h c i", i=64)[:, :, :, 63],
                                             ACT.Exp).then_inc(S("hg_total_exp"), 1)
                act.wait_ge(S("hg_cross_mm"), ev)
                nc.scalar.activation(hg_cross.rearrange("p h t -> p (h t)"), bank(0), ACT.Copy).then_inc(S("hg_cross_ready"), 1)
                act.wait_ge(S("hg_o_mm"), ev)
                nc.scalar.activation(hg_sq.rearrange("p h t -> p (h t)"), bank(0, 2), ACT.Square).then_inc(S("hg_squares"), 1)
                act.wait_ge(S("hg_var"), ev)
                nc.scalar.activation(small[:, 192:200], small[:, 184:192], ACT.Sqrt).then_inc(S("hg_std"), 1)
                act.wait_ge(S("hg_o_turned"), ev)
                nc.scalar.activation(hT_hi[:, 0:4, :], bank(2, 2).rearrange("p (h t) -> p h t", h=4),
                                     ACT.Copy).then_inc(S("hg_mix_hi"), 1)

                spans = ((0, 512), (512, 768), (768, 832))
                for k, (a, b) in enumerate(spans):
                    for t in range(TT):
                        nc.scalar.activation(hg_e[0].rearrange("p h t -> p (h t)")[:, 0:b - a], p_mla[:, t, a:b], ACT.Square,
                                             accum_out=small[:, 8 + 2 * k + t:9 + 2 * k + t]).then_inc(S("mla_in_squares"), 1)
                        act.wait_ge(S("mla_in_squares"), 6 * l + 2 * k + t + 1)
                act.wait_ge(S("mla_in_var"), ev)
                nc.scalar.activation(small[:, 24:30], small[:, 16:22], ACT.Sqrt).then_inc(S("mla_in_std"), 1)
                act.wait_ge(S("mla_in_turned"), ev)
                act.wait_ge(S("hg_o_used"), ev)
                for k in range(6):
                    dst = qaT[:, k, :] if k < 4 else kvaT[:, k - 4, :]
                    g = par_of(l, "q_a")[:, k:k + 1] if k < 4 else par_of(l, "kv_a")[:, k - 4:k - 3]
                    nc.scalar.activation(dst, bank(0, 3)[:, k * SEQ:(k + 1) * SEQ], ACT.Copy,
                                         scale=g).then_inc(S("mla_inT_ready"), 1)
                for c in range(8):
                    act.wait_ge(S("mla_up_mm"), 8 * l + c + 1)
                    b0 = (4 + 2 * c) % 8
                    w = 384 if c < 4 else CH
                    dst = qrow[:, :, c * 384:(c + 1) * 384] if c < 4 else kvrow[:, :, (c - 4) * CH:(c - 3) * CH]
                    nc.scalar.activation(dst, psum[:, b0:b0 + 2, 0:w], ACT.Copy).then_inc(S("mla_up_ready"), 1)
                    if c == 3:
                        act.wait_ge(S("mla_up_ready"), 8 * l + 4)
                        nc.scalar.activation(mla_sq[:, :], qrow.rearrange("p t n -> p (t n)"), ACT.Square).then_inc(
                            S("mla_q_squares"), 1)
                act.wait_ge(S("mla_up_ready"), 8 * ev)
                nc.scalar.activation(k_sq.rearrange("p (t h) n -> p t h n", t=TT),
                                     kvrow.rearrange("p t (h n) -> p t h n", n=256)[:, :, :, 0:NOPE],
                                     ACT.Square).then_inc(S("mla_k_squares"), 1)
                act.wait_ge(S("mla_var"), ev)
                nc.scalar.activation(small[:, 80:128], small[:, 32:80], ACT.Sqrt).then_inc(S("mla_std"), 1)
                act.wait_ge(S("mla_q_turned"), ev)
                nc.scalar.activation(qnT.rearrange("p h t -> p (h t)"), bank(0, 4), ACT.Copy,
                                     scale=par_of(l, "gq")).then_inc(S("mla_qT_ready"), 1)
                act.wait_ge(S("mla_r_turned"), ev)
                nc.scalar.activation(rT.rearrange("p h t -> p (h t)"), bank(0, 2), ACT.Copy).then_inc(S("mla_rT_ready"), 1)
                nc.scalar.activation(rkT, bank(2)[:, 0:SEQ], ACT.Copy).then_inc(S("mla_rT_ready"), 1)
                act.wait_ge(S("mla_shifted"), ev)
                nc.scalar.activation(scores[:, :, :], scores[:, :, :], ACT.Exp).then_inc(S("mla_exp"), 1)
                for k in range(2):
                    act.wait_ge(S("mla_p_turned"), 8 * l + 4 * k + 4)
                    nc.scalar.activation(probsT[:, 4 * k:4 * k + 4, :], psum[:, 4 * k:4 * k + 4, 0:384],
                                         ACT.Copy).then_inc(S("mla_pT_ready"), 1)
                act.wait_ge(S("mla_o_mm"), ev)
                nc.scalar.activation(hT_hi[:, 4:12, :], bank(0, 4).rearrange("p (h t) -> p h t", h=8),
                                     ACT.Copy).then_inc(S("mla_mix_hi"), 1)

                act.wait_ge(S("mla_mix_lo"), ev)
                act.wait_ge(S("rw_turned"), 2 * l + 1)
                nc.scalar.activation(pT[:, 0:8, 1:SEQ + 1], bank(4, 4).rearrange("p (f t) -> p f t", f=8),
                                     ACT.Copy).then_inc(S("rw_pT_ready"), 1)
                act.wait_ge(S("rw_turned"), 2 * l + 2)
                nc.scalar.activation(pT[:, 8:14, 1:SEQ + 1], bank(0, 3).rearrange("p (f t) -> p f t", f=6),
                                     ACT.Copy).then_inc(S("rw_pT_ready"), 1)
                act.wait_ge(S("rw_shifted"), ev)
                nc.scalar.activation(rw_sig[0:64, :], pm[0:64, 12, :], ACT.Tanh).then_inc(S("rw_lora_in"), 1)
                nc.scalar.activation(rw_tmp[:, 0, :], pm[:, 13, :], ACT.Sigmoid).then_inc(S("rw_lora_in"), 1)
                act.wait_ge(S("rw_lora_mm"), 3 * l + 1)
                for j in range(4):
                    nc.scalar.activation(rw_w[:, j, :], bank(0, 2)[:, j * SEQ:(j + 1) * SEQ], ACT.Sigmoid,
                                         bias=par_of(l, "w0")[:, j:j + 1]).then_inc(S("rw_w_ready"), 1)
                act.wait_ge(S("rw_lora_mm"), 3 * l + 2)
                for j in range(4):
                    nc.scalar.activation(rw_a[:, j, :], bank(2, 2)[:, j * SEQ:(j + 1) * SEQ], ACT.Sigmoid,
                                         bias=par_of(l, "a0")[:, j:j + 1]).then_inc(S("rw_a_ready"), 1)
                act.wait_ge(S("rw_lora_mm"), 3 * l + 3)
                nc.scalar.activation(rw_g.rearrange("p j t -> p (j t)"), bank(4, 2), ACT.Copy).then_inc(S("rw_g_ready"), 1)
                if l:
                    act.wait_ge(S("rw_v1_mm"), l)
                    nc.scalar.activation(rw_bonus[0:32, 0, :], bank(6)[0:32, 0:SEQ], ACT.Copy).then_inc(S("rw_v1_ready"), 1)
                    act.wait_ge(S("rw_v2_mm"), l)
                    for j in range(4):
                        nc.scalar.activation(rw_e[0][:, j, :], bank(6, 2)[:, j * SEQ:(j + 1) * SEQ], ACT.Sigmoid,
                                             bias=par_of(l, "v0")[:, j:j + 1]).then_inc(S("rw_vmix_ready"), 1)
                act.wait_ge(S("rw_kk_mm"), ev)
                nc.scalar.activation(rw_e[1].rearrange("p j t -> p (j t)"), bank(0, 2), ACT.Sqrt).then_inc(S("rw_kk_norm"), 1)
                act.wait_ge(S("rw_exponent"), 3 * l + 1)
                nc.scalar.activation(rw_e[0], rw_b, ACT.Exp, scale=-C0).then_inc(S("rw_exp"), 1)
                nc.scalar.activation(rw_e[1], rw_b, ACT.Exp, scale=C0).then_inc(S("rw_exp"), 1)
                act.wait_ge(S("rw_exponent"), 3 * l + 2)
                nc.scalar.activation(small[:, 48:64], small[:, 32:48], ACT.Exp, scale=-C0).then_inc(S("rw_half_decay"), 1)
                act.wait_ge(S("rw_exponent"), 3 * l + 3)
                nc.scalar.activation(rw_e[2], rw_e[2], ACT.Exp, scale=-C0).then_inc(S("rw_exp"), 1)
                for k, dst in enumerate((v_st, b_st, k_st)):
                    act.wait_ge(S("rw_stack_mm"), 3 * l + k + 1)
                    nc.scalar.activation(dst.rearrange("p a b -> p (a b)"), bank(2 * k, 2), ACT.Copy).then_inc(
                        S("rw_stacked"), 1)
                for k in range(len(RW_LEVELS)):
                    for hf in range(2):
                        act.wait_ge(S("rw_gt_mm"), 10 * l + 2 * k + hf + 1)
                        nc.scalar.activation(g_t[:, 8 * hf:8 * hf + 8, :].rearrange("p a b -> p (a b)"), bank(hf),
                                             ACT.Copy).then_inc(S("rw_gt_ready"), 1)
                for c in range(NC):
                    act.wait_ge(S("rw_sa_mm"), NC * l + c + 1)
                    nc.scalar.activation(sa.rearrange("p a b -> p (a b)"), bank(1)[:, 0:256], ACT.Copy).then_inc(
                        S("rw_sa_ready"), 1)
                act.wait_ge(S("rw_y_centred"), ev)
                nc.scalar.activation(ysq, yc, ACT.Square).then_inc(S("rw_y_squares"), 1)
                act.wait_ge(S("rw_y_var"), ev)
                nc.scalar.activation(small[:, 112:128], small[:, 96:112], ACT.Sqrt).then_inc(S("rw_y_std"), 1)
                act.wait_ge(S("rw_out"), ev)
                nc.scalar.activation(hT_hi[:, 12:16, :], rw_e[1], ACT.Copy).then_inc(S("rw_mix_hi"), 1)

                act.wait_ge(S("rw_mix_lo"), ev)
                s4o, g4o = s4 + N_IN // 4, g4 + (N_IN + N_PLAIN) // 4
                for j in range(N_O):
                    split_hi(g4o, s4o, j)
                norm(2 * l + 1)

                g4f, s4f = g4o + N_O // 4, s4o + N_O // 4
                pair0 = sum(PAIRS) * l
                for pairs in PAIRS:
                    def pair(i, first):
                        gi, si = i * 2 + g4f, i * 2 + s4f
                        for j in range(8):
                            if j == 6:
                                act.wait_ge(half_used, chunk_ends(si, 4))
                                if not (first and pair0 == 0):
                                    act.wait_ge(S("act_row_ready"), i + pair0)
                                nc.scalar.activation(silu[:, :, :], psum[:, 0:2, :], ACT.Silu).then_inc(acc_free[0], 1)
                                if not first:
                                    turned_hi(i - 1, pair0)
                            split_hi(gi, si, j)

                    def turned_hi(i, p0):
                        act.wait_ge(S("act_turned"), i + (p0 + 1))
                        dst = act_hi[:, bass.ds(i * 4, 4), :] if not isinstance(i, int) else act_hi[:, 4 * i:4 * i + 4, :]
                        nc.scalar.activation(dst, bank(4, 2).rearrange("p (k t) -> p k t", k=4),
                                             ACT.Copy).then_inc(S("act_hi_ready"), 1)

                    pair(0, True)
                    with act.Fori(1, pairs) as i:
                        pair(i, False)
                    g4f, s4f = g4f + 2 * pairs, s4f + 2 * pairs
                    for j in range(4 * pairs):
                        split_hi(g4f, s4f, j)
                        if j == 3:
                            turned_hi(pairs - 1, pair0)
                    g4f, s4f = g4f + pairs, s4f + pairs
                    pair0 += pairs

        @block.vector
        def _(dve):
            steps = [0]
            chain = sem("dve_steps")

            def v(ins):
                steps[0] += 1
                ins.then_inc(chain, 1)
                dve.wait_ge(chain, steps[0])

            def vs(ins, name, value):
                ins.then_inc(S(name), 1)
                dve.wait_ge(S(name), value)

            tt, ts, stt = nc.vector.tensor_tensor, nc.vector.tensor_scalar, nc.vector.scalar_tensor_tensor
            red, rec, cp = nc.vector.tensor_reduce, nc.vector.reciprocal, nc.vector.tensor_copy
            ADD, SUB, MUL, MAX = ALU.add, ALU.subtract, ALU.mult, ALU.max

            def split_lo(s4, j, w=CH):
                for hf in range(2):
                    q = 2 * j + hf
                    dve.wait_ge(hi_done, s4 * 8 + (q + 1))
                    tt(w_lo[:, q % HALF_RING, 0:2 * w], raw[:, j % 4, hf * 2 * w:(hf + 1) * 2 * w],
                       w_hi[:, q % HALF_RING, 0:2 * w].bitcast(F32), SUB).then_inc(lo_done, 1)

            def norm(n):
                dve.wait_ge(S("x_squares"), 2 * n + 2)
                vs(ts(small[:, 2:4], small[:, 0:2], 1.0 / D, EPS, MUL, ADD), "x_var", n + 1)
                dve.wait_ge(S("x_std"), n + 1)
                v(rec(small[:, 6:8], small[:, 4:6]))
                dve.wait_ge(gain_in, 16 * (n + 1))
                for t in range(TT):
                    vs(stt(hrow[:, t, :], x[:, t, :], small[:, 6 + t:7 + t], gain[:, :], MUL, MUL),
                       "hrow_ready", 2 * n + t + 1)
                for g in range(8):
                    dve.wait_ge(S("hT_hi_ready"), 8 * n + g + 1)
                    tt(hT_lo[:, 2 * g:2 * g + 2, :], bank(g).rearrange("p (k t) -> p k t", k=2),
                       hT_hi[:, 2 * g:2 * g + 2, :].bitcast(F32), SUB).then_inc(S("hT_ready"), 1)

            dve.wait_ge(pos_in, 16)
            dve.wait_ge(con_in, 16)
            v(cp(small[:, 202:204], small[:, 200:202].bitcast(I32)))
            ang = small[:, 72:136].rearrange("p (t n) -> p t n", t=TT)
            co = small[:, 8:72]
            turns = arena[:, RING_END + 4096:RING_END + 4096 + 64]
            for t in range(TT):
                v(ts(ang[:, t, :], C("inv_freq"), small[:, 202 + t:203 + t], None, MUL))
            ang = small[:, 72:136]
            v(ts(turns, ang, 1.0 / (2 * np.pi), MAGIC, MUL, ADD))
            v(ts(turns, turns, MAGIC, None, SUB))
            for part in (6.28125, 0.0019340515136718750, 1.2556659146e-06):
                v(stt(ang, turns, -part, ang, MUL, ADD))
            v(ts(ang, ang, 3.1415925, -3.1415925, ALU.min, MAX))
            v(stt(co, ang, -1.0, ang, MUL, MAX))
            vs(ts(co, co, -1.0, float(np.pi / 2), MUL, ADD), "angle_ready", 1)
            dve.sem_inc(S("angle_ready"), 1)
            dve.wait_ge(par_in, 16)
            lb0, lb1 = par_of(0, "hg_lb"), par_of(1, "hg_lb")
            v(tt(small[:, 136:140], lb0, lb1, MAX))
            v(tt(small[:, 144:148], lb0, small[:, 136:140], SUB))
            vs(tt(small[:, 148:152], lb1, small[:, 136:140], SUB), "lb_shifted", 1)
            dve.wait_ge(S("lb_exp"), 1)
            v(tt(small[:, 136:140], small[:, 144:148], small[:, 148:152], ADD))
            v(rec(small[:, 140:144], small[:, 136:140]))
            v(tt(small[:, 144:148], small[:, 144:148], small[:, 140:144], MUL))
            v(tt(small[:, 148:152], small[:, 148:152], small[:, 140:144], MUL))
            v(tt(derived[:, 0, 0:4], small[:, 144:148], small[:, 144:148], SUB))
            v(tt(derived[:, 1, 0:4], small[:, 144:148], small[:, 148:152], ADD))
            v(tt(derived[:, 1, 0:4], derived[:, 1, 0:4], small[:, 144:148], SUB))
            for l in range(DEPTH):
                v(ts(derived[:, l, 4:8], derived[:, l, 0:4], -1.0, 1.0, MUL, ADD))
                v(ts(derived[:, l, 8:12], par_of(l, "k_a"), -1.0, 1.0, MUL, ADD))
            dve.sem_inc(S("derived_ready"), 1)

            for l in range(DEPTH):
                ev = l + 1
                s4 = l * SPLIT_PER_LAYER // 4
                norm(2 * l)

                def store_p(c):
                    w = IN_CHUNKS[c][1]
                    dst = (p_hg[:, :, c * CH:(c + 1) * CH] if c < 4 else p_mla[:, :, 0:512] if c == 4
                           else p_rw[:, :, (c - 5) * CH:(c - 4) * CH] if c < 8
                           else p_mla[:, :, 512:832] if c == 8 else p_rw[:, :, 1536:1792])
                    dve.wait_ge(half_used, chunk_ends(s4, 4 * c + 4))
                    cp(dst, psum[:, 2 * (c % 2):2 * (c % 2) + 2, 0:w]).then_inc(acc_free[c % 2], 1)
                    dve.wait_ge(acc_free[c % 2], acc_base(l) + c // 2 + 2)
                    dve.sem_inc(S("p_ready"), 1)

                def acc_base(layer):
                    return layer * (len(IN_CHUNKS) // 2 + 2 + sum(PAIRS) + 4)

                for c in range(len(IN_CHUNKS)):
                    for j in range(4):
                        if j == 2 and c:
                            store_p(c - 1)
                        split_lo(s4, 4 * c + j, IN_CHUNKS[c][1])
                store_p(len(IN_CHUNKS) - 1)

                flat = "p h t -> p (h t)"
                dve.wait_ge(row_in, 16 * ev)
                dve.wait_ge(S("hg_gate_silu"), ev)
                vs(tt(hg_gate.rearrange("p t (h n) -> p (t h) n", n=P), hg_gate.rearrange("p t (h n) -> p (t h) n", n=P),
                      over(row[:, 0:128], 8, P), MUL), "hg_gate_ready", ev)
                v(nc.vector.memset(hg_diag[:, :, :], 0.0))
                dve.wait_ge(S("hg_sig_ready"), 2 * l + 1)
                vs(ts(hg_sig[:, :, :], hg_sig[:, :, :], TINY, None, MAX), "hg_sig_floor", ev)
                dve.wait_ge(S("hg_sig_ready"), 2 * l + 2)
                v(tt(hg_k, hg_k, along(derived[:, l, 4:8], SEQ), MUL))
                dve.wait_ge(S("hg_q_ready"), ev)
                dve.sem_inc(S("hg_qk_ready"), 1)
                dve.wait_ge(S("hg_logf"), 4 * ev)
                v(nc.vector.tensor_tensor_scan(hg_sig.rearrange(flat), C("reset"), hg_b.rearrange(flat), 0.0, MUL, ADD))
                v(cp(hg_b, hg_sig))
                b4 = hg_b.rearrange("p h (c i) -> p (h c) i", i=64)
                v(tt(hg_kend.rearrange("p h (c i) -> p (h c) i", i=64),
                     b4[:, :, 63:64].broadcast_to([P, JC, 64]), b4, SUB))
                dve.sem_inc(S("hg_exponent"), 2)

                def exponent(k):
                    m = HG_LEVELS[k]
                    if k >= 4:
                        dve.wait_ge(S("hg_level_mm"), 8 * l + k - 1)
                    e = hg_e[k % 2].rearrange("p h (n two m) -> p (h n) two m", two=2, m=m)
                    b = hg_b.rearrange("p h (n two m) -> p (h n) two m", two=2, m=m)
                    n = 1024 // (2 * m)
                    r = b[:, :, 0, m - 1:m].broadcast_to([P, n, m])
                    v(tt(e[:, :, 0, :], r, b[:, :, 0, :], SUB))
                    vs(tt(e[:, :, 1, :], b[:, :, 1, :], r, SUB), "hg_exponent", 8 * l + k + 1)

                def factors(k):
                    m = HG_LEVELS[k]
                    dve.wait_ge(S("hg_exp"), 8 * l + k + 1)
                    if k < 2:
                        dst, src = ((hg_kend, hg_k), (hg_qbeg, hg_q))[k]
                        v(tt(dst, dst, src, MUL))
                        if k == 1:
                            dve.sem_inc(S("hg_factors"), 1)
                        return
                    e, kk, qq = (z.rearrange("p h (n two m) -> p (h n) two m", two=2, m=m)
                                 for z in (hg_e[k % 2], hg_k, hg_q))
                    v(tt(e[:, :, 0, :], e[:, :, 0, :], kk[:, :, 0, :], MUL))
                    vs(tt(e[:, :, 1, :], e[:, :, 1, :], qq[:, :, 1, :], MUL), "hg_factors", 7 * l + k)

                def masked(k):
                    dve.wait_ge(S("hg_level_mm"), 8 * l + k + 1)
                    vs(nc.vector.copy_predicated(hg_diag[:, :, :], over(hg_masks[:, k, :], 8, P).bitcast(U32),
                                                 bank(4 + 2 * (k % 2), 2).rearrange("p (n t) -> p n t", n=8)),
                       "hg_masked", 8 * l + k + 1)

                exponent(2)
                factors(0)
                factors(1)
                exponent(3)
                dve.wait_ge(S("hg_total_exp"), ev)
                tot = small[:, 160:176].rearrange("p (h c) -> p h c", h=4)
                v(tt(hg_k128[:, :, 0:64], hg_kend[:, :, 0:64], tot[:, :, 1:2].broadcast_to([P, 4, 64]), MUL))
                v(cp(hg_k128[:, :, 64:128], hg_kend[:, :, 64:128]))
                v(cp(hg_q128[:, :, 0:64], hg_qbeg[:, :, 128:192]))
                v(tt(hg_q128[:, :, 64:128], hg_qbeg[:, :, 192:256], tot[:, :, 2:3].broadcast_to([P, 4, 64]), MUL))
                dve.sem_inc(S("hg_cross_factors"), 1)
                masked(0)
                masked(1)
                for k in range(2, 8):
                    factors(k)
                    if 2 <= k - 1 and k + 1 < 8 and k + 1 >= 4:
                        exponent(k + 1)
                    masked(k)
                dve.wait_ge(S("hg_squares"), ev)
                v(red(small[:, 176:184], hg_sq.rearrange("p h (d n) -> p (h d) n", n=P), AX.X, ADD))
                vs(ts(small[:, 184:192], small[:, 176:184], 1.0 / P, EPS, MUL, ADD), "hg_var", ev)
                dve.wait_ge(S("hg_std"), ev)
                v(rec(small[:, 176:184], small[:, 192:200]))
                o3, ps3 = hg_o.rearrange("p t (h n) -> p (t h) n", n=P), bank(0, 2).rearrange("p (n v) -> p n v", n=8)
                v(tt(o3, ps3, along(small[:, 176:184], P), MUL))
                vs(tt(hg_o, hg_o, hg_gate, MUL), "hg_o_ready", ev)
                dve.wait_ge(S("hg_mix_hi"), ev)
                vs(tt(hT_lo[:, 0:4, :], bank(2, 2).rearrange("p (h t) -> p h t", h=4), hT_hi[:, 0:4, :].bitcast(F32), SUB),
                   "hg_o_used", ev)

                dve.wait_ge(S("mla_in_squares"), 6 * ev)
                for k, n in enumerate((Q_RANK, KV_RANK, ROPE)):
                    v(ts(small[:, 16 + 2 * k:18 + 2 * k], small[:, 8 + 2 * k:10 + 2 * k], 1.0 / n, EPS, MUL, ADD))
                dve.sem_inc(S("mla_in_var"), 1)
                dve.wait_ge(S("mla_in_std"), ev)
                v(rec(small[:, 8:14], small[:, 24:30]))
                for t in range(TT):
                    v(ts(p_mla[:, t, 0:512], p_mla[:, t, 0:512], small[:, 8 + t:9 + t], None, MUL))
                    v(ts(p_mla[:, t, 512:768], p_mla[:, t, 512:768], small[:, 10 + t:11 + t], None, MUL))
                dve.sem_inc(S("mla_in_normed"), 1)
                for t in range(TT):
                    v(ts(rb[:, t, 512:576], p_mla[:, t, 768:832], small[:, 12 + t:13 + t], None, MUL))
                dve.wait_ge(S("mla_q_squares"), ev)
                sq3 = mla_sq.rearrange("p (n d) -> p n d", d=QK)
                v(red(small[:, 32:48], sq3[:, :, 0:NOPE], AX.X, ADD))
                v(red(small[:, 48:64], sq3[:, :, NOPE:QK], AX.X, ADD))
                dve.wait_ge(S("mla_k_squares"), ev)
                v(red(small[:, 64:80], k_sq, AX.X, ADD))
                v(ts(small[:, 32:48], small[:, 32:48], 1.0 / NOPE, EPS, MUL, ADD))
                v(ts(small[:, 48:64], small[:, 48:64], 1.0 / ROPE, EPS, MUL, ADD))
                vs(ts(small[:, 64:80], small[:, 64:80], 1.0 / NOPE, EPS, MUL, ADD), "mla_var", ev)
                dve.wait_ge(S("mla_std"), ev)
                v(rec(small[:, 32:80], small[:, 80:128]))
                q3 = qrow.rearrange("p t (h d) -> p (t h) d", d=QK)
                v(tt(q3[:, :, 0:NOPE], q3[:, :, 0:NOPE], along(small[:, 32:48], NOPE), MUL))
                dve.sem_inc(S("mla_q_normed"), 1)
                k3 = kvrow.rearrange("p t (h d) -> p (t h) d", d=256)[:, :, 0:NOPE]
                v(tt(k3, k3, along(small[:, 64:80], NOPE), MUL))
                dve.sem_inc(S("mla_k_normed"), 1)
                q4 = qrow.rearrange("p t (h d) -> p t h d", d=QK)
                rb4 = rb.rearrange("p t (h d) -> p t h d", d=ROPE)
                ro4 = ro.rearrange("p t (h d) -> p t h d", d=ROPE)
                for t in range(TT):
                    v(tt(rb4[:, t, 0:8, :], q4[:, t, :, NOPE:QK], along(small[:, 48 + 8 * t:56 + 8 * t], ROPE), MUL))
                    v(tt(rb[:, t, 0:576], rb[:, t, 0:576], row[:, 128:704], MUL))
                for t in range(TT):
                    x1, x2 = rb4[:, t, 0:9, 0:32], rb4[:, t, 0:9, 32:64]
                    co_, si_ = over(cs[:, 0, t, :], 9, 32), over(cs[:, 1, t, :], 9, 32)
                    dve.wait_ge(S("cs_ready"), 2)
                    v(tt(ro4[:, t, 0:9, 0:32], x1, co_, MUL))
                    v(tt(rtmp[:, t, :, :], x2, si_, MUL))
                    v(tt(ro4[:, t, 0:9, 0:32], ro4[:, t, 0:9, 0:32], rtmp[:, t, :, :], SUB))
                    v(tt(ro4[:, t, 0:9, 32:64], x2, co_, MUL))
                    v(tt(rtmp[:, t, :, :], x1, si_, MUL))
                    v(tt(ro4[:, t, 0:9, 32:64], ro4[:, t, 0:9, 32:64], rtmp[:, t, :, :], ADD))
                    v(cp(ro4[:, t, 9, :], ro4[:, t, 8, :]))
                dve.sem_inc(S("mla_rope_done"), 1)
                dve.wait_ge(S("mla_k_turned"), ev)
                vs(ts(knT.rearrange(flat), bank(4, 4), par_of(l, "gk"), None, MUL), "mla_kT_ready", ev)
                for k in range(2):
                    dve.wait_ge(S("mla_s_mm"), 8 * l + 4 * k + 4)
                    vs(stt(scores[:, 4 * k:4 * k + 4, :], psum[:, 4 * k:4 * k + 4, 0:384], float(QK ** -0.5),
                           over(C("attn"), 4, 384), MUL, ADD), "mla_scores_out", 2 * l + k + 1)
                s0, s1 = scores[:, :, 0:128], scores[:, :, 128:384]
                v(red(small[:, 32:40], s0, AX.X, MAX))
                v(red(small[:, 40:48], s1, AX.X, MAX))
                v(tt(s0, s0, along(small[:, 32:40], 128), SUB))
                v(tt(s1, s1, along(small[:, 40:48], 256), SUB))
                dve.sem_inc(S("mla_shifted"), 1)
                dve.wait_ge(S("mla_exp"), ev)
                v(red(small[:, 32:40], s0, AX.X, ADD))
                v(red(small[:, 40:48], s1, AX.X, ADD))
                v(rec(small[:, 48:64], small[:, 32:48]))
                v(tt(s0, s0, along(small[:, 48:56], 128), MUL))
                v(tt(s1, s1, along(small[:, 56:64], 256), MUL))
                dve.sem_inc(S("mla_probs"), 1)
                dve.wait_ge(S("mla_mix_hi"), ev)
                vs(tt(hT_lo[:, 4:12, :], bank(0, 4).rearrange("p (h t) -> p h t", h=8), hT_hi[:, 4:12, :].bitcast(F32), SUB),
                   "mla_mix_lo", ev)

                v(nc.vector.memset(pT[:, :, 0:1], 0.0))
                dve.wait_ge(S("rw_pT_ready"), 2 * ev)
                v(tt(pm, pT[:, :, 0:SEQ], pT[:, :, 1:SEQ + 1], SUB))
                for f in range(RW_F):
                    v(stt(pm[:, f, :], pm[:, f, :], par_of(l, "mu")[:, f:f + 1], pT[:, f, 1:SEQ + 1], MUL, ADD))
                dve.sem_inc(S("rw_shifted"), 1)
                v(tt(rw_kk, rw_k, along(par_of(l, "k_k"), SEQ), MUL))
                v(tt(rw_b, rw_kk, rw_kk, MUL))
                for j in range(4):
                    v(ts(rkb[:, j, :], C("ones2"), par_of(l, "r_k")[:, j:j + 1], None, MUL))
                dve.sem_inc(S("rw_kk_squares"), 1)
                if l:
                    dve.wait_ge(S("rw_vmix_ready"), 4 * l)
                    v(tt(rw_e[2], v_first[:, :, :], rw_v, SUB))
                    v(tt(rw_e[2], rw_e[2], rw_e[0], MUL))
                    v(tt(rw_v, rw_v, rw_e[2], ADD))
                else:
                    v(cp(v_first[:, :, :], rw_v))
                dve.wait_ge(S("rw_kk_norm"), ev)
                v(ts(rw_e[1], rw_e[1], 1e-12, None, MAX))
                v(rec(rw_e[1], rw_e[1]))
                v(tt(rw_kk, rw_kk, rw_e[1], MUL))
                dve.wait_ge(S("rw_a_ready"), 4 * ev)
                for j in range(4):
                    v(ts(rw_e[2][:, j, :], rw_a[:, j, :], par_of(l, "k_a")[:, j:j + 1], derived[:, l, 8 + j:9 + j], MUL, ADD))
                v(tt(rw_k, rw_k, rw_e[2], MUL))
                v(tt(rw_a, rw_a, rw_kk, MUL))
                v(tt(rw_e[2], rw_r, rw_k, MUL))
                dve.sem_inc(S("rw_rk"), 1)
                dve.wait_ge(S("rw_w_ready"), 4 * ev)
                v(nc.vector.tensor_tensor_scan(rw_b.rearrange(flat), C("reset"), rw_w.rearrange(flat), 0.0, MUL, ADD))
                b3 = rw_b.rearrange("p j (c i) -> p (j c) i", i=RC)
                v(ts(small[:, 32:48], b3[:, :, RC - 1], 0.5, None, MUL))
                v(tt(b3, b3, along(small[:, 32:48], RC), SUB))
                dve.sem_inc(S("rw_exponent"), 2)
                dve.wait_ge(S("rw_bonus_mm"), ev)
                v(tt(rw_bonus.rearrange(flat), bank(2, 2), rw_v.rearrange(flat), MUL))
                v(tt(rw_e[2], rw_b, rw_w, SUB))
                dve.sem_inc(S("rw_exponent"), 1)
                dve.wait_ge(S("rw_exp"), 3 * l + 1)
                v(tt(rw_r, rw_r, rw_e[0], MUL))
                dve.wait_ge(S("rw_exp"), 3 * l + 2)
                v(tt(rw_a, rw_a, rw_e[1], MUL))
                v(tt(rw_k, rw_k, rw_e[1], MUL))
                dve.wait_ge(S("rw_exp"), 3 * l + 3)
                v(tt(rw_kk, rw_kk, rw_e[2], MUL))
                dve.sem_inc(S("rw_factors"), 1)
                dve.wait_ge(S("rw_half_decay"), ev)
                hd = small[:, 48:64].rearrange("p (j c) -> p j c", j=4)
                md = small[:, 64:80].rearrange("p (j c) -> p j c", j=4)
                v(tt(md[:, :, 0:3], hd[:, :, 0:3], hd[:, :, 1:4], MUL))
                for k, (dst, mask) in enumerate(((mab, "strict_lo"), (mab_t, "strict_up"), (mak_t, "strict_up"),
                                                 (mrb_t, "incl_up"), (mrk_t, "incl_up"))):
                    b0 = (0, 2, 4, 6, 0)[k]
                    dve.wait_ge(S("rw_m_mm"), 5 * l + k + 1)
                    vs(tt(dst, bank(b0, 2).rearrange("p (n t) -> p n t", n=JC), over(C(mask), JC, RC), MUL),
                       "rw_m_ready", 5 * l + k + 1)
                v(tt(inv, mab, over(C("pair_lo"), JC, RC), MUL))
                v(stt(inv, inv, -1.0, over(idst, JC, RC), MUL, ADD))
                v(tt(inv_t, mab_t, over(C("pair_up"), JC, RC), MUL))
                v(stt(inv_t, inv_t, -1.0, over(idst, JC, RC), MUL, ADD))
                for k in range(len(RW_LEVELS)):
                    v(tt(b_lev, mab, over(lev_lo[:, k, :], JC, RC), MUL))
                    dve.sem_inc(S("rw_level_ready"), 1)
                    last = k == len(RW_LEVELS) - 1
                    for hf in range(2):
                        h8 = slice(8 * hf, 8 * hf + 8)
                        dve.wait_ge(S("rw_dinv_mm"), 10 * l + 2 * k + hf + 1)
                        if not last:
                            v(tt(inv[:, h8, :], inv[:, h8, :], bank(2 + hf).rearrange("p (n t) -> p n t", n=8), SUB))
                        v(tt(inv_t[:, h8, :], inv_t[:, h8, :], bank(4 + hf).rearrange("p (n t) -> p n t", n=8), SUB))
                    dve.sem_inc(S("rw_inv_ready"), 1)
                for c in range(NC):
                    dve.wait_ge(S("rw_rhs_mm"), NC * l + c + 1)
                    vs(ts(rhs.rearrange("p a b -> p (a b)"), bank(0)[:, 0:256], -1.0, None, MUL), "rw_rhs_ready", NC * l + c + 1)
                    if c < NC - 1:
                        dve.wait_ge(S("rw_state_mm"), 3 * l + c + 1)
                        st = bank(2)[:, 0:256].rearrange("p (j n) -> p j n", j=4)
                        if c == 0:
                            v(tt(state[1], st, md[:, :, 0:1].broadcast_to([P, 4, RC]), MUL))
                        else:
                            v(tt(rhs, state[c % 2], st, ADD))
                            v(tt(state[(c + 1) % 2], rhs, md[:, :, c:c + 1].broadcast_to([P, 4, RC]), MUL))
                        dve.sem_inc(S("rw_state_ready"), 1)
                dve.wait_ge(S("rw_y_mm"), ev)
                y3 = bank(6, 2).rearrange("p (n v) -> p n v", n=JC)
                v(red(small[:, 80:96], y3, AX.X, ADD))
                v(ts(small[:, 80:96], small[:, 80:96], 1.0 / RC, None, MUL))
                v(tt(yc, y3, along(small[:, 80:96], RC), SUB))
                dve.sem_inc(S("rw_y_centred"), 1)
                dve.wait_ge(S("rw_y_squares"), ev)
                v(red(small[:, 80:96], ysq, AX.X, ADD))
                vs(ts(small[:, 96:112], small[:, 80:96], 1.0 / RC, GN_EPS, MUL, ADD), "rw_y_var", ev)
                dve.wait_ge(S("rw_y_std"), ev)
                v(rec(small[:, 80:96], small[:, 112:128]))
                v(tt(yc, yc, along(small[:, 80:96], RC), MUL))
                dve.sem_inc(S("rw_y_normed"), 1)
                dve.wait_ge(S("rw_y_turned"), ev)
                for j in range(4):
                    v(ts(rw_e[1][:, j, :], bank(0, 2)[:, j * SEQ:(j + 1) * SEQ], par_of(l, "ln_w")[:, j:j + 1],
                         par_of(l, "ln_b")[:, j:j + 1], MUL, ADD))
                v(tt(rw_e[1], rw_e[1], rw_bonus, ADD))
                dve.wait_ge(S("rw_g_ready"), ev)
                v(tt(rw_e[1], rw_e[1], rw_g, MUL))
                dve.sem_inc(S("rw_out"), 1)
                dve.wait_ge(S("rw_mix_hi"), ev)
                vs(tt(hT_lo[:, 12:16, :], rw_e[1], hT_hi[:, 12:16, :].bitcast(F32), SUB), "rw_mix_lo", ev)

                s4o = s4 + N_IN // 4

                def add_x(s, j, c, b0):
                    dve.wait_ge(half_used, chunk_ends(s, j))
                    xs = x[:, :, c * CH:(c + 1) * CH]
                    tt(xs, xs, psum[:, b0:b0 + 2, :], ADD).then_inc(acc_free[b0 // 2], 1)

                for c in range(4):
                    for j in range(4):
                        if j == 2 and c:
                            add_x(s4o, 4 * c, c - 1, 2 * ((c - 1) % 2))
                        split_lo(s4o, 4 * c + j)
                add_x(s4o, 16, 3, 2)
                dve.wait_ge(acc_free[1], acc_base(l) + len(IN_CHUNKS) // 2 + 3)
                dve.wait_ge(acc_free[0], acc_base(l) + len(IN_CHUNKS) // 2 + 3)
                dve.sem_inc(x_updated, 1)
                norm(2 * l + 1)

                s4f = s4o + N_O // 4
                pair0 = sum(PAIRS) * l
                odd0 = acc_base(l) + len(IN_CHUNKS) // 2 + 2

                for n, pairs in enumerate(PAIRS):
                    def act_rows(i, si, p0):
                        dve.wait_ge(half_used, chunk_ends(si, 8))
                        dve.wait_ge(acc_free[0], i + (gate_base + 2))
                        if not isinstance(i, int) or i + p0 > 0:
                            dve.wait_ge(S("act_turned"), i + p0)
                        tt(act_row[:, :, :], psum[:, 2:4, :], silu[:, :, :], MUL).then_inc(acc_free[1], 1)
                        dve.wait_ge(acc_free[1], i + (gate_base + 2))
                        dve.sem_inc(S("act_row_ready"), 1)

                    def turned_lo(i, p0):
                        dve.wait_ge(S("act_hi_ready"), i + (p0 + 1))
                        k = bass.ds(i * 4, 4) if not isinstance(i, int) else slice(4 * i, 4 * i + 4)
                        tt(act_lo[:, k, :], bank(4, 2).rearrange("p (k t) -> p k t", k=4), act_hi[:, k, :].bitcast(F32),
                           SUB).then_inc(S("act_lo_ready"), 1)

                    gate_base = odd0 + sum(PAIRS[:n]) + 4 * n // 2

                    def pair(i, first):
                        si = i * 2 + s4f
                        for j in range(8):
                            if j == 2 and not first:
                                act_rows(i - 1, si - 2, pair0)
                            if j == 6 and not first:
                                turned_lo(i - 1, pair0)
                            split_lo(si, j)

                    pair(0, True)
                    with dve.Fori(1, pairs) as i:
                        pair(i, False)
                    last_si = s4f + 2 * (pairs - 1)
                    s4f = s4f + 2 * pairs
                    for c in range(4):
                        for j in range(pairs):
                            if j == 2 and c == 0:
                                act_rows(pairs - 1, last_si, pair0)
                            if j == 2 and c:
                                add_x(s4f, pairs * c, c - 1, 2 * ((c - 1) % 2))
                            split_lo(s4f, pairs * c + j)
                            if j == 3 and c == 0:
                                turned_lo(pairs - 1, pair0)
                    add_x(s4f, 4 * pairs, 3, 2)
                    s4f = s4f + pairs
                    pair0 += pairs
                dve.wait_ge(acc_free[1], acc_base(l + 1) + 1)
                dve.wait_ge(acc_free[0], acc_base(l + 1) + 1)
                dve.sem_inc(x_updated, 1)

        @block.tensor
        def _(pe):
            mm, tr = nc.tensor.matmul, nc.tensor.transpose
            pe.sem_inc(half_used, HALF_RING)
            pe.sem_inc(acc_free[0], 1)
            pe.sem_inc(acc_free[1], 1)

            def slots(s4, js, k0, n_k, b0, lhi, llo, w=CH):
                for n, j in enumerate(js):
                    for hf in range(2):
                        q = 2 * j + hf
                        pe.wait_ge(lo_done, s4 * 8 + (q + 1))
                        r = q % HALF_RING
                        for k2 in range(2):
                            k = k0 + 4 * n + 2 * hf + k2
                            cols = slice(k2 * w, (k2 + 1) * w)
                            for t in range(TT):
                                o = psum[:, b0 + t, 0:w]
                                a_hi, a_lo = lhi[:, k, t * P:(t + 1) * P], llo[:, k, t * P:(t + 1) * P]
                                mm(o, a_hi, w_hi[:, r, cols], start=(k == 0), stop=False)
                                mm(o, a_hi, w_lo[:, r, cols], start=False, stop=False)
                                last = mm(o, a_lo, w_hi[:, r, cols], start=False, stop=(k == n_k - 1))
                        last.then_inc(half_used, 1)

            def norm(n):
                for g in range(8):
                    for k in range(2):
                        for t in range(TT):
                            pe.wait_ge(S("hrow_ready"), 2 * n + t + 1)
                            last = tr(bank(g)[:, k * SEQ + t * P:k * SEQ + (t + 1) * P],
                                      hrow[:, t, (2 * g + k) * P:(2 * g + k + 1) * P], ident)
                    last.then_inc(S("norm_turned"), 1)
                pe.wait_ge(S("hT_ready"), 8 * (n + 1))

            def heads(fn):
                last = None
                for p0 in (0, 64):
                    last = fn(slice(p0, p0 + 64))
                return last

            pe.wait_ge(con_in, 16)
            for l in range(DEPTH):
                ev = l + 1
                s4 = l * SPLIT_PER_LAYER // 4
                acc0 = l * (len(IN_CHUNKS) // 2 + 2 + sum(PAIRS) + 4)
                norm(2 * l)
                for c, (_, w) in enumerate(IN_CHUNKS):
                    pe.wait_ge(acc_free[c % 2], acc0 + c // 2 + 1)
                    slots(s4, range(4 * c, 4 * c + 4), 0, KT, 2 * (c % 2), hT_hi, hT_lo, w)

                pe.wait_ge(S("p_ready"), len(IN_CHUNKS) * ev)
                for k in range(2):
                    for h in range(HG_H):
                        for t in range(TT):
                            last = tr(bank(2 * k, 2)[:, h * SEQ + t * P:h * SEQ + (t + 1) * P],
                                      p_hg[:, t, k * CH + h * P:k * CH + (h + 1) * P], ident)
                    last.then_inc(S("hg_turned"), 1)

                def level(k):
                    if k >= 2:
                        pe.wait_ge(S("hg_masked"), 8 * l + k - 1)
                    if k == 0:
                        pe.wait_ge(S("hg_qk_ready"), ev)
                    else:
                        pe.wait_ge(S("hg_factors"), 7 * l + k)
                    left, right = ((hg_k, hg_q) if k == 0 else (hg_kend, hg_qbeg) if k == 1 else (hg_e[k % 2],) * 2)
                    for h in range(HG_H):
                        for d in range(TT):
                            n = h * TT + d
                            last = mm(bank(4 + 2 * (k % 2), 2)[:, n * P:(n + 1) * P], left[:, h, d * P:(d + 1) * P],
                                      right[:, h, d * P:(d + 1) * P], start=True, stop=True)
                    last.then_inc(S("hg_level_mm"), 1)

                level(0)
                level(1)
                pe.wait_ge(S("hg_cross_factors"), ev)
                for h in range(HG_H):
                    last = mm(bank(0)[:, h * P:(h + 1) * P], hg_k128[:, h, :], hg_q128[:, h, :], start=True, stop=True)
                last.then_inc(S("hg_cross_mm"), 1)
                for k in range(2, 8):
                    level(k)
                pe.wait_ge(S("hg_masked"), 8 * ev)
                pe.wait_ge(S("hg_cross_ready"), ev)
                for d in range(TT):
                    for h in range(HG_H):
                        o = psum[:, d, h * P:(h + 1) * P]
                        vv = [p_hg[:, t, 1024 + h * P:1024 + (h + 1) * P] for t in range(TT)]
                        if d:
                            mm(o, hg_cross[:, h, :], vv[0], start=True, stop=False)
                        last = mm(o, hg_diag[:, h * TT + d, :], vv[d], start=(d == 0), stop=True)
                last.then_inc(S("hg_o_mm"), 1)
                pe.wait_ge(S("hg_o_ready"), ev)
                for h in range(HG_H):
                    for t in range(TT):
                        last = tr(bank(2, 2)[:, h * SEQ + t * P:h * SEQ + (t + 1) * P], hg_o[:, t, h * P:(h + 1) * P], ident)
                last.then_inc(S("hg_o_turned"), 1)

                pe.wait_ge(S("mla_in_normed"), ev)
                for k in range(6):
                    for t in range(TT):
                        last = tr(bank(0, 3)[:, k * SEQ + t * P:k * SEQ + (t + 1) * P], p_mla[:, t, k * P:(k + 1) * P], ident)
                last.then_inc(S("mla_in_turned"), 1)
                pe.wait_ge(S("mla_inT_ready"), 6 * ev)
                g4 = (l * SLOTS_PER_LAYER + N_IN) // 4
                for c in range(8):
                    if c >= 4:
                        pe.wait_ge(S("mla_up_ready"), 8 * l + c - 3)
                    pe.wait_ge(raw_in[c % 4], 16 * (g4 + c // 4 + 1))
                    w, nk, src = (384, 4, qaT) if c < 4 else (CH, 2, kvaT)
                    for t in range(TT):
                        for k in range(nk):
                            last = mm(psum[:, (4 + 2 * c) % 8 + t, 0:w], src[:, k, t * P:(t + 1) * P],
                                      raw[:, c % 4, k * w:(k + 1) * w], start=(k == 0), stop=(k == nk - 1))
                    last.then_inc(S("mla_up_mm"), 1)
                    pe.wait_ge(S("mla_up_mm"), 8 * l + c + 1)
                    pe.sem_inc(plain_used, 1)
                pe.wait_ge(S("mla_up_ready"), 8 * ev)
                for src, b0, off, width, wait, done in ((qrow, 0, 0, QK, "mla_q_normed", "mla_q_turned"),
                                                        (kvrow, 4, 0, 256, "mla_k_normed", "mla_k_turned")):
                    pe.wait_ge(S(wait), ev)
                    for h in range(MLA_H):
                        for t in range(TT):
                            last = tr(bank(b0, 4)[:, h * SEQ + t * P:h * SEQ + (t + 1) * P],
                                      src[:, t, h * width:h * width + NOPE], ident)
                    last.then_inc(S(done), 1)
                pe.wait_ge(S("mla_rope_done"), ev)
                pe.wait_ge(S("mla_qT_ready"), ev)
                for k in range(5):
                    for t in range(TT):
                        last = tr(bank(0, 3)[:, k * SEQ + t * P:k * SEQ + (t + 1) * P], ro[:, t, k * P:(k + 1) * P], ident)
                last.then_inc(S("mla_r_turned"), 1)
                pe.wait_ge(S("mla_kT_ready"), ev)
                pe.wait_ge(S("mla_rT_ready"), 2 * ev)
                for h in range(MLA_H):
                    hp = slice(64 * (h % 2), 64 * (h % 2) + 64)
                    for qt, cols, keys in ((0, slice(0, 128), 128), (1, slice(128, 384), 256)):
                        o = psum[:, h, cols]
                        tq = slice(qt * P, (qt + 1) * P)
                        mm(o, qnT[:, h, tq], knT[:, h, 0:keys], start=True, stop=False)
                        last = mm(o, rT[hp, h // 2, tq], rkT[hp, 0:keys], start=False, stop=True)
                    last.then_inc(S("mla_s_mm"), 1)
                pe.wait_ge(S("mla_probs"), ev)
                for h in range(MLA_H):
                    for n in range(3):
                        last = tr(psum[:, h, n * P:(n + 1) * P], scores[:, h, n * P:(n + 1) * P], ident)
                    last.then_inc(S("mla_p_turned"), 1)
                pe.wait_ge(S("mla_pT_ready"), 2 * ev)
                for h in range(MLA_H):
                    o = bank(0, 4)[:, h * SEQ:(h + 1) * SEQ]
                    vv = [kvrow[:, t, h * 256 + NOPE:(h + 1) * 256] for t in range(TT)]
                    mm(o, vv[0], probsT[:, h, 0:256], start=True, stop=False)
                    last = mm(o[:, 128:256], vv[1], probsT[:, h, 256:384], start=False, stop=True)
                last.then_inc(S("mla_o_mm"), 1)

                for f in range(RW_F):
                    if f == 8:
                        pe.wait_ge(S("mla_mix_lo"), ev)
                    b0 = 4 if f < 8 else 0
                    for t in range(TT):
                        last = tr(bank(b0, 4)[:, (f % 8) * SEQ + t * P:(f % 8) * SEQ + (t + 1) * P],
                                  p_rw[:, t, f * P:(f + 1) * P], ident)
                    if f in (7, 13):
                        last.then_inc(S("rw_turned"), 1)
                pe.wait_ge(lora_in, 16 * ev)
                pe.wait_ge(S("rw_pT_ready"), 2 * ev)
                pe.wait_ge(S("rw_lora_in"), 2 * ev)
                for k, (w, src, hp) in enumerate(((lora_of("wa"), rw_sig, slice(0, 64)), (lora_of("wa"), pm[:, 12, :], slice(64, 128)),
                                                  (lora_of("g2"), rw_tmp[:, 0, :], slice(0, 128)))):
                    for j in range(4):
                        last = mm(bank(2 * k, 2)[:, j * SEQ:(j + 1) * SEQ], w[hp, j * P:(j + 1) * P], src[hp, :],
                                  start=True, stop=True)
                    last.then_inc(S("rw_lora_mm"), 1)
                if l:
                    v1 = lora_of("v1")
                    for k in range(4):
                        last = mm(bank(6)[0:32, 0:SEQ], v1[:, k * 32:(k + 1) * 32], rw_v[:, k, :], start=(k == 0), stop=(k == 3))
                    last.then_inc(S("rw_v1_mm"), 1)
                    pe.wait_ge(S("rw_v1_ready"), l)
                    for j in range(4):
                        last = mm(bank(6, 2)[:, j * SEQ:(j + 1) * SEQ], lora_of("v2")[0:32, j * P:(j + 1) * P],
                                  rw_bonus[0:32, 0, :], start=True, stop=True)
                    last.then_inc(S("rw_v2_mm"), 1)
                pe.wait_ge(S("rw_kk_squares"), ev)
                pe.wait_ge(S("rw_w_ready"), 4 * ev)
                for j in range(4):
                    last = mm(bank(0, 2)[:, j * SEQ:(j + 1) * SEQ], C("ones2"), rw_b[:, j, :], start=True, stop=True)
                last.then_inc(S("rw_kk_mm"), 1)
                pe.wait_ge(S("rw_rk"), ev)
                pe.wait_ge(S("rw_a_ready"), 4 * ev)
                for j in range(4):
                    last = mm(bank(2, 2)[:, j * SEQ:(j + 1) * SEQ], rkb[:, j, :], rw_e[2][:, j, :], start=True, stop=True)
                last.then_inc(S("rw_bonus_mm"), 1)

                def pairwise(b0, left, right):
                    last = None
                    for n in range(JC):
                        j, c = n // NC, n % NC
                        cols = slice(c * RC, (c + 1) * RC)
                        last = heads(lambda hp: mm(bank(b0, 2)[hp, n * RC:(n + 1) * RC], left[hp, j, cols], right[hp, j, cols],
                                                   start=True, stop=True))
                    return last

                pe.wait_ge(S("rw_factors"), ev)
                pe.wait_ge(S("rw_g_ready"), ev)
                for k, src in enumerate((rw_v, rw_a, rw_k)):
                    for n in range(JC):
                        j, c = n // NC, n % NC
                        last = heads(lambda hp: mm(bank(2 * k, 2)[hp, n * RC:(n + 1) * RC], src[hp, j, c * RC:(c + 1) * RC],
                                                   idst[hp, :], start=True, stop=True))
                    last.then_inc(S("rw_stack_mm"), 1)
                for k, (b0, left, right) in enumerate(((0, rw_kk, rw_a), (2, rw_a, rw_kk), (4, rw_k, rw_kk), (6, rw_a, rw_r),
                                                       (0, rw_k, rw_r))):
                    if k < 3:
                        pe.wait_ge(S("rw_stacked"), 3 * l + k + 1)
                    if k == 4:
                        pe.wait_ge(S("rw_m_ready"), 5 * l + 1)
                    pairwise(b0, left, right).then_inc(S("rw_m_mm"), 1)

                def products(b0, left, right, hf):
                    last = None
                    for n in range(8 * hf, 8 * hf + 8):
                        last = heads(lambda hp: mm(bank(b0 + hf)[hp, (n % 8) * RC:(n % 8 + 1) * RC], left[hp, n, :],
                                                   right[hp, n, :], start=True, stop=True))
                    return last

                pe.wait_ge(S("rw_m_ready"), 5 * ev)
                for k in range(len(RW_LEVELS)):
                    pe.wait_ge(S("rw_level_ready"), 5 * l + k + 1)
                    if k:
                        pe.wait_ge(S("rw_inv_ready"), 5 * l + k)
                    for hf in range(2):
                        products(0, b_lev, inv_t, hf).then_inc(S("rw_gt_mm"), 1)
                    for hf in range(2):
                        pe.wait_ge(S("rw_gt_ready"), 10 * l + 2 * k + hf + 1)
                        if k < len(RW_LEVELS) - 1:
                            products(2, g_t, inv, hf)
                        products(4, inv, g_t, hf).then_inc(S("rw_dinv_mm"), 1)
                pe.wait_ge(S("rw_inv_ready"), 5 * ev)
                for c in range(NC):
                    cols = slice(c * RC, (c + 1) * RC)

                    def each(b0, off, terms):
                        last = None
                        for j in range(4):
                            for hp in (slice(0, 64), slice(64, 128)):
                                for n, (left, right) in enumerate(terms):
                                    last = mm(bank(b0, 2)[hp, off + j * RC:off + (j + 1) * RC], left(hp, j), right(hp, j),
                                              start=(n == 0), stop=(n == len(terms) - 1))
                        return last

                    def feat(z):
                        return lambda hp, j: z[hp, j, cols]

                    def stacked(z):
                        return lambda hp, j: z[hp, NC * j + c, :]

                    def pair_of(z):
                        return lambda hp, j: z[hp, j, :]

                    if c:
                        pe.wait_ge(S("rw_state_ready"), 3 * l + c)
                    carried = [(feat(rw_kk), pair_of(state[c % 2]))] if c else []
                    each(0, 0, carried + [(stacked(mak_t), stacked(v_st))]).then_inc(S("rw_rhs_mm"), 1)
                    pe.wait_ge(S("rw_rhs_ready"), NC * l + c + 1)
                    each(1, 0, [(stacked(inv_t), pair_of(rhs))]).then_inc(S("rw_sa_mm"), 1)
                    pe.wait_ge(S("rw_sa_ready"), NC * l + c + 1)
                    if c < NC - 1:
                        each(2, 0, [(stacked(b_st), pair_of(sa)), (stacked(k_st), stacked(v_st))]).then_inc(S("rw_state_mm"), 1)
                    carried = [(feat(rw_r), pair_of(state[c % 2]))] if c else []
                    last = each(6, 256 * c, carried + [(stacked(mrb_t), pair_of(sa)), (stacked(mrk_t), stacked(v_st))])
                last.then_inc(S("rw_y_mm"), 1)
                pe.wait_ge(S("rw_y_normed"), ev)
                for c in range(NC):
                    for j in range(4):
                        last = heads(lambda hp: mm(bank(0, 2)[hp, j * SEQ + c * RC:j * SEQ + (c + 1) * RC], yc[hp, 4 * c + j, :],
                                                   idst[hp, :], start=True, stop=True))
                last.then_inc(S("rw_y_turned"), 1)

                pe.wait_ge(S("rw_mix_lo"), ev)
                s4o = s4 + N_IN // 4
                acc = acc0 + len(IN_CHUNKS) // 2
                for c in range(4):
                    pe.wait_ge(acc_free[c % 2], acc + c // 2 + 1)
                    slots(s4o, range(4 * c, 4 * c + 4), 0, KT, 2 * (c % 2), hT_hi, hT_lo)
                acc += 2
                norm(2 * l + 1)

                s4f = s4o + N_O // 4
                pair0 = sum(PAIRS) * l
                for pairs in PAIRS:
                    def turn(i, p0):
                        pe.wait_ge(S("act_row_ready"), i + (p0 + 1))
                        if not isinstance(i, int) or i + p0 > 0:
                            pe.wait_ge(S("act_lo_ready"), i + p0)
                        for k in range(4):
                            for t in range(TT):
                                last = tr(bank(4, 2)[:, k * SEQ + t * P:k * SEQ + (t + 1) * P],
                                          act_row[:, t, k * P:(k + 1) * P], ident)
                        last.then_inc(S("act_turned"), 1)

                    def pair(i, first):
                        si = i * 2 + s4f
                        for u in range(2):
                            pe.wait_ge(acc_free[u], i + (acc + 1))
                            slots(si, range(4 * u, 4 * u + 4), 0, KT, 2 * u, hT_hi, hT_lo)
                            if u == 0 and not first:
                                turn(i - 1, pair0)

                    pair(0, True)
                    with pe.Fori(1, pairs) as i:
                        pair(i, False)
                    s4f, acc = s4f + 2 * pairs, acc + pairs
                    for c in range(4):
                        pe.wait_ge(acc_free[c % 2], acc + c // 2 + 1)
                        for j in range(pairs):
                            if c == 0 and j == 3:
                                turn(pairs - 1, pair0)
                            if c == 0 and j == pairs - 1:
                                pe.wait_ge(S("act_lo_ready"), pair0 + pairs)
                            slots(s4f, [pairs * c + j], 4 * j, 4 * pairs, 2 * (c % 2), act_hi, act_lo)
                    s4f, acc = s4f + pairs, acc + 2
                    pair0 += pairs


def shape_constants():
    i, j = np.arange(P)[:, None], np.arange(P)[None, :]
    out = {"ident": (i == j)}
    masks = []
    for m in HG_LEVELS:
        masks.append((i == j) if m == 0 else
                     (i // (2 * m) == j // (2 * m)) & (i // m % 2 == 0) & (j // m % 2 == 1))
    out["hg_masks"] = np.concatenate(masks, 1)
    low = np.where(j <= i, 0.0, -1e30)
    out["attn"] = np.concatenate([low, np.zeros((P, P)), low], 1)
    out["reset"] = np.broadcast_to((np.arange(1024) % 64 != 0)[None, :], (P, 1024))
    out["ones2"] = (i // 64 == j // 64)
    a, b = (np.arange(P) % RC)[:, None], np.arange(RC)[None, :]
    out["idst"] = a == b
    out["strict_lo"] = a > b
    out["strict_up"] = a < b
    out["incl_up"] = a <= b
    out["pair_lo"] = (a // 2 == b // 2) & (a > b)
    out["pair_up"] = (a // 2 == b // 2) & (a < b)
    out["lev_lo"] = np.concatenate([(a // (2 * m) == b // (2 * m)) & (a // m % 2 == 1) & (b // m % 2 == 0)
                                    for m in RW_LEVELS], 1)
    half = ROPE // 2
    freq = np.float32(10000.0) ** (-np.arange(half, dtype=np.float32) / np.float32(half))
    out["inv_freq"] = np.broadcast_to(freq[None, :], (P, half))
    return np.ascontiguousarray(np.concatenate([np.asarray(out[n], np.float32) for n in CONST_COLS], 1))


def kernel(**inputs):
    import concourse.bacc as bacc
    from concourse.bass_utils import run_bass_kernel_spmd

    a = {k: np.asarray(z) for k, z in inputs.items()}

    def tiles(w, k_rows, cols):
        K, N = w.shape
        t = w.reshape(K // k_rows, k_rows // P, P, N // cols, cols).transpose(3, 0, 2, 1, 4)
        return t.reshape(N // cols, K // k_rows, P, (k_rows // P) * cols)

    def padded(t):
        full = np.zeros(t.shape[:-1] + (4 * CH,), np.float32)
        full[..., :t.shape[-1]] = t
        return full.reshape(-1, P, 4 * CH)

    slots = []
    for l in range(DEPTH):
        for c, w in IN_CHUNKS:
            slots.append(padded(tiles(a["w_in"][l][:, c:c + w], 512, w)))
        slots.append(padded(tiles(a["mla_w_qb"][l], 512, 384)))
        slots.append(padded(tiles(a["mla_w_kvb"][l], 256, CH)))
        slots.append(padded(tiles(a["w_o"][l], 512, CH)))
        first = 0
        for pairs in PAIRS:
            cols = slice(first * CH, (first + pairs) * CH)
            gate = tiles(a["w_gate_up"][l][:, :D_FF][:, cols], 512, CH)
            up = tiles(a["w_gate_up"][l][:, D_FF:][:, cols], 512, CH)
            slots.append(np.stack([gate, up], 1).reshape(-1, P, 4 * CH))
            slots.append(padded(tiles(a["w_down"][l][cols], 512, CH)))
            first += pairs
    stream = np.concatenate(slots, 0)
    assert stream.shape[0] == DEPTH * SLOTS_PER_LAYER

    def cols(z):
        return z.reshape(-1, P).T

    params, lora, rows, gains = [], [], [], []
    for l in range(DEPTH):
        qn, kn = a["mla_q_norm"][l], a["mla_k_norm"][l]
        par = dict(hg_lb=cols(a["hg_lower_bounds"][l]), q_a=cols(a["mla_q_a_norm"][l]), kv_a=cols(a["mla_kv_a_norm"][l]),
                   gq=cols(qn[:NOPE]), gk=cols(kn[:NOPE]), mu=cols(a["rw_mu"][l]), w0=cols(a["rw_w0"][l]),
                   a0=cols(a["rw_a0"][l]), v0=cols(a["rw_v0"][max(l - 1, 0)]), k_k=cols(a["rw_k_k"][l]),
                   k_a=cols(a["rw_k_a"][l]), r_k=cols(a["rw_r_k"][l].reshape(-1)), ln_w=cols(a["rw_ln_w"][l]),
                   ln_b=cols(a["rw_ln_b"][l]))
        params.append(np.concatenate([par[n] for n in PARAM_COLS], 1))
        v1 = a["rw_v1"][max(l - 1, 0)].reshape(4, P, 32).transpose(1, 0, 2).reshape(P, 128)
        v2 = a["rw_v2"][max(l - 1, 0)]
        lora.append(np.concatenate([np.concatenate([a["rw_w2"][l], a["rw_a2"][l]], 0), a["rw_g2"][l], v1,
                                    np.concatenate([v2] * 4, 0)], 1))
        rows.append(np.concatenate([a["hg_out_norm"][l]] + [qn[NOPE:]] * MLA_H + [kn[NOPE:]]))
        gains += [a["attn_norm"][l], a["ffn_norm"][l]]
    arrays = dict(
        stream=stream, x_in=a["x"].reshape(SEQ, D), positions=np.ascontiguousarray(a["positions"].reshape(TT, P).T),
        params=np.ascontiguousarray(np.concatenate(params, 1)), consts=shape_constants(),
        lora=np.stack(lora), gains=np.stack(gains), rows=np.stack(rows))
    nc = bacc.Bacc("TRN2", target_bir_lowering=False, num_devices=1)
    args = {n: nc.dram_tensor(n + "_dram", z.shape, mybir.dt.from_np(z.dtype), kind="ExternalInput").ap()
            for n, z in arrays.items()}
    out = nc.dram_tensor("out_dram", (SEQ, D), F32, kind="ExternalOutput").ap()
    build(nc, out=out, **args)
    r = run_bass_kernel_spmd(nc, [{n + "_dram": z for n, z in arrays.items()}], core_ids=[0])
    return r.results[0]["out_dram"].reshape(1, SEQ, D)
```

```python
from contextlib import ExitStack

import numpy as np

import concourse.bass as bass
from concourse import mybir

F32 = mybir.dt.float32
F32R = mybir.dt.float32r
U32 = mybir.dt.uint32
I32 = mybir.dt.int32
ALU = mybir.AluOpType
ACT = mybir.ActivationFunctionType
AX = mybir.AxisListType

P = 128
D = 2048
SEQ = 256
TT = SEQ // P
DEPTH = 2
KT = D // P
CH = 512

HG_H = 4
MLA_H = 8
NOPE = 128
ROPE = 64
QK = NOPE + ROPE
Q_RANK = 512
KV_RANK = 256
D_FF = 5632
RW_IN = 1792
RW_F = RW_IN // P
RC = 64
NC = SEQ // RC
JC = 4 * NC
IN_W = 4672
EPS = 1e-6
GN_EPS = 64e-5
C0 = float(np.exp(np.float32(-0.5)))
MAGIC = 12582912.0
TINY = float(2.0 ** -63)

IN_CHUNKS = [(c * CH, CH) for c in range(5)] + [(2880 + c * CH, CH) for c in range(3)] + [(2560, 320), (4416, 256)]
PAIRS = [6, 5]
RAW_SLOTS = 4
HALF_RING = 4
N_IN = len(IN_CHUNKS) * 4
N_PLAIN = 8
N_O = 16
N_FFN = sum(8 * p + 4 * p for p in PAIRS)
SPLIT_PER_LAYER = N_IN + N_O + N_FFN
SLOTS_PER_LAYER = SPLIT_PER_LAYER + N_PLAIN
FFN_AT = N_IN + N_PLAIN + N_O
assert N_IN % 4 == N_PLAIN % 4 == N_O % 4 == N_FFN % 4 == 0

PARAM_COLS = dict(hg_lb=4, q_a=4, kv_a=2, gq=1, gk=1, mu=14, w0=4, a0=4, v0=4, k_k=4, k_a=4, r_k=4, ln_w=4, ln_b=4)
CONST_COLS = dict(ident=128, hg_masks=8 * 128, attn=384, reset=1024, ones2=128, idst=64, strict_lo=64,
                  strict_up=64, incl_up=64, pair_lo=64, pair_up=64, lev_lo=5 * 64, inv_freq=32)
LORA_COLS = dict(wa=512, g2=512, v1=128, v2=512)
HG_LEVELS = [0, 64, 32, 16, 8, 4, 2, 1]
RW_LEVELS = [2, 4, 8, 16, 32]

HG_LEVEL_SLOT = [14, 17, 20, 21, 23, 24, 26, 27]
HG_TURN, HG_GATES, HG_LOGF, HG_CROSS, HG_CROSS_OUT, HG_SILU, HG_GAIN, HG_OUT = 11, 14, 15, 18, 21, 24, 28, 30
HG_SQUARES, HG_STD, HG_NORMED = 33, 34, 35


def offsets(cols):
    at, out = 0, {}
    for name, n in cols.items():
        out[name] = (at, at + n)
        at += n
    return out, at


PAR, N_PAR = offsets(PARAM_COLS)
CON, N_CON = offsets(CONST_COLS)
LOR, N_LOR = offsets(LORA_COLS)


def build(nc, stream, x_in, positions, params, consts, lora, gains, rows, out):
    with ExitStack() as ctx:
        def sb(name, shape, dt=F32, on=ctx):
            return on.enter_context(nc.sbuf_tensor(name, shape, dt))

        def sem(name):
            return ctx.enter_context(nc.semaphore(name))

        x = sb("x", [P, TT, D])
        hT_hi = sb("hT_hi", [P, KT, SEQ], F32R)
        hT_lo = sb("hT_lo", [P, KT, SEQ], F32R)
        raw = sb("raw", [P, RAW_SLOTS, 4 * CH])
        v_first = sb("v_first", [P, 4, SEQ])
        gain = sb("gain", [P, D])
        con = sb("con", [P, N_CON])
        par = sb("par", [P, DEPTH, N_PAR])
        lor = sb("lor", [P, N_LOR])
        row = sb("row", [P, 128 + 9 * ROPE])
        derived = sb("derived", [P, DEPTH, 12])
        rkb = sb("rkb", [P, 4, P])
        cs = sb("cs", [P, 2, TT, 32])
        small = sb("small", [P, 256])

        with ExitStack() as on:
            w_hi = sb("w_hi", [P, HALF_RING, 2 * CH], F32R, on)
            w_lo = sb("w_lo", [P, HALF_RING, 2 * CH], F32R, on)
            act_hi = sb("act_hi", [P, 4 * PAIRS[0], SEQ], F32R, on)
            act_lo = sb("act_lo", [P, 4 * PAIRS[0], SEQ], F32R, on)
            silu = sb("silu", [P, TT, CH], F32, on)
            act_row = sb("act_row", [P, TT, CH], F32, on)
        ARENA = 22528
        arena = sb("arena", [P, ARENA])

        def at(off, *shape):
            n = int(np.prod(shape))
            assert off + n <= ARENA
            v = arena[:, off:off + n]
            if len(shape) == 2:
                return v.rearrange("p (a b) -> p a b", b=shape[1])
            if len(shape) == 3:
                return v.rearrange("p (a b c) -> p a b c", b=shape[1], c=shape[2])
            return v

        RING_END = 8192
        xg_first = at(RING_END, TT, D)
        rstd = small[:, 220:222]
        p_rw = at(RING_END, TT, RW_IN)
        p_mla = at(RING_END + 3584, TT, 832)
        p_hg = at(RING_END + 5248, TT, 2048)
        HG_AT = RING_END + 5248 + 4096

        ring_gain = gain[:, :].rearrange("p (n h t) -> p n h t", n=2, h=4)
        hg_q = at(HG_AT, 4, SEQ)
        hg_sig = at(HG_AT + 1024, 4, SEQ)
        hg_b = hg_sig
        hg_k = at(HG_AT + 2048, 4, SEQ)
        hg_e = [ring_gain[:, 0], ring_gain[:, 1], at(HG_AT + 3072, 4, SEQ), at(RING_END + 5248 + 2048, 4, SEQ)]
        hg_kend, hg_qbeg, hg_logf = hg_e[0], hg_e[1], hg_e[2]
        hg_diag = at(RING_END + 5248, 8, P)
        hg_gate = p_hg[:, :, 1536:2048]
        hg_k128 = at(HG_AT + 4096, 4, P)
        hg_cross = hg_k128
        hg_q128 = rkb
        hg_o = hg_q.rearrange("p h t -> p (h t)").rearrange("p (t n) -> p t n", t=TT)
        hg_sq = hg_k

        qrow = at(0, TT, MLA_H * QK)
        kvrow = at(3072, TT, MLA_H * 2 * NOPE)
        qaT = at(7168, 4, SEQ)
        MB = RING_END + 5248
        kvaT = at(MB, 2, SEQ)
        mla_sq = at(MB + 512, 3072)
        scores = at(MB + 512, MLA_H, 384)
        qnT = at(MB + 3584, MLA_H, SEQ)
        knT = at(MB + 5632, MLA_H, SEQ)
        k_sq = at(MB + 5632, TT * MLA_H, NOPE)
        ro = at(MB + 7680, TT, 640)
        probsT = at(0, MLA_H, 384)
        rT = at(7168, 4, SEQ)
        rkT = kvaT[:, 0, :]
        rb = gain[:, 0:1280].rearrange("p (t n) -> p t n", t=TT)
        rtmp = gain[:, 1280:1280 + 576].rearrange("p (t h n) -> p t h n", t=TT, h=9)

        pT = at(0, RW_F, SEQ + 1)
        pm = at(3600, RW_F, SEQ)
        rw_r, rw_k, rw_v = pm[:, 0:4, :], pm[:, 4:8, :], pm[:, 8:12, :]
        rw_sig = at(7184, 256)
        RB = 11776
        rw_w = at(RB, 4, SEQ)
        rw_tmp = at(RB + 1024, 4, SEQ)
        rw_a = at(RB + 2048, 4, SEQ)
        rw_g = at(RB + 3072, 4, SEQ)
        rw_kk = at(RB + 4096, 4, SEQ)
        rw_b = at(RB + 5120, 4, SEQ)
        rw_e = [at(RB + 6144, 4, SEQ), at(RB + 7168, 4, SEQ), at(RB + 8192, 4, SEQ)]
        rw_bonus = at(RB + 9216, 4, SEQ)
        ar = at(RB, JC, 2, RC)
        diag_v = at(0, JC, P)
        diag_b = at(8192, JC, P)
        diag_k = at(RB + 5120, JC, P)
        diag_a = at(RB + 7168, JC, P)
        v_st = at(2048, JC, RC)
        k_st = at(3072, JC, RC)
        b_st = at(10240, JC, RC)
        mab = at(4096, JC, RC)
        mab_t = at(5120, JC, RC)
        mak_t = at(6144, JC, RC)
        mrk_t = at(7168, JC, RC)
        mrb_t = at(RB + 4096, JC, RC)
        inv = at(0, JC, RC)
        inv_t = at(1024, JC, RC)
        g_t = mab_t
        diag_x, diag_g, diag_l = diag_b, diag_k, diag_a
        rhs = at(RB + 2048, 4, RC)
        sa = at(RB + 2048 + 256, 4, RC)
        state = [at(RB + 2048 + 512, 4, RC), at(RB + 2048 + 768, 4, RC)]
        yc = at(0, JC, RC)
        ysq = at(RB + 5120, JC, RC)
        y_out = at(RB + 6144, 4, SEQ)
        EVEN, ODD = slice(0, 64), slice(64, 128)

        psum = ctx.enter_context(nc.psum_tensor("psum", [P, 8, CH], F32))

        def bank(b, n=1):
            return psum[:, b:b + n, :].rearrange("p a b -> p (a b)")

        def C(name):
            return con[:, CON[name][0]:CON[name][1]]

        ident = C("ident")
        idst = C("idst")
        hg_masks = C("hg_masks").rearrange("p (l t) -> p l t", t=P)
        lev_lo = C("lev_lo").rearrange("p (l t) -> p l t", t=RC)

        def par_of(l, name):
            return par[:, l, PAR[name][0]:PAR[name][1]]

        def lora_of(name):
            return lor[:, LOR[name][0]:LOR[name][1]]

        def over(v, n, m):
            return v.unsqueeze(1).broadcast_to([P, n, m])

        def along(v, m):
            return v.unsqueeze(2).broadcast_to([P, v.shape[1], m])

        raw_in = [sem(f"raw_in{s}") for s in range(RAW_SLOTS)]
        x_in_sem = [sem(f"x_loaded{t}") for t in range(TT)]
        ident_in, con_in, par_in, row_in, lora_in, pos_in = (sem(n) for n in (
            "ident_loaded", "consts_loaded", "params_loaded", "rows_loaded", "lora_loaded", "positions_loaded"))
        gain_in = sem("gain_loaded")
        out_done = sem("out_stored")
        hi_done, lo_done = sem("w_hi_written"), sem("w_lo_written")
        half_used = sem("half_used")
        plain_used = sem("plain_slot_used")
        acc_free = [sem("acc_even_free"), sem("acc_odd_free")]
        names = {}

        def S(name):
            if name not in names:
                names[name] = sem(name)
            return names[name]

        block = ctx.enter_context(nc.Block())

        def xg_tile(n, c):
            return act_row[:, :, :] if n else xg_first[:, :, c * CH:(c + 1) * CH]

        def x_turn_bank(n, c):
            return 6 if n or c == 3 else 2 * c

        def chunk_ends(s4, j):
            return s4 * 8 + (2 * j + HALF_RING)

        @block.sync
        def _(sp):
            for t in range(TT):
                sp.dma_start(x[:, t, :], x_in[t * P:(t + 1) * P, :]).then_inc(x_in_sem[t], 16)
            for l in range(DEPTH):
                g0, s0 = l * SLOTS_PER_LAYER, l * SPLIT_PER_LAYER
                for j in range(FFN_AT):
                    if j < N_IN + 4:
                        if l or j >= 4:
                            sp.wait_ge(lo_done, 2 * (s0 + j - 3))
                    elif j < N_IN + N_PLAIN + 4:
                        sp.wait_ge(plain_used, N_PLAIN * l + j - N_IN - 3)
                    else:
                        sp.wait_ge(lo_done, 2 * (s0 + j - N_PLAIN - 3))
                    n = 4 * (IN_CHUNKS[j // 4][1] if j < N_IN else 384 if j < N_IN + 4
                             else 256 if j < N_IN + N_PLAIN else CH)
                    sp.dma_start(raw[:, j % 4, 0:n], stream[g0 + j, :, 0:n]).then_inc(raw_in[j % 4], 16)
                with sp.Fori(0, N_FFN // 4) as i:
                    for j in range(4):
                        sp.wait_ge(lo_done, i * 8 + 2 * (s0 + N_IN + N_O + j - 3))
                        sp.dma_start(raw[:, j, :],
                                     stream[bass.ds(i * 4 + (g0 + FFN_AT + j), 1), :, :].rearrange(
                                         "o p n -> (o p) n")).then_inc(raw_in[j], 16)
            for c in range(4):
                cols = slice(c * CH, (c + 1) * CH)
                sp.wait_ge(S("x_added"), 12 * DEPTH - 3 + c)
                sp.dma_start(out.rearrange("(t p) d -> p t d", p=P)[:, :, cols], x[:, :, cols]).then_inc(out_done, 16)
            sp.wait_ge(out_done, 64)

        @block.gpsimd
        def _(pool):
            pool.dma_start(gain[:, :], gains[0:1, :].broadcast_to([P, D])).then_inc(gain_in, 16)
            pool.dma_start(con[:, 0:P], consts[:, 0:P]).then_inc(ident_in, 16)
            pool.wait_ge(raw_in[RAW_SLOTS - 1], 16)
            pool.dma_start(con[:, P:N_CON], consts[:, P:N_CON]).then_inc(con_in, 16)
            pool.dma_start(par[:, :, :], params.rearrange("p (l n) -> p l n", l=DEPTH)).then_inc(par_in, 16)
            pool.dma_start(small[:, 200:202].bitcast(I32), positions).then_inc(pos_in, 16)
            for l in range(DEPTH):
                if l:
                    pool.wait_ge(S("hg_gate_ready"), l)
                    pool.wait_ge(S("rw_mix_lo"), l)
                    pool.wait_ge(S("xg_ready"), 8 * l)
                    pool.dma_start(gain[:, :], gains[2 * l:2 * l + 1, :].broadcast_to([P, D])).then_inc(gain_in, 16)
                pool.dma_start(row[:, :], rows[l:l + 1, :].broadcast_to([P, 128 + 9 * ROPE])).then_inc(row_in, 16)
                pool.dma_start(lor[:, :], lora[l, :, :]).then_inc(lora_in, 16)
                pool.wait_ge(S("mla_rope_done"), l + 1)
                pool.dma_start(gain[:, :], gains[2 * l + 1:2 * l + 2, :].broadcast_to([P, D])).then_inc(gain_in, 16)
                for tile, free in ((diag_b, (("rw_pT_ready", 2),)), (diag_v, (("rw_shifted", 1),)),
                                   (diag_k, (("rw_exp", 3), ("rw_r_done", 1))), (diag_a, (("rw_ab_done", 1),))):
                    for name, n in free:
                        pool.wait_ge(S(name), n * (l + 1))
                    nc.gpsimd.memset(tile[EVEN, :, 64:128], 0.0).then_inc(S("rw_zeroed"), 1)
                    nc.gpsimd.memset(tile[ODD, :, 0:64], 0.0).then_inc(S("rw_zeroed"), 1)
                pool.wait_ge(S("rw_m_ready"), 5 * l + 1)
                for k in range(len(RW_LEVELS)):
                    if k:
                        pool.wait_ge(S("rw_gt_mm"), 10 * l + 2 * k)
                    for hp in (EVEN, ODD):
                        nc.gpsimd.tensor_tensor(diag_l[hp, :, hp], mab[hp, :, :],
                                                lev_lo[hp, k, :].unsqueeze(1).broadcast_to([64, JC, RC]),
                                                ALU.mult).then_inc(S("rw_level_ready"), 1)

        @block.scalar
        def _(act):
            def chained(ins, s, value):
                ins.then_inc(s, 1)
                act.wait_ge(s, value)

            def split_hi(g4, s4, j, w=CH):
                act.wait_ge(raw_in[j % 4], g4 * 16 + 16 * (j // 4 + 1))
                for hf in range(2):
                    q = 2 * j + hf
                    act.wait_ge(half_used, s4 * 8 + (q + 1))
                    nc.scalar.activation(w_hi[:, q % HALF_RING, 0:2 * w], raw[:, j % 4, hf * 2 * w:(hf + 1) * 2 * w],
                                         ACT.Copy).then_inc(hi_done, 1)

            def tables():
                for k in range(2):
                    act.wait_ge(S("angle_ready"), k + 1)
                    nc.scalar.activation(cs[:, k, :, :], small[:, 64 * k + 8:64 * k + 72].rearrange(
                        "p (t n) -> p t n", t=TT), ACT.Sin).then_inc(S("cs_ready"), 1)
                act.wait_ge(S("lb_shifted"), 1)
                nc.scalar.activation(small[:, 144:152], small[:, 144:152], ACT.Exp).then_inc(S("lb_exp"), 1)

            def x_hi(n, c):
                act.wait_ge(S("x_turned"), 4 * n + c + 1)
                nc.scalar.activation(hT_hi[:, 4 * c:4 * c + 4, :], bank(x_turn_bank(n, c), 2).rearrange(
                    "p (k t) -> p k t", k=4), ACT.Copy).then_inc(S("hT_hi_ready"), 1)

            def x_squares(n, c):
                if n:
                    act.wait_ge(S("x_added"), 12 * ((n - 1) // 2) + (4 if n % 2 else 12) - 3 + c)
                    if n > 1:
                        act.wait_ge(S("act_row_ready"), sum(PAIRS) * (n // 2))
                    act.wait_ge(S("x_squares"), 8 * n + 2 * c)
                for t in range(TT):
                    if n == 0:
                        act.wait_ge(x_in_sem[t], 16)
                        if c:
                            act.wait_ge(S("x_squares"), 2 * c + t - 1)
                    nc.scalar.activation(silu[:, t, :], x[:, t, c * CH:(c + 1) * CH], ACT.Square,
                                         accum_out=small[:, 208 + 4 * t + c:209 + 4 * t + c]).then_inc(
                                             S("x_squares"), 1)

            def x_std(n):
                act.wait_ge(S("x_var"), n + 1)
                nc.scalar.activation(small[:, 218:220], small[:, 216:218], ACT.Sqrt).then_inc(S("x_std"), 1)

            def norm_tail(n, j):
                if j == 3:
                    x_hi(n, 3)
                    for c in range(0 if n == 0 else 3, 4):
                        x_squares(n, c)
                if j == 5:
                    x_std(n)

            for l in range(DEPTH):
                ev = l + 1
                g4, s4 = l * SLOTS_PER_LAYER // 4, l * SPLIT_PER_LAYER // 4
                if l == 0:
                    for c in range(3):
                        x_hi(0, c)
                for j in range(N_IN):
                    if l == 0 and j == 8:
                        tables()
                    split_hi(g4, s4, j, IN_CHUNKS[j // 4][1])
                    norm_tail(2 * l, j)

                    if j == HG_GATES:
                        act.wait_ge(S("hg_turned"), 2 * l + 1)
                        nc.scalar.activation(hg_q.rearrange("p h t -> p (h t)"), bank(4, 2), ACT.Silu).then_inc(
                            S("hg_q_ready"), 1)
                        act.wait_ge(S("hg_turned"), 2 * l + 2)
                        nc.scalar.activation(hg_sig.rearrange("p h t -> p (h t)"), bank(6, 2), ACT.Sigmoid).then_inc(
                            S("hg_sig_ready"), 1)
                        nc.scalar.activation(hg_k.rearrange("p h t -> p (h t)"), bank(6, 2), ACT.Sigmoid,
                                             scale=-1.0).then_inc(S("hg_sig_ready"), 1)
                    if j == HG_LOGF:
                        act.wait_ge(S("hg_sig_floor"), ev)
                        act.wait_ge(S("derived_ready"), 1)
                        for h in range(HG_H):
                            nc.scalar.activation(hg_logf[:, h, :], hg_sig[:, h, :], ACT.Ln, bias=derived[:, l, h:h + 1],
                                                 scale=derived[:, l, 4 + h:5 + h]).then_inc(S("hg_logf"), 1)
                    for k in range(1, 8):
                        if j != HG_LEVEL_SLOT[k] - 1:
                            continue
                        if k == 1:
                            act.wait_ge(S("hg_exponent"), 8 * l + 1)
                            nc.scalar.activation(hg_kend, hg_kend, ACT.Exp).then_inc(S("hg_exp"), 1)
                            nc.scalar.activation(small[:, 160:176].rearrange("p (h c) -> p h c", h=4),
                                                 hg_b.rearrange("p h (c i) -> p h c i", i=64)[:, :, :, 63],
                                                 ACT.Exp).then_inc(S("hg_total_exp"), 1)
                        act.wait_ge(S("hg_exponent"), 8 * l + k + 1)
                        nc.scalar.activation(hg_e[k % 4], hg_b if k == 1 else hg_e[k % 4], ACT.Exp).then_inc(
                            S("hg_exp"), 1)
                    if j == HG_CROSS_OUT:
                        act.wait_ge(S("hg_cross_mm"), ev)
                        nc.scalar.activation(hg_cross.rearrange("p h t -> p (h t)"), bank(4), ACT.Copy).then_inc(
                            S("hg_cross_ready"), 1)
                    if j == HG_SILU:
                        act.wait_ge(S("p_ready"), len(IN_CHUNKS) * l + 4)
                        nc.scalar.activation(hg_gate, hg_gate, ACT.Silu).then_inc(S("hg_gate_silu"), 1)
                    if j == HG_SQUARES:
                        act.wait_ge(S("hg_o_mm"), ev)
                        nc.scalar.activation(hg_sq.rearrange("p h t -> p (h t)"), bank(4, 2), ACT.Square).then_inc(
                            S("hg_squares"), 1)
                    if j == HG_STD:
                        act.wait_ge(S("hg_var"), ev)
                        nc.scalar.activation(small[:, 192:200], small[:, 184:192], ACT.Sqrt).then_inc(S("hg_std"), 1)
                act.wait_ge(S("hg_o_turned"), ev)
                nc.scalar.activation(hT_hi[:, 0:4, :], bank(6, 2).rearrange("p (h t) -> p h t", h=4),
                                     ACT.Copy).then_inc(S("hg_mix_hi"), 1)

                act.wait_ge(S("p_ready"), len(IN_CHUNKS) * ev)
                spans = ((0, 512), (512, 768), (768, 832))
                for k, (a, b) in enumerate(spans):
                    for t in range(TT):
                        nc.scalar.activation(hg_e[0].rearrange("p h t -> p (h t)")[:, 0:b - a], p_mla[:, t, a:b], ACT.Square,
                                             accum_out=small[:, 8 + 2 * k + t:9 + 2 * k + t]).then_inc(S("mla_in_squares"), 1)
                        act.wait_ge(S("mla_in_squares"), 6 * l + 2 * k + t + 1)
                act.wait_ge(S("mla_in_var"), ev)
                nc.scalar.activation(small[:, 24:30], small[:, 16:22], ACT.Sqrt).then_inc(S("mla_in_std"), 1)
                act.wait_ge(S("mla_in_turned"), ev)
                act.wait_ge(S("hg_o_used"), ev)
                for k in range(6):
                    dst = qaT[:, k, :] if k < 4 else kvaT[:, k - 4, :]
                    g = par_of(l, "q_a")[:, k:k + 1] if k < 4 else par_of(l, "kv_a")[:, k - 4:k - 3]
                    nc.scalar.activation(dst, bank(0, 3)[:, k * SEQ:(k + 1) * SEQ], ACT.Copy,
                                         scale=g).then_inc(S("mla_inT_ready"), 1)
                for c in range(8):
                    act.wait_ge(S("mla_up_mm"), 8 * l + c + 1)
                    b0 = (4 + 2 * c) % 8
                    w = 384 if c < 4 else CH
                    dst = qrow[:, :, c * 384:(c + 1) * 384] if c < 4 else kvrow[:, :, (c - 4) * CH:(c - 3) * CH]
                    nc.scalar.activation(dst, psum[:, b0:b0 + 2, 0:w], ACT.Copy).then_inc(S("mla_up_ready"), 1)
                    if c == 3:
                        act.wait_ge(S("mla_up_ready"), 8 * l + 4)
                        nc.scalar.activation(mla_sq[:, :], qrow.rearrange("p t n -> p (t n)"), ACT.Square).then_inc(
                            S("mla_q_squares"), 1)
                act.wait_ge(S("mla_up_ready"), 8 * ev)
                nc.scalar.activation(k_sq.rearrange("p (t h) n -> p t h n", t=TT),
                                     kvrow.rearrange("p t (h n) -> p t h n", n=256)[:, :, :, 0:NOPE],
                                     ACT.Square).then_inc(S("mla_k_squares"), 1)
                act.wait_ge(S("mla_var"), ev)
                nc.scalar.activation(small[:, 80:128], small[:, 32:80], ACT.Sqrt).then_inc(S("mla_std"), 1)
                act.wait_ge(S("mla_q_turned"), ev)
                nc.scalar.activation(qnT.rearrange("p h t -> p (h t)"), bank(0, 4), ACT.Copy,
                                     scale=par_of(l, "gq")).then_inc(S("mla_qT_ready"), 1)
                act.wait_ge(S("mla_r_turned"), ev)
                nc.scalar.activation(rT.rearrange("p h t -> p (h t)"), bank(0, 2), ACT.Copy).then_inc(S("mla_rT_ready"), 1)
                nc.scalar.activation(rkT, bank(2)[:, 0:SEQ], ACT.Copy).then_inc(S("mla_rT_ready"), 1)
                act.wait_ge(S("mla_shifted"), ev)
                nc.scalar.activation(scores[:, :, :], scores[:, :, :], ACT.Exp).then_inc(S("mla_exp"), 1)
                for k in range(2):
                    act.wait_ge(S("mla_p_turned"), 8 * l + 4 * k + 4)
                    nc.scalar.activation(probsT[:, 4 * k:4 * k + 4, :], psum[:, 4 * k:4 * k + 4, 0:384],
                                         ACT.Copy).then_inc(S("mla_pT_ready"), 1)
                act.wait_ge(S("mla_o_mm"), ev)
                nc.scalar.activation(hT_hi[:, 4:12, :], bank(0, 4).rearrange("p (h t) -> p h t", h=8),
                                     ACT.Copy).then_inc(S("mla_mix_hi"), 1)

                act.wait_ge(S("mla_mix_lo"), ev)
                act.wait_ge(S("rw_turned"), 2 * l + 1)
                nc.scalar.activation(pT[:, 0:8, 1:SEQ + 1], bank(4, 4).rearrange("p (f t) -> p f t", f=8),
                                     ACT.Copy).then_inc(S("rw_pT_ready"), 1)
                act.wait_ge(S("rw_turned"), 2 * l + 2)
                nc.scalar.activation(pT[:, 8:14, 1:SEQ + 1], bank(0, 3).rearrange("p (f t) -> p f t", f=6),
                                     ACT.Copy).then_inc(S("rw_pT_ready"), 1)
                act.wait_ge(S("rw_shifted"), ev)
                nc.scalar.activation(rw_sig[0:64, :], pm[0:64, 12, :], ACT.Tanh).then_inc(S("rw_lora_in"), 1)
                nc.scalar.activation(rw_tmp[:, 0, :], pm[:, 13, :], ACT.Sigmoid).then_inc(S("rw_lora_in"), 1)
                act.wait_ge(S("rw_lora_mm"), 3 * l + 1)
                for j in range(4):
                    nc.scalar.activation(rw_w[:, j, :], bank(0, 2)[:, j * SEQ:(j + 1) * SEQ], ACT.Sigmoid,
                                         bias=par_of(l, "w0")[:, j:j + 1]).then_inc(S("rw_w_ready"), 1)
                act.wait_ge(S("rw_lora_mm"), 3 * l + 2)
                for j in range(4):
                    nc.scalar.activation(rw_a[:, j, :], bank(2, 2)[:, j * SEQ:(j + 1) * SEQ], ACT.Sigmoid,
                                         bias=par_of(l, "a0")[:, j:j + 1]).then_inc(S("rw_a_ready"), 1)
                act.wait_ge(S("rw_lora_mm"), 3 * l + 3)
                nc.scalar.activation(rw_g.rearrange("p j t -> p (j t)"), bank(4, 2), ACT.Copy).then_inc(S("rw_g_ready"), 1)
                if l:
                    act.wait_ge(S("rw_v1_mm"), l)
                    nc.scalar.activation(rw_bonus[0:32, 0, :], bank(6)[0:32, 0:SEQ], ACT.Copy).then_inc(S("rw_v1_ready"), 1)
                    act.wait_ge(S("rw_v2_mm"), l)
                    for j in range(4):
                        nc.scalar.activation(rw_e[0][:, j, :], bank(6, 2)[:, j * SEQ:(j + 1) * SEQ], ACT.Sigmoid,
                                             bias=par_of(l, "v0")[:, j:j + 1]).then_inc(S("rw_vmix_ready"), 1)
                act.wait_ge(S("rw_kk_mm"), ev)
                nc.scalar.activation(rw_e[1].rearrange("p j t -> p (j t)"), bank(0, 2), ACT.Sqrt).then_inc(S("rw_kk_norm"), 1)
                v3, b3 = (z.rearrange("p j (c i) -> p (j c) i", i=RC) for z in (rw_v, rw_a))
                act.wait_ge(S("rw_v_ready"), ev)
                for hp in (EVEN, ODD):
                    nc.scalar.activation(diag_v[hp, :, hp], v3[hp, :, :], ACT.Copy).then_inc(S("rw_diag_act"), 1)
                act.wait_ge(S("rw_exponent"), 3 * l + 1)
                nc.scalar.activation(rw_e[0], rw_b, ACT.Exp, scale=-C0).then_inc(S("rw_exp"), 1)
                nc.scalar.activation(rw_e[1], rw_b, ACT.Exp, scale=C0).then_inc(S("rw_exp"), 1)
                act.wait_ge(S("rw_exponent"), 3 * l + 2)
                nc.scalar.activation(small[:, 48:64], small[:, 32:48], ACT.Exp, scale=-C0).then_inc(S("rw_half_decay"), 1)
                act.wait_ge(S("rw_exponent"), 3 * l + 3)
                nc.scalar.activation(rw_e[2], rw_e[2], ACT.Exp, scale=-C0).then_inc(S("rw_exp"), 1)
                act.wait_ge(S("rw_b_done"), ev)
                nc.scalar.activation(diag_b[EVEN, :, EVEN], b3[EVEN, :, :], ACT.Copy).then_inc(S("rw_diag_act"), 1)
                act.wait_ge(S("rw_ab_done"), ev)
                nc.scalar.activation(diag_a[EVEN, :, EVEN], ar[EVEN, :, 0, :], ACT.Copy).then_inc(S("rw_diag_act"), 1)
                for k, dst in enumerate((v_st, b_st, k_st)):
                    act.wait_ge(S("rw_stack_mm"), 3 * l + k + 1)
                    nc.scalar.activation(dst.rearrange("p a b -> p (a b)"), bank(2 * k, 2), ACT.Copy).then_inc(
                        S("rw_stacked"), 1)

                def spread_x(n):
                    act.wait_ge(S("rw_x"), 10 * l + n + 1)
                    h8 = slice(8 * (n % 2), 8 * (n % 2) + 8)
                    nc.scalar.activation(diag_x[EVEN, h8, EVEN], inv[EVEN, h8, :], ACT.Copy).then_inc(S("rw_diag_x_act"), 1)

                spread_x(0)
                spread_x(1)
                for k in range(len(RW_LEVELS)):
                    last = k == len(RW_LEVELS) - 1
                    for hf in range(2):
                        h8 = slice(8 * hf, 8 * hf + 8)
                        act.wait_ge(S("rw_gt_mm"), 10 * l + 2 * k + hf + 1)
                        nc.scalar.activation(g_t[:, h8, :].rearrange("p a b -> p (a b)"), bank(hf),
                                             ACT.Copy).then_inc(S("rw_gt_ready"), 1)
                        if not last:
                            nc.scalar.activation(diag_g[EVEN, h8, EVEN], bank(hf)[EVEN, :].rearrange(
                                "p (n t) -> p n t", n=8), ACT.Copy).then_inc(S("rw_diag_g_act"), 1)
                    if not last:
                        spread_x(2 * k + 2)
                        spread_x(2 * k + 3)
                for c in range(NC):
                    act.wait_ge(S("rw_sa_mm"), NC * l + c + 1)
                    nc.scalar.activation(sa.rearrange("p a b -> p (a b)"), bank(1)[:, 0:256], ACT.Copy).then_inc(
                        S("rw_sa_ready"), 1)
                act.wait_ge(S("rw_y_centred"), ev)
                nc.scalar.activation(ysq, yc, ACT.Square).then_inc(S("rw_y_squares"), 1)
                act.wait_ge(S("rw_y_var"), ev)
                nc.scalar.activation(small[:, 112:128], small[:, 96:112], ACT.Sqrt).then_inc(S("rw_y_std"), 1)
                act.wait_ge(S("rw_out"), ev)
                nc.scalar.activation(hT_hi[:, 12:16, :], y_out, ACT.Copy).then_inc(S("rw_mix_hi"), 1)

                act.wait_ge(S("rw_mix_lo"), ev)
                s4o, g4o = s4 + N_IN // 4, g4 + (N_IN + N_PLAIN) // 4
                for j in range(N_O):
                    split_hi(g4o, s4o, j)
                    if j < 4:
                        nc.scalar.activation(act_hi[:, 4 * j:4 * j + 4, :], hT_hi[:, 4 * j:4 * j + 4, :].bitcast(F32),
                                             ACT.Copy).then_inc(S("mix_hi_kept"), 1)
                    elif j % 4 == 3:
                        x_hi(2 * l + 1, j // 4 - 1)
                        x_squares(2 * l + 1, j // 4 - 1)

                g4f, s4f = g4o + N_O // 4, s4o + N_O // 4
                pair0 = sum(PAIRS) * l
                norm_of_ffn = 2 * l + 1
                for part, pairs in enumerate(PAIRS):
                    fresh = part == 0
                    makes_norm = part == len(PAIRS) - 1 and l < DEPTH - 1

                    def pair(i, first):
                        gi, si = i * 2 + g4f, i * 2 + s4f
                        for j in range(8):
                            if j == 6:
                                act.wait_ge(half_used, chunk_ends(si, 4))
                                if not (first and pair0 == 0):
                                    act.wait_ge(S("act_row_ready"), i + pair0)
                                act.wait_ge(S("rstd_ready"), norm_of_ffn + 1)
                                nc.scalar.activation(silu[:, 0, :], psum[:, 0, :], ACT.Silu, scale=rstd[:, 0:1])
                                nc.scalar.activation(silu[:, 1, :], psum[:, 1, :], ACT.Silu, scale=rstd[:, 1:2]).then_inc(
                                    acc_free[0], 1)
                                if not first:
                                    turned_hi(i - 1, pair0)
                            split_hi(gi, si, j)
                            if first and fresh:
                                norm_tail(norm_of_ffn, j)

                    def turned_hi(i, p0):
                        act.wait_ge(S("act_turned"), i + (p0 + 1))
                        dst = act_hi[:, bass.ds(i * 4, 4), :] if not isinstance(i, int) else act_hi[:, 4 * i:4 * i + 4, :]
                        nc.scalar.activation(dst, bank(4, 2).rearrange("p (k t) -> p k t", k=4),
                                             ACT.Copy).then_inc(S("act_hi_ready"), 1)

                    pair(0, True)
                    with act.Fori(1, pairs) as i:
                        pair(i, False)
                    g4f, s4f = g4f + 2 * pairs, s4f + 2 * pairs
                    for j in range(4 * pairs):
                        split_hi(g4f, s4f, j)
                        if j == 3:
                            turned_hi(pairs - 1, pair0)
                        if makes_norm and j > pairs and j % pairs == 3:
                            x_hi(2 * l + 2, j // pairs - 1)
                            x_squares(2 * l + 2, j // pairs - 1)
                    g4f, s4f = g4f + pairs, s4f + pairs
                    pair0 += pairs

        @block.vector
        def _(dve):
            steps = [0]
            chain = sem("dve_steps")

            def v(ins):
                steps[0] += 1
                ins.then_inc(chain, 1)
                dve.wait_ge(chain, steps[0])

            def u(ins):
                steps[0] += 1
                ins.then_inc(chain, 1)

            def settle():
                dve.wait_ge(chain, steps[0])

            def vs(ins, name, value):
                ins.then_inc(S(name), 1)
                dve.wait_ge(S(name), value)

            tt, ts, stt = nc.vector.tensor_tensor, nc.vector.tensor_scalar, nc.vector.scalar_tensor_tensor
            red, rec, cp = nc.vector.tensor_reduce, nc.vector.reciprocal, nc.vector.tensor_copy
            ADD, SUB, MUL, MAX = ALU.add, ALU.subtract, ALU.mult, ALU.max

            def split_lo(s4, j, w=CH):
                for hf in range(2):
                    q = 2 * j + hf
                    dve.wait_ge(hi_done, s4 * 8 + (q + 1))
                    tt(w_lo[:, q % HALF_RING, 0:2 * w], raw[:, j % 4, hf * 2 * w:(hf + 1) * 2 * w],
                       w_hi[:, q % HALF_RING, 0:2 * w].bitcast(F32), SUB).then_inc(lo_done, 1)

            def x_gain(n, c):
                if n == 0:
                    for t in range(TT):
                        dve.wait_ge(x_in_sem[t], 16)
                elif c == 0:
                    if n > 1:
                        dve.wait_ge(S("act_turned"), sum(PAIRS) * (n // 2))
                else:
                    dve.wait_ge(S("x_turned"), 4 * n + c)
                dve.wait_ge(gain_in, 16 * (n + 1))
                vs(tt(xg_tile(n, c), x[:, :, c * CH:(c + 1) * CH], over(gain[:, c * CH:(c + 1) * CH], TT, CH), MUL),
                   "xg_ready", 4 * n + c + 1)

            def x_lo(n, c):
                dve.wait_ge(S("hT_hi_ready"), 4 * n + c + 1)
                tt(hT_lo[:, 4 * c:4 * c + 4, :], bank(x_turn_bank(n, c), 2).rearrange("p (k t) -> p k t", k=4),
                   hT_hi[:, 4 * c:4 * c + 4, :].bitcast(F32), SUB).then_inc(S("hT_ready"), 1)

            def norm_tail(n, j):
                if j == 3:
                    x_lo(n, 3)
                if j == 4:
                    dve.wait_ge(S("x_squares"), 8 * (n + 1))
                    v(red(small[:, 222:224], small[:, 208:216].rearrange("p (t c) -> p t c", t=TT), AX.X, ADD))
                    vs(ts(small[:, 216:218], small[:, 222:224], 1.0 / D, EPS, MUL, ADD), "x_var", n + 1)
                if j == 5:
                    dve.wait_ge(S("x_std"), n + 1)
                    vs(rec(rstd, small[:, 218:220]), "rstd_ready", n + 1)

            def add_x(s, j, c, n_added):
                b0 = 2 * (c % 2)
                dve.wait_ge(half_used, chunk_ends(s, j))
                xs = x[:, :, c * CH:(c + 1) * CH]
                vs(tt(xs, xs, psum[:, b0:b0 + 2, :], ADD), "x_added", n_added)
                dve.sem_inc(acc_free[b0 // 2], 1)

            def tables():
                dve.wait_ge(pos_in, 16)
                dve.wait_ge(con_in, 16)
                v(cp(small[:, 202:204], small[:, 200:202].bitcast(I32)))
                ang = small[:, 72:136].rearrange("p (t n) -> p t n", t=TT)
                co = small[:, 8:72]
                turns = arena[:, HG_AT:HG_AT + 64]
                for t in range(TT):
                    v(ts(ang[:, t, :], C("inv_freq"), small[:, 202 + t:203 + t], None, MUL))
                ang = small[:, 72:136]
                v(ts(turns, ang, 1.0 / (2 * np.pi), MAGIC, MUL, ADD))
                v(ts(turns, turns, MAGIC, None, SUB))
                for part in (6.28125, 0.0019340515136718750, 1.2556659146e-06):
                    v(stt(ang, turns, -part, ang, MUL, ADD))
                v(ts(ang, ang, 3.1415925, -3.1415925, ALU.min, MAX))
                v(stt(co, ang, -1.0, ang, MUL, MAX))
                vs(ts(co, co, -1.0, float(np.pi / 2), MUL, ADD), "angle_ready", 1)
                dve.sem_inc(S("angle_ready"), 1)
                dve.wait_ge(par_in, 16)
                lb0, lb1 = par_of(0, "hg_lb"), par_of(1, "hg_lb")
                v(tt(small[:, 136:140], lb0, lb1, MAX))
                v(tt(small[:, 144:148], lb0, small[:, 136:140], SUB))
                vs(tt(small[:, 148:152], lb1, small[:, 136:140], SUB), "lb_shifted", 1)
                dve.wait_ge(S("lb_exp"), 1)
                v(tt(small[:, 136:140], small[:, 144:148], small[:, 148:152], ADD))
                v(rec(small[:, 140:144], small[:, 136:140]))
                v(tt(small[:, 144:148], small[:, 144:148], small[:, 140:144], MUL))
                v(tt(small[:, 148:152], small[:, 148:152], small[:, 140:144], MUL))
                v(tt(derived[:, 0, 0:4], small[:, 144:148], small[:, 144:148], SUB))
                v(tt(derived[:, 1, 0:4], small[:, 144:148], small[:, 148:152], ADD))
                v(tt(derived[:, 1, 0:4], derived[:, 1, 0:4], small[:, 144:148], SUB))
                for l in range(DEPTH):
                    v(ts(derived[:, l, 4:8], derived[:, l, 0:4], -1.0, 1.0, MUL, ADD))
                    v(ts(derived[:, l, 8:12], par_of(l, "k_a"), -1.0, 1.0, MUL, ADD))
                dve.sem_inc(S("derived_ready"), 1)

            for l in range(DEPTH):
                ev = l + 1
                s4 = l * SPLIT_PER_LAYER // 4

                def store_p(c):
                    w = IN_CHUNKS[c][1]
                    dst = (p_hg[:, :, c * CH:(c + 1) * CH] if c < 4 else p_mla[:, :, 0:512] if c == 4
                           else p_rw[:, :, (c - 5) * CH:(c - 4) * CH] if c < 8
                           else p_mla[:, :, 512:832] if c == 8 else p_rw[:, :, 1536:1792])
                    dve.wait_ge(half_used, chunk_ends(s4, 4 * c + 4))
                    for t in range(TT):
                        u(ts(dst[:, t, :], psum[:, 2 * (c % 2) + t, 0:w], rstd[:, t:t + 1], None, MUL))
                    settle()
                    dve.sem_inc(acc_free[c % 2], 1)
                    dve.sem_inc(S("p_ready"), 1)

                def acc_base(layer):
                    return layer * (len(IN_CHUNKS) // 2 + 2 + sum(PAIRS) + 4)

                def exponent(k):
                    m = HG_LEVELS[k]
                    if k >= 4:
                        dve.wait_ge(S("hg_level_mm"), 8 * l + max(2, k - 3))
                    e = hg_e[k % 4].rearrange("p h (n two m) -> p (h n) two m", two=2, m=m)
                    b = hg_b.rearrange("p h (n two m) -> p (h n) two m", two=2, m=m)
                    n = 1024 // (2 * m)
                    r = b[:, :, 0, m - 1:m].broadcast_to([P, n, m])
                    v(tt(e[:, :, 0, :], r, b[:, :, 0, :], SUB))
                    vs(tt(e[:, :, 1, :], b[:, :, 1, :], r, SUB), "hg_exponent", 8 * l + k + 1)

                def factors(k):
                    m = HG_LEVELS[k]
                    dve.wait_ge(S("hg_exp"), 8 * l + k + 1)
                    if k < 2:
                        dst, src = ((hg_kend, hg_k), (hg_qbeg, hg_q))[k]
                        v(tt(dst, dst, src, MUL))
                        if k == 1:
                            dve.sem_inc(S("hg_factors"), 1)
                        return
                    e, kk, qq = (z.rearrange("p h (n two m) -> p (h n) two m", two=2, m=m)
                                 for z in (hg_e[k % 4], hg_k, hg_q))
                    v(tt(e[:, :, 0, :], e[:, :, 0, :], kk[:, :, 0, :], MUL))
                    vs(tt(e[:, :, 1, :], e[:, :, 1, :], qq[:, :, 1, :], MUL), "hg_factors", 7 * l + k)

                def masked(k):
                    dve.wait_ge(S("hg_level_mm"), 8 * l + k + 1)
                    vs(nc.vector.copy_predicated(hg_diag[:, :, :], over(hg_masks[:, k, :], 8, P).bitcast(U32),
                                                 bank(4 + 2 * (k % 2), 2).rearrange("p (n t) -> p n t", n=8)),
                       "hg_masked", 8 * l + k + 1)

                flat = "p h t -> p (h t)"
                if l == 0:
                    for c in range(3):
                        x_gain(0, c)
                    for c in range(3):
                        x_lo(0, c)
                for j in range(N_IN):
                    if j == 2:
                        if l:
                            add_x(s4, 0, 3, 12 * l)
                        x_gain(2 * l, 3)
                    elif j % 4 == 2:
                        store_p(j // 4 - 1)
                    if l == 0 and j == 8:
                        tables()
                    split_lo(s4, j, IN_CHUNKS[j // 4][1])
                    norm_tail(2 * l, j)

                    if j == HG_GATES:
                        dve.wait_ge(S("hg_turned"), 2 * ev)
                        v(nc.vector.memset(hg_diag[:, :, :], 0.0))
                        dve.wait_ge(S("hg_sig_ready"), 2 * l + 1)
                        vs(ts(hg_sig[:, :, :], hg_sig[:, :, :], TINY, None, MAX), "hg_sig_floor", ev)
                        dve.wait_ge(S("hg_sig_ready"), 2 * l + 2)
                        dve.wait_ge(S("derived_ready"), 1)
                        v(tt(hg_k, hg_k, along(derived[:, l, 4:8], SEQ), MUL))
                        dve.wait_ge(S("hg_q_ready"), ev)
                        dve.sem_inc(S("hg_qk_ready"), 1)
                    if j == HG_LOGF:
                        dve.wait_ge(S("hg_logf"), 4 * ev)
                        v(nc.vector.tensor_tensor_scan(hg_b.rearrange(flat), C("reset"), hg_logf.rearrange(flat), 0.0,
                                                       MUL, ADD))
                        b4 = hg_b.rearrange("p h (c i) -> p (h c) i", i=64)
                        v(tt(hg_kend.rearrange("p h (c i) -> p (h c) i", i=64),
                             b4[:, :, 63:64].broadcast_to([P, JC, 64]), b4, SUB))
                        dve.sem_inc(S("hg_exponent"), 2)
                    for k in range(8):
                        if j == HG_LEVEL_SLOT[k] + 3:
                            masked(k)
                        if k and j == HG_LEVEL_SLOT[k]:
                            if k == 1:
                                factors(0)
                            factors(k)
                        if k >= 2 and j == HG_LEVEL_SLOT[k] - 2:
                            exponent(k)
                    if j == HG_CROSS:
                        dve.wait_ge(S("hg_total_exp"), ev)
                        tot = small[:, 160:176].rearrange("p (h c) -> p h c", h=4)
                        v(tt(hg_k128[:, :, 0:64], hg_kend[:, :, 0:64], tot[:, :, 1:2].broadcast_to([P, 4, 64]), MUL))
                        v(cp(hg_k128[:, :, 64:128], hg_kend[:, :, 64:128]))
                        v(cp(hg_q128[:, :, 0:64], hg_qbeg[:, :, 128:192]))
                        v(tt(hg_q128[:, :, 64:128], hg_qbeg[:, :, 192:256], tot[:, :, 2:3].broadcast_to([P, 4, 64]), MUL))
                        dve.sem_inc(S("hg_cross_factors"), 1)
                    if j == HG_GAIN:
                        dve.wait_ge(row_in, 16 * ev)
                        dve.wait_ge(S("hg_gate_silu"), ev)
                        for t in range(TT):
                            g3 = hg_gate[:, t, :].rearrange("p (h n) -> p h n", n=P)
                            u(tt(g3, g3, over(row[:, 0:128], 4, P), MUL))
                        settle()
                        dve.sem_inc(S("hg_gate_ready"), 1)
                    if j == HG_SQUARES:
                        dve.wait_ge(S("hg_squares"), ev)
                        v(red(small[:, 176:184], hg_sq.rearrange("p h (d n) -> p (h d) n", n=P), AX.X, ADD))
                        vs(ts(small[:, 184:192], small[:, 176:184], 1.0 / P, EPS, MUL, ADD), "hg_var", ev)
                    if j == HG_NORMED:
                        dve.wait_ge(S("hg_std"), ev)
                        v(rec(small[:, 176:184], small[:, 192:200]))
                        o3 = hg_o.rearrange("p t (h n) -> p (t h) n", n=P)
                        v(tt(o3, bank(4, 2).rearrange("p (n v) -> p n v", n=8), along(small[:, 176:184], P), MUL))
                        vs(tt(hg_o, hg_o, hg_gate, MUL), "hg_o_ready", ev)
                store_p(len(IN_CHUNKS) - 1)
                dve.wait_ge(S("hg_mix_hi"), ev)
                vs(tt(hT_lo[:, 0:4, :], bank(6, 2).rearrange("p (h t) -> p h t", h=4), hT_hi[:, 0:4, :].bitcast(F32), SUB),
                   "hg_o_used", ev)

                dve.wait_ge(S("mla_in_squares"), 6 * ev)
                for k, n in enumerate((Q_RANK, KV_RANK, ROPE)):
                    v(ts(small[:, 16 + 2 * k:18 + 2 * k], small[:, 8 + 2 * k:10 + 2 * k], 1.0 / n, EPS, MUL, ADD))
                dve.sem_inc(S("mla_in_var"), 1)
                dve.wait_ge(S("mla_in_std"), ev)
                v(rec(small[:, 8:14], small[:, 24:30]))
                for t in range(TT):
                    v(ts(p_mla[:, t, 0:512], p_mla[:, t, 0:512], small[:, 8 + t:9 + t], None, MUL))
                    v(ts(p_mla[:, t, 512:768], p_mla[:, t, 512:768], small[:, 10 + t:11 + t], None, MUL))
                dve.sem_inc(S("mla_in_normed"), 1)
                for t in range(TT):
                    v(ts(rb[:, t, 512:576], p_mla[:, t, 768:832], small[:, 12 + t:13 + t], None, MUL))
                dve.wait_ge(S("mla_q_squares"), ev)
                sq3 = mla_sq.rearrange("p (n d) -> p n d", d=QK)
                v(red(small[:, 32:48], sq3[:, :, 0:NOPE], AX.X, ADD))
                v(red(small[:, 48:64], sq3[:, :, NOPE:QK], AX.X, ADD))
                dve.wait_ge(S("mla_k_squares"), ev)
                v(red(small[:, 64:80], k_sq, AX.X, ADD))
                v(ts(small[:, 32:48], small[:, 32:48], 1.0 / NOPE, EPS, MUL, ADD))
                v(ts(small[:, 48:64], small[:, 48:64], 1.0 / ROPE, EPS, MUL, ADD))
                vs(ts(small[:, 64:80], small[:, 64:80], 1.0 / NOPE, EPS, MUL, ADD), "mla_var", ev)
                dve.wait_ge(S("mla_std"), ev)
                v(rec(small[:, 32:80], small[:, 80:128]))
                q3 = qrow.rearrange("p t (h d) -> p (t h) d", d=QK)
                v(tt(q3[:, :, 0:NOPE], q3[:, :, 0:NOPE], along(small[:, 32:48], NOPE), MUL))
                dve.sem_inc(S("mla_q_normed"), 1)
                k3 = kvrow.rearrange("p t (h d) -> p (t h) d", d=256)[:, :, 0:NOPE]
                v(tt(k3, k3, along(small[:, 64:80], NOPE), MUL))
                dve.sem_inc(S("mla_k_normed"), 1)
                q4 = qrow.rearrange("p t (h d) -> p t h d", d=QK)
                rb4 = rb.rearrange("p t (h d) -> p t h d", d=ROPE)
                ro4 = ro.rearrange("p t (h d) -> p t h d", d=ROPE)
                for t in range(TT):
                    v(tt(rb4[:, t, 0:8, :], q4[:, t, :, NOPE:QK], along(small[:, 48 + 8 * t:56 + 8 * t], ROPE), MUL))
                    v(tt(rb[:, t, 0:576], rb[:, t, 0:576], row[:, 128:704], MUL))
                for t in range(TT):
                    x1, x2 = rb4[:, t, 0:9, 0:32], rb4[:, t, 0:9, 32:64]
                    co_, si_ = over(cs[:, 0, t, :], 9, 32), over(cs[:, 1, t, :], 9, 32)
                    dve.wait_ge(S("cs_ready"), 2)
                    v(tt(ro4[:, t, 0:9, 0:32], x1, co_, MUL))
                    v(tt(rtmp[:, t, :, :], x2, si_, MUL))
                    v(tt(ro4[:, t, 0:9, 0:32], ro4[:, t, 0:9, 0:32], rtmp[:, t, :, :], SUB))
                    v(tt(ro4[:, t, 0:9, 32:64], x2, co_, MUL))
                    v(tt(rtmp[:, t, :, :], x1, si_, MUL))
                    v(tt(ro4[:, t, 0:9, 32:64], ro4[:, t, 0:9, 32:64], rtmp[:, t, :, :], ADD))
                    v(cp(ro4[:, t, 9, :], ro4[:, t, 8, :]))
                dve.sem_inc(S("mla_rope_done"), 1)
                dve.wait_ge(S("mla_k_turned"), ev)
                vs(ts(knT.rearrange(flat), bank(4, 4), par_of(l, "gk"), None, MUL), "mla_kT_ready", ev)
                for k in range(2):
                    dve.wait_ge(S("mla_s_mm"), 8 * l + 4 * k + 4)
                    vs(stt(scores[:, 4 * k:4 * k + 4, :], psum[:, 4 * k:4 * k + 4, 0:384], float(QK ** -0.5),
                           over(C("attn"), 4, 384), MUL, ADD), "mla_scores_out", 2 * l + k + 1)
                s0, s1 = scores[:, :, 0:128], scores[:, :, 128:384]
                v(red(small[:, 32:40], s0, AX.X, MAX))
                v(red(small[:, 40:48], s1, AX.X, MAX))
                v(tt(s0, s0, along(small[:, 32:40], 128), SUB))
                v(tt(s1, s1, along(small[:, 40:48], 256), SUB))
                dve.sem_inc(S("mla_shifted"), 1)
                dve.wait_ge(S("mla_exp"), ev)
                v(red(small[:, 32:40], s0, AX.X, ADD))
                v(red(small[:, 40:48], s1, AX.X, ADD))
                v(rec(small[:, 48:64], small[:, 32:48]))
                v(tt(s0, s0, along(small[:, 48:56], 128), MUL))
                v(tt(s1, s1, along(small[:, 56:64], 256), MUL))
                dve.sem_inc(S("mla_probs"), 1)
                dve.wait_ge(S("mla_mix_hi"), ev)
                vs(tt(hT_lo[:, 4:12, :], bank(0, 4).rearrange("p (h t) -> p h t", h=8), hT_hi[:, 4:12, :].bitcast(F32), SUB),
                   "mla_mix_lo", ev)

                v(nc.vector.memset(pT[:, :, 0:1], 0.0))
                dve.wait_ge(S("rw_pT_ready"), 2 * ev)
                v(tt(pm, pT[:, :, 0:SEQ], pT[:, :, 1:SEQ + 1], SUB))
                for f in range(RW_F):
                    u(stt(pm[:, f, :], pm[:, f, :], par_of(l, "mu")[:, f:f + 1], pT[:, f, 1:SEQ + 1], MUL, ADD))
                settle()
                dve.sem_inc(S("rw_shifted"), 1)
                v(tt(rw_kk, rw_k, along(par_of(l, "k_k"), SEQ), MUL))
                v(tt(rw_b, rw_kk, rw_kk, MUL))
                for j in range(4):
                    u(ts(rkb[:, j, :], C("ones2"), par_of(l, "r_k")[:, j:j + 1], None, MUL))
                settle()
                dve.sem_inc(S("rw_kk_squares"), 1)
                if l:
                    dve.wait_ge(S("rw_vmix_ready"), 4 * l)
                    v(tt(rw_e[2], v_first[:, :, :], rw_v, SUB))
                    v(tt(rw_e[2], rw_e[2], rw_e[0], MUL))
                    v(tt(rw_v, rw_v, rw_e[2], ADD))
                else:
                    v(cp(v_first[:, :, :], rw_v))
                dve.sem_inc(S("rw_v_ready"), 1)
                dve.wait_ge(S("rw_kk_norm"), ev)
                v(ts(rw_e[1], rw_e[1], 1e-12, None, MAX))
                v(rec(rw_e[1], rw_e[1]))
                v(tt(rw_kk, rw_kk, rw_e[1], MUL))
                dve.wait_ge(S("rw_a_ready"), 4 * ev)
                for j in range(4):
                    v(ts(rw_e[2][:, j, :], rw_a[:, j, :], par_of(l, "k_a")[:, j:j + 1], derived[:, l, 8 + j:9 + j], MUL, ADD))
                v(tt(rw_k, rw_k, rw_e[2], MUL))
                v(tt(rw_a, rw_a, rw_kk, MUL))
                v(tt(rw_e[2], rw_r, rw_k, MUL))
                dve.sem_inc(S("rw_rk"), 1)
                dve.wait_ge(S("rw_w_ready"), 4 * ev)
                v(nc.vector.tensor_tensor_scan(rw_b.rearrange(flat), C("reset"), rw_w.rearrange(flat), 0.0, MUL, ADD))
                b3 = rw_b.rearrange("p j (c i) -> p (j c) i", i=RC)
                v(ts(small[:, 32:48], b3[:, :, RC - 1], 0.5, None, MUL))
                v(tt(b3, b3, along(small[:, 32:48], RC), SUB))
                dve.sem_inc(S("rw_exponent"), 2)
                dve.wait_ge(S("rw_bonus_mm"), ev)
                v(tt(rw_bonus.rearrange(flat), bank(2, 2), rw_v.rearrange(flat), MUL))
                v(tt(rw_e[2], rw_b, rw_w, SUB))
                dve.sem_inc(S("rw_exponent"), 1)
                dve.wait_ge(S("rw_exp"), 3 * l + 1)
                r3, k3r, kk3, b3r, e0, e1, e2 = (z.rearrange("p j (c i) -> p (j c) i", i=RC) for z in (
                    rw_r, rw_k, rw_kk, rw_a, rw_e[0], rw_e[1], rw_e[2]))
                vs(tt(ar[:, :, 1, :], r3, e0, MUL), "rw_r_done", ev)
                dve.wait_ge(S("rw_exp"), 3 * l + 2)
                vs(tt(rw_a, rw_a, rw_e[1], MUL), "rw_b_done", ev)
                cp(diag_b[ODD, :, ODD], b3r[ODD, :, :]).then_inc(S("rw_diag_dve"), 1)
                dve.wait_ge(S("rw_exp"), 3 * l + 3)
                for hp in (EVEN, ODD):
                    tt(diag_k[hp, :, hp], k3r[hp, :, :], e1[hp, :, :], MUL).then_inc(S("rw_diag_dve"), 1)
                dve.wait_ge(S("rw_diag_dve"), 4 * l + 3)
                vs(tt(ar[:, :, 0, :], kk3, e2, MUL), "rw_ab_done", ev)
                cp(diag_a[ODD, :, ODD], ar[ODD, :, 0, :]).then_inc(S("rw_diag_dve"), 1)
                dve.wait_ge(S("rw_half_decay"), ev)
                hd = small[:, 48:64].rearrange("p (j c) -> p j c", j=4)
                md = small[:, 64:80].rearrange("p (j c) -> p j c", j=4)
                v(tt(md[:, :, 0:3], hd[:, :, 0:3], hd[:, :, 1:4], MUL))
                left4, right4 = (bank(b0, 4).rearrange("p (n two t) -> p n two t", n=JC, two=2) for b0 in (0, 4))
                for k, (dst, src, mask, product) in enumerate((
                        (mab, bank(6, 2).rearrange("p (n t) -> p n t", n=JC), "strict_lo", 1),
                        (mab_t, left4[:, :, 0, :], "strict_up", 2), (mrb_t, left4[:, :, 1, :], "incl_up", 2),
                        (mak_t, right4[:, :, 0, :], "strict_up", 3), (mrk_t, right4[:, :, 1, :], "incl_up", 3))):
                    dve.wait_ge(S("rw_m_mm"), 3 * l + product)
                    vs(tt(dst, src, over(C(mask), JC, RC), MUL), "rw_m_ready", 5 * l + k + 1)
                    if k == 2:
                        v(tt(inv, mab, over(C("pair_lo"), JC, RC), MUL))
                        v(stt(inv, inv, -1.0, over(idst, JC, RC), MUL, ADD))
                        dve.sem_inc(S("rw_x"), 2)
                        v(tt(inv_t, mab_t, over(C("pair_up"), JC, RC), MUL))
                        v(stt(inv_t, inv_t, -1.0, over(idst, JC, RC), MUL, ADD))
                        dve.sem_inc(S("rw_xt"), 2)
                        for hf in range(2):
                            h8 = slice(8 * hf, 8 * hf + 8)
                            cp(diag_x[ODD, h8, ODD], inv[ODD, h8, :]).then_inc(S("rw_diag_x_dve"), 1)
                for k in range(len(RW_LEVELS)):
                    last = k == len(RW_LEVELS) - 1
                    for hf in range(2):
                        if not last:
                            h8 = slice(8 * hf, 8 * hf + 8)
                            dve.wait_ge(S("rw_gt_ready"), 10 * l + 2 * k + hf + 1)
                            cp(diag_g[ODD, h8, ODD], g_t[ODD, h8, :]).then_inc(S("rw_diag_g_dve"), 1)
                    for hf in range(2):
                        h8 = slice(8 * hf, 8 * hf + 8)
                        dve.wait_ge(S("rw_dinv_mm"), 10 * l + 2 * k + hf + 1)
                        if not last:
                            vs(tt(inv[:, h8, :], inv[:, h8, :], bank(2 + hf).rearrange("p (n t) -> p n t", n=8), SUB),
                               "rw_x", 10 * l + 2 * k + hf + 3)
                            cp(diag_x[ODD, h8, ODD], inv[ODD, h8, :]).then_inc(S("rw_diag_x_dve"), 1)
                        tt(inv_t[:, h8, :], inv_t[:, h8, :], bank(4 + hf).rearrange("p (n t) -> p n t", n=8), SUB).then_inc(
                            S("rw_xt"), 1)
                dve.wait_ge(S("rw_xt"), 12 * ev)
                for c in range(NC):
                    dve.wait_ge(S("rw_rhs_mm"), NC * l + c + 1)
                    vs(ts(rhs.rearrange("p a b -> p (a b)"), bank(0)[:, 0:256], -1.0, None, MUL), "rw_rhs_ready", NC * l + c + 1)
                    if c < NC - 1:
                        dve.wait_ge(S("rw_state_mm"), 3 * l + c + 1)
                        st = bank(2)[:, 0:256].rearrange("p (j n) -> p j n", j=4)
                        if c == 0:
                            v(tt(state[1], st, md[:, :, 0:1].broadcast_to([P, 4, RC]), MUL))
                        else:
                            v(tt(rhs, state[c % 2], st, ADD))
                            v(tt(state[(c + 1) % 2], rhs, md[:, :, c:c + 1].broadcast_to([P, 4, RC]), MUL))
                        dve.sem_inc(S("rw_state_ready"), 1)
                dve.wait_ge(S("rw_y_mm"), ev)
                y3 = bank(6, 2).rearrange("p (n v) -> p n v", n=JC)
                v(red(small[:, 80:96], y3, AX.X, ADD))
                v(ts(small[:, 80:96], small[:, 80:96], 1.0 / RC, None, MUL))
                v(tt(yc, y3, along(small[:, 80:96], RC), SUB))
                dve.sem_inc(S("rw_y_centred"), 1)
                dve.wait_ge(S("rw_y_squares"), ev)
                v(red(small[:, 80:96], ysq, AX.X, ADD))
                vs(ts(small[:, 96:112], small[:, 80:96], 1.0 / RC, GN_EPS, MUL, ADD), "rw_y_var", ev)
                dve.wait_ge(S("rw_y_std"), ev)
                v(rec(small[:, 80:96], small[:, 112:128]))
                v(tt(yc, yc, along(small[:, 80:96], RC), MUL))
                dve.sem_inc(S("rw_y_normed"), 1)
                dve.wait_ge(S("rw_y_turned"), ev)
                for j in range(4):
                    u(ts(y_out[:, j, :], bank(0, 2)[:, j * SEQ:(j + 1) * SEQ], par_of(l, "ln_w")[:, j:j + 1],
                         par_of(l, "ln_b")[:, j:j + 1], MUL, ADD))
                settle()
                v(tt(y_out, y_out, rw_bonus, ADD))
                dve.wait_ge(S("rw_g_ready"), ev)
                v(tt(y_out, y_out, rw_g, MUL))
                dve.sem_inc(S("rw_out"), 1)
                dve.wait_ge(S("rw_mix_hi"), ev)
                vs(tt(hT_lo[:, 12:16, :], y_out, hT_hi[:, 12:16, :].bitcast(F32), SUB), "rw_mix_lo", ev)

                s4o = s4 + N_IN // 4

                for c in range(4):
                    for j in range(4):
                        if j == 2 and c:
                            add_x(s4o, 4 * c, c - 1, 12 * l + c)
                            x_gain(2 * l + 1, c - 1)
                        split_lo(s4o, 4 * c + j)
                        if c == 0:
                            cp(act_lo[:, 4 * j:4 * j + 4, :], hT_lo[:, 4 * j:4 * j + 4, :].bitcast(F32)).then_inc(
                                S("mix_lo_kept"), 1)
                        elif j == 3:
                            x_lo(2 * l + 1, c - 1)

                s4f = s4o + N_O // 4
                pair0 = sum(PAIRS) * l
                odd0 = acc_base(l) + len(IN_CHUNKS) // 2 + 2

                for n, pairs in enumerate(PAIRS):
                    def act_rows(i, si, p0):
                        dve.wait_ge(half_used, chunk_ends(si, 8))
                        dve.wait_ge(acc_free[0], i + (gate_base + 2))
                        if not isinstance(i, int) or i + p0 > 0:
                            dve.wait_ge(S("act_turned"), i + p0)
                        stt(act_row[:, 0, :], psum[:, 2, :], rstd[:, 0:1], silu[:, 0, :], MUL, MUL)
                        stt(act_row[:, 1, :], psum[:, 3, :], rstd[:, 1:2], silu[:, 1, :], MUL, MUL).then_inc(acc_free[1], 1)
                        dve.wait_ge(acc_free[1], i + (gate_base + 2))
                        dve.sem_inc(S("act_row_ready"), 1)

                    def turned_lo(i, p0):
                        dve.wait_ge(S("act_hi_ready"), i + (p0 + 1))
                        k = bass.ds(i * 4, 4) if not isinstance(i, int) else slice(4 * i, 4 * i + 4)
                        tt(act_lo[:, k, :], bank(4, 2).rearrange("p (k t) -> p k t", k=4), act_hi[:, k, :].bitcast(F32),
                           SUB).then_inc(S("act_lo_ready"), 1)

                    gate_base = odd0 + sum(PAIRS[:n]) + 4 * n // 2

                    def pair(i, first):
                        si = i * 2 + s4f
                        for j in range(8):
                            if j == 2 and not first:
                                act_rows(i - 1, si - 2, pair0)
                            if j == 2 and first:
                                add_x(s4f, 0, 3, 12 * l + 4 * (n + 1))
                                if n == 0:
                                    x_gain(2 * l + 1, 3)
                            if j == 6 and not first:
                                turned_lo(i - 1, pair0)
                            split_lo(si, j)
                            if n == 0 and first:
                                norm_tail(2 * l + 1, j)

                    pair(0, True)
                    with dve.Fori(1, pairs) as i:
                        pair(i, False)
                    last_si = s4f + 2 * (pairs - 1)
                    s4f = s4f + 2 * pairs
                    for c in range(4):
                        for j in range(pairs):
                            if j == 2 and c == 0:
                                act_rows(pairs - 1, last_si, pair0)
                            makes_norm = n == len(PAIRS) - 1 and l < DEPTH - 1
                            if j == 2 and c:
                                add_x(s4f, pairs * c, c - 1, 12 * l + 4 * (n + 1) + c)
                                if makes_norm:
                                    x_gain(2 * l + 2, c - 1)
                            split_lo(s4f, pairs * c + j)
                            if j == 3 and c == 0:
                                turned_lo(pairs - 1, pair0)
                            if j == 3 and c and makes_norm:
                                x_lo(2 * l + 2, c - 1)
                    s4f = s4f + pairs
                    pair0 += pairs
                if l == DEPTH - 1:
                    add_x(s4f, 0, 3, 12 * DEPTH)

        @block.tensor
        def _(pe):
            mm, tr = nc.tensor.matmul, nc.tensor.transpose
            pe.sem_inc(half_used, HALF_RING)
            pe.sem_inc(acc_free[0], 1)
            pe.sem_inc(acc_free[1], 1)

            def slots(s4, js, k0, n_k, b0, lhi, llo, w=CH):
                for n, j in enumerate(js):
                    for hf in range(2):
                        q = 2 * j + hf
                        pe.wait_ge(lo_done, s4 * 8 + (q + 1))
                        r = q % HALF_RING
                        for k2 in range(2):
                            k = k0 + 4 * n + 2 * hf + k2
                            cols = slice(k2 * w, (k2 + 1) * w)
                            for t in range(TT):
                                o = psum[:, b0 + t, 0:w]
                                a_hi, a_lo = lhi[:, k, t * P:(t + 1) * P], llo[:, k, t * P:(t + 1) * P]
                                mm(o, a_hi, w_hi[:, r, cols], start=(k == 0), stop=False)
                                mm(o, a_hi, w_lo[:, r, cols], start=False, stop=False)
                                last = mm(o, a_lo, w_hi[:, r, cols], start=False, stop=(k == n_k - 1))
                        last.then_inc(half_used, 1)

            def x_turn(n, c):
                pe.wait_ge(S("xg_ready"), 4 * n + c + 1)
                if n:
                    pe.wait_ge(S("hT_ready"), 4 * n + c)
                for k in range(4):
                    for t in range(TT):
                        last = tr(bank(x_turn_bank(n, c), 2)[:, k * SEQ + t * P:k * SEQ + (t + 1) * P],
                                  xg_tile(n, c)[:, t, k * P:(k + 1) * P], ident)
                last.then_inc(S("x_turned"), 1)

            def first_slot(n, s4, j, b0, w=CH):
                pe.wait_ge(S("hT_ready"), 4 * n + j + 1)
                slots(s4, [j], 4 * j, KT, b0, hT_hi, hT_lo, w)
                if j == 1:
                    x_turn(n, 3)

            def heads(fn):
                last = None
                for p0 in (0, 64):
                    last = fn(slice(p0, p0 + 64))
                return last

            pe.wait_ge(ident_in, 16)
            for l in range(DEPTH):
                ev = l + 1
                s4 = l * SPLIT_PER_LAYER // 4
                acc0 = l * (len(IN_CHUNKS) // 2 + 2 + sum(PAIRS) + 4)
                if l == 0:
                    for c in range(3):
                        x_turn(0, c)

                def level(k):
                    if k >= 2:
                        pe.wait_ge(S("hg_masked"), 8 * l + k - 1)
                    if k == 2:
                        pe.wait_ge(S("hg_cross_ready"), ev)
                    if k == 0:
                        pe.wait_ge(S("hg_qk_ready"), ev)
                    else:
                        pe.wait_ge(S("hg_factors"), 7 * l + k)
                    left, right = ((hg_k, hg_q) if k == 0 else (hg_kend, hg_qbeg) if k == 1 else (hg_e[k % 4],) * 2)
                    for h in range(HG_H):
                        for d in range(TT):
                            n = h * TT + d
                            last = mm(bank(4 + 2 * (k % 2), 2)[:, n * P:(n + 1) * P], left[:, h, d * P:(d + 1) * P],
                                      right[:, h, d * P:(d + 1) * P], start=True, stop=True)
                    last.then_inc(S("hg_level_mm"), 1)

                for j in range(N_IN):
                    c = j // 4
                    if j % 4 == 0:
                        pe.wait_ge(acc_free[c % 2], acc0 + c // 2 + 1)
                    if c == 0:
                        first_slot(2 * l, s4, j, 0)
                    else:
                        slots(s4, [j], 4 * (j % 4), KT, 2 * (c % 2), hT_hi, hT_lo, IN_CHUNKS[c][1])

                    if j == HG_TURN:
                        pe.wait_ge(S("p_ready"), len(IN_CHUNKS) * l + 2)
                        for k in range(2):
                            for h in range(HG_H):
                                for t in range(TT):
                                    last = tr(bank(4 + 2 * k, 2)[:, h * SEQ + t * P:h * SEQ + (t + 1) * P],
                                              p_hg[:, t, k * CH + h * P:k * CH + (h + 1) * P], ident)
                            last.then_inc(S("hg_turned"), 1)
                    for k in range(8):
                        if j == HG_LEVEL_SLOT[k]:
                            level(k)
                    if j == HG_CROSS:
                        pe.wait_ge(S("hg_cross_factors"), ev)
                        pe.wait_ge(S("hg_masked"), 8 * l + 1)
                        for h in range(HG_H):
                            last = mm(bank(4)[:, h * P:(h + 1) * P], hg_k128[:, h, :], hg_q128[:, h, :],
                                      start=True, stop=True)
                        last.then_inc(S("hg_cross_mm"), 1)
                    if j == HG_OUT:
                        pe.wait_ge(S("hg_masked"), 8 * ev)
                        pe.wait_ge(S("p_ready"), len(IN_CHUNKS) * l + 3)
                        for d in range(TT):
                            for h in range(HG_H):
                                o = psum[:, 4 + d, h * P:(h + 1) * P]
                                vv = [p_hg[:, t, 1024 + h * P:1024 + (h + 1) * P] for t in range(TT)]
                                if d:
                                    mm(o, hg_cross[:, h, :], vv[0], start=True, stop=False)
                                last = mm(o, hg_diag[:, h * TT + d, :], vv[d], start=(d == 0), stop=True)
                        last.then_inc(S("hg_o_mm"), 1)
                pe.wait_ge(S("hg_o_ready"), ev)
                for h in range(HG_H):
                    for t in range(TT):
                        last = tr(bank(6, 2)[:, h * SEQ + t * P:h * SEQ + (t + 1) * P], hg_o[:, t, h * P:(h + 1) * P], ident)
                last.then_inc(S("hg_o_turned"), 1)

                pe.wait_ge(S("mla_in_normed"), ev)
                pe.wait_ge(S("p_ready"), len(IN_CHUNKS) * ev)
                for k in range(6):
                    for t in range(TT):
                        last = tr(bank(0, 3)[:, k * SEQ + t * P:k * SEQ + (t + 1) * P], p_mla[:, t, k * P:(k + 1) * P], ident)
                last.then_inc(S("mla_in_turned"), 1)
                pe.wait_ge(S("mla_inT_ready"), 6 * ev)
                g4 = (l * SLOTS_PER_LAYER + N_IN) // 4
                for c in range(8):
                    if c >= 4:
                        pe.wait_ge(S("mla_up_ready"), 8 * l + c - 3)
                    pe.wait_ge(raw_in[c % 4], 16 * (g4 + c // 4 + 1))
                    w, nk, src = (384, 4, qaT) if c < 4 else (CH, 2, kvaT)
                    for t in range(TT):
                        for k in range(nk):
                            last = mm(psum[:, (4 + 2 * c) % 8 + t, 0:w], src[:, k, t * P:(t + 1) * P],
                                      raw[:, c % 4, k * w:(k + 1) * w], start=(k == 0), stop=(k == nk - 1))
                    last.then_inc(S("mla_up_mm"), 1)
                    pe.wait_ge(S("mla_up_mm"), 8 * l + c + 1)
                    pe.sem_inc(plain_used, 1)
                pe.wait_ge(S("mla_up_ready"), 8 * ev)
                for src, b0, off, width, wait, done in ((qrow, 0, 0, QK, "mla_q_normed", "mla_q_turned"),
                                                        (kvrow, 4, 0, 256, "mla_k_normed", "mla_k_turned")):
                    pe.wait_ge(S(wait), ev)
                    for h in range(MLA_H):
                        for t in range(TT):
                            last = tr(bank(b0, 4)[:, h * SEQ + t * P:h * SEQ + (t + 1) * P],
                                      src[:, t, h * width:h * width + NOPE], ident)
                    last.then_inc(S(done), 1)
                pe.wait_ge(S("mla_rope_done"), ev)
                pe.wait_ge(S("mla_qT_ready"), ev)
                for k in range(5):
                    for t in range(TT):
                        last = tr(bank(0, 3)[:, k * SEQ + t * P:k * SEQ + (t + 1) * P], ro[:, t, k * P:(k + 1) * P], ident)
                last.then_inc(S("mla_r_turned"), 1)
                pe.wait_ge(S("mla_kT_ready"), ev)
                pe.wait_ge(S("mla_rT_ready"), 2 * ev)
                for h in range(MLA_H):
                    hp = slice(64 * (h % 2), 64 * (h % 2) + 64)
                    for qt, cols, keys in ((0, slice(0, 128), 128), (1, slice(128, 384), 256)):
                        o = psum[:, h, cols]
                        tq = slice(qt * P, (qt + 1) * P)
                        mm(o, qnT[:, h, tq], knT[:, h, 0:keys], start=True, stop=False)
                        last = mm(o, rT[hp, h // 2, tq], rkT[hp, 0:keys], start=False, stop=True)
                    last.then_inc(S("mla_s_mm"), 1)
                pe.wait_ge(S("mla_probs"), ev)
                for h in range(MLA_H):
                    for n in range(3):
                        last = tr(psum[:, h, n * P:(n + 1) * P], scores[:, h, n * P:(n + 1) * P], ident)
                    last.then_inc(S("mla_p_turned"), 1)
                pe.wait_ge(S("mla_pT_ready"), 2 * ev)
                for h in range(MLA_H):
                    o = bank(0, 4)[:, h * SEQ:(h + 1) * SEQ]
                    vv = [kvrow[:, t, h * 256 + NOPE:(h + 1) * 256] for t in range(TT)]
                    mm(o, vv[0], probsT[:, h, 0:256], start=True, stop=False)
                    last = mm(o[:, 128:256], vv[1], probsT[:, h, 256:384], start=False, stop=True)
                last.then_inc(S("mla_o_mm"), 1)

                for f in range(RW_F):
                    if f == 8:
                        pe.wait_ge(S("mla_mix_lo"), ev)
                    b0 = 4 if f < 8 else 0
                    for t in range(TT):
                        last = tr(bank(b0, 4)[:, (f % 8) * SEQ + t * P:(f % 8) * SEQ + (t + 1) * P],
                                  p_rw[:, t, f * P:(f + 1) * P], ident)
                    if f in (7, 13):
                        last.then_inc(S("rw_turned"), 1)
                pe.wait_ge(lora_in, 16 * ev)
                pe.wait_ge(S("rw_pT_ready"), 2 * ev)
                pe.wait_ge(S("rw_lora_in"), 2 * ev)
                for k, (w, src, hp) in enumerate(((lora_of("wa"), rw_sig, slice(0, 64)), (lora_of("wa"), pm[:, 12, :], slice(64, 128)),
                                                  (lora_of("g2"), rw_tmp[:, 0, :], slice(0, 128)))):
                    for j in range(4):
                        last = mm(bank(2 * k, 2)[:, j * SEQ:(j + 1) * SEQ], w[hp, j * P:(j + 1) * P], src[hp, :],
                                  start=True, stop=True)
                    last.then_inc(S("rw_lora_mm"), 1)
                if l:
                    v1 = lora_of("v1")
                    for k in range(4):
                        last = mm(bank(6)[0:32, 0:SEQ], v1[:, k * 32:(k + 1) * 32], rw_v[:, k, :], start=(k == 0), stop=(k == 3))
                    last.then_inc(S("rw_v1_mm"), 1)
                    pe.wait_ge(S("rw_v1_ready"), l)
                    for j in range(4):
                        last = mm(bank(6, 2)[:, j * SEQ:(j + 1) * SEQ], lora_of("v2")[0:32, j * P:(j + 1) * P],
                                  rw_bonus[0:32, 0, :], start=True, stop=True)
                    last.then_inc(S("rw_v2_mm"), 1)
                pe.wait_ge(S("rw_kk_squares"), ev)
                pe.wait_ge(S("rw_w_ready"), 4 * ev)
                for j in range(4):
                    last = mm(bank(0, 2)[:, j * SEQ:(j + 1) * SEQ], C("ones2"), rw_b[:, j, :], start=True, stop=True)
                last.then_inc(S("rw_kk_mm"), 1)
                pe.wait_ge(S("rw_rk"), ev)
                pe.wait_ge(S("rw_a_ready"), 4 * ev)
                for j in range(4):
                    last = mm(bank(2, 2)[:, j * SEQ:(j + 1) * SEQ], rkb[:, j, :], rw_e[2][:, j, :], start=True, stop=True)
                last.then_inc(S("rw_bonus_mm"), 1)

                def both_heads(b0, ns, left, right, w):
                    last = None
                    for m, n in enumerate(ns):
                        last = mm(bank(b0, 8 - b0)[:, m * w:(m + 1) * w], left[:, n, :], right(n), start=True, stop=True)
                    return last

                def b_of(n):
                    return rw_a[:, n // NC, (n % NC) * RC:(n % NC + 1) * RC]

                def ar_of(n):
                    return ar[:, n, :, :].rearrange("p two i -> p (two i)")

                pe.wait_ge(S("rw_zeroed"), 8 * l + 4)
                pe.wait_ge(S("rw_diag_act"), 4 * l + 2)
                both_heads(0, range(JC), diag_v, lambda n: idst, RC).then_inc(S("rw_stack_mm"), 1)
                pe.wait_ge(S("rw_diag_act"), 4 * l + 3)
                pe.wait_ge(S("rw_diag_dve"), 4 * l + 1)
                pe.wait_ge(S("rw_a_ready"), 4 * ev)
                both_heads(2, range(JC), diag_b, lambda n: idst, RC).then_inc(S("rw_stack_mm"), 1)
                pe.wait_ge(S("rw_zeroed"), 8 * l + 6)
                pe.wait_ge(S("rw_diag_dve"), 4 * l + 3)
                pe.wait_ge(S("rw_g_ready"), ev)
                both_heads(4, range(JC), diag_k, lambda n: idst, RC).then_inc(S("rw_stack_mm"), 1)
                pe.wait_ge(S("rw_zeroed"), 8 * ev)
                pe.wait_ge(S("rw_diag_act"), 4 * ev)
                pe.wait_ge(S("rw_diag_dve"), 4 * ev)
                both_heads(6, range(JC), diag_a, b_of, RC).then_inc(S("rw_m_mm"), 1)
                pe.wait_ge(S("rw_stacked"), 3 * l + 2)
                both_heads(0, range(JC), diag_b, ar_of, 2 * RC).then_inc(S("rw_m_mm"), 1)
                pe.wait_ge(S("rw_stacked"), 3 * ev)
                pe.wait_ge(S("rw_m_ready"), 5 * l + 1)
                both_heads(4, range(JC), diag_k, ar_of, 2 * RC).then_inc(S("rw_m_mm"), 1)
                for k in range(len(RW_LEVELS)):
                    last = k == len(RW_LEVELS) - 1
                    pe.wait_ge(S("rw_level_ready"), 10 * l + 2 * k + 2)
                    for hf in range(2):
                        ns = range(8 * hf, 8 * hf + 8)
                        pe.wait_ge(S("rw_xt"), 12 * l + 2 * k + hf + 1)
                        both_heads(hf, ns, diag_l, lambda n: inv_t[:, n, :], RC).then_inc(S("rw_gt_mm"), 1)
                    if k == 0:
                        pe.wait_ge(S("rw_m_ready"), 5 * ev)
                    for hf in range(2):
                        ns = range(8 * hf, 8 * hf + 8)
                        pe.wait_ge(S("rw_gt_ready"), 10 * l + 2 * k + hf + 1)
                        if not last:
                            pe.wait_ge(S("rw_diag_g_act"), 8 * l + 2 * k + hf + 1)
                            pe.wait_ge(S("rw_diag_g_dve"), 8 * l + 2 * k + hf + 1)
                            both_heads(2 + hf, ns, diag_g, lambda n: inv[:, n, :], RC)
                        pe.wait_ge(S("rw_diag_x_act"), 10 * l + 2 * k + hf + 1)
                        pe.wait_ge(S("rw_diag_x_dve"), 10 * l + 2 * k + hf + 1)
                        both_heads(4 + hf, ns, diag_x, lambda n: g_t[:, n, :], RC).then_inc(S("rw_dinv_mm"), 1)
                pe.wait_ge(S("rw_xt"), 12 * ev)
                for c in range(NC):
                    def each(b0, off, terms):
                        last = None
                        for j in range(4):
                            for hp in (slice(0, 64), slice(64, 128)):
                                for n, (left, right) in enumerate(terms):
                                    last = mm(bank(b0, 2)[hp, off + j * RC:off + (j + 1) * RC], left(hp, j), right(hp, j),
                                              start=(n == 0), stop=(n == len(terms) - 1))
                        return last

                    def in_ar(which):
                        return lambda hp, j: ar[hp, NC * j + c, which, :]

                    def stacked(z):
                        return lambda hp, j: z[hp, NC * j + c, :]

                    def pair_of(z):
                        return lambda hp, j: z[hp, j, :]

                    if c:
                        pe.wait_ge(S("rw_state_ready"), 3 * l + c)
                    carried = [(in_ar(0), pair_of(state[c % 2]))] if c else []
                    each(0, 0, carried + [(stacked(mak_t), stacked(v_st))]).then_inc(S("rw_rhs_mm"), 1)
                    pe.wait_ge(S("rw_rhs_ready"), NC * l + c + 1)
                    each(1, 0, [(stacked(inv_t), pair_of(rhs))]).then_inc(S("rw_sa_mm"), 1)
                    pe.wait_ge(S("rw_sa_ready"), NC * l + c + 1)
                    if c < NC - 1:
                        each(2, 0, [(stacked(b_st), pair_of(sa)), (stacked(k_st), stacked(v_st))]).then_inc(S("rw_state_mm"), 1)
                    carried = [(in_ar(1), pair_of(state[c % 2]))] if c else []
                    last = each(6, 256 * c, carried + [(stacked(mrb_t), pair_of(sa)), (stacked(mrk_t), stacked(v_st))])
                last.then_inc(S("rw_y_mm"), 1)
                pe.wait_ge(S("rw_y_normed"), ev)
                for c in range(NC):
                    for j in range(4):
                        last = heads(lambda hp: mm(bank(0, 2)[hp, j * SEQ + c * RC:j * SEQ + (c + 1) * RC], yc[hp, 4 * c + j, :],
                                                   idst[hp, :], start=True, stop=True))
                last.then_inc(S("rw_y_turned"), 1)

                pe.wait_ge(S("rw_mix_lo"), ev)
                s4o = s4 + N_IN // 4
                acc = acc0 + len(IN_CHUNKS) // 2
                for c in range(4):
                    pe.wait_ge(acc_free[c % 2], acc + c // 2 + 1)
                    if c == 1:
                        pe.wait_ge(S("mix_hi_kept"), 4 * ev)
                        pe.wait_ge(S("mix_lo_kept"), 4 * ev)
                    for j in range(4):
                        slots(s4o, [4 * c + j], 4 * j, KT, 2 * (c % 2), *((act_hi, act_lo) if c else (hT_hi, hT_lo)))
                        if c and j == 1:
                            x_turn(2 * l + 1, c - 1)
                acc += 2

                s4f = s4o + N_O // 4
                pair0 = sum(PAIRS) * l
                for part, pairs in enumerate(PAIRS):
                    makes_norm = part == len(PAIRS) - 1 and l < DEPTH - 1

                    def turn(i, p0):
                        pe.wait_ge(S("act_row_ready"), i + (p0 + 1))
                        if not isinstance(i, int) or i + p0 > 0:
                            pe.wait_ge(S("act_lo_ready"), i + p0)
                        for k in range(4):
                            for t in range(TT):
                                last = tr(bank(4, 2)[:, k * SEQ + t * P:k * SEQ + (t + 1) * P],
                                          act_row[:, t, k * P:(k + 1) * P], ident)
                        last.then_inc(S("act_turned"), 1)

                    def pair(i, first):
                        si = i * 2 + s4f
                        for u in range(2):
                            pe.wait_ge(acc_free[u], i + (acc + 1))
                            if part == 0 and first and u == 0:
                                for j in range(4):
                                    first_slot(2 * l + 1, si, j, 0)
                            else:
                                slots(si, range(4 * u, 4 * u + 4), 0, KT, 2 * u, hT_hi, hT_lo)
                            if u == 0 and not first:
                                turn(i - 1, pair0)

                    pair(0, True)
                    with pe.Fori(1, pairs) as i:
                        pair(i, False)
                    s4f, acc = s4f + 2 * pairs, acc + pairs
                    for c in range(4):
                        pe.wait_ge(acc_free[c % 2], acc + c // 2 + 1)
                        for j in range(pairs):
                            if c == 0 and j == 3:
                                turn(pairs - 1, pair0)
                            if c == 0 and j == pairs - 1:
                                pe.wait_ge(S("act_lo_ready"), pair0 + pairs)
                            slots(s4f, [pairs * c + j], 4 * j, 4 * pairs, 2 * (c % 2), act_hi, act_lo)
                            if makes_norm and c and j == 1:
                                x_turn(2 * l + 2, c - 1)
                    s4f, acc = s4f + pairs, acc + 2
                    pair0 += pairs


def shape_constants():
    i, j = np.arange(P)[:, None], np.arange(P)[None, :]
    out = {"ident": (i == j)}
    masks = []
    for m in HG_LEVELS:
        masks.append((i == j) if m == 0 else
                     (i // (2 * m) == j // (2 * m)) & (i // m % 2 == 0) & (j // m % 2 == 1))
    out["hg_masks"] = np.concatenate(masks, 1)
    low = np.where(j <= i, 0.0, -1e30)
    out["attn"] = np.concatenate([low, np.zeros((P, P)), low], 1)
    out["reset"] = np.broadcast_to((np.arange(1024) % 64 != 0)[None, :], (P, 1024))
    out["ones2"] = (i // 64 == j // 64)
    a, b = (np.arange(P) % RC)[:, None], np.arange(RC)[None, :]
    out["idst"] = a == b
    out["strict_lo"] = a > b
    out["strict_up"] = a < b
    out["incl_up"] = a <= b
    out["pair_lo"] = (a // 2 == b // 2) & (a > b)
    out["pair_up"] = (a // 2 == b // 2) & (a < b)
    out["lev_lo"] = np.concatenate([(a // (2 * m) == b // (2 * m)) & (a // m % 2 == 1) & (b // m % 2 == 0)
                                    for m in RW_LEVELS], 1)
    half = ROPE // 2
    freq = np.float32(10000.0) ** (-np.arange(half, dtype=np.float32) / np.float32(half))
    out["inv_freq"] = np.broadcast_to(freq[None, :], (P, half))
    return np.ascontiguousarray(np.concatenate([np.asarray(out[n], np.float32) for n in CONST_COLS], 1))


def kernel(**inputs):
    import concourse.bacc as bacc
    from concourse.bass_utils import run_bass_kernel_spmd

    a = {k: np.asarray(z) for k, z in inputs.items()}

    def tiles(w, k_rows, cols):
        K, N = w.shape
        t = w.reshape(K // k_rows, k_rows // P, P, N // cols, cols).transpose(3, 0, 2, 1, 4)
        return t.reshape(N // cols, K // k_rows, P, (k_rows // P) * cols)

    def padded(t):
        full = np.zeros(t.shape[:-1] + (4 * CH,), np.float32)
        full[..., :t.shape[-1]] = t
        return full.reshape(-1, P, 4 * CH)

    slots = []
    for l in range(DEPTH):
        for c, w in IN_CHUNKS:
            slots.append(padded(tiles(a["w_in"][l][:, c:c + w], 512, w)))
        slots.append(padded(tiles(a["mla_w_qb"][l], 512, 384)))
        slots.append(padded(tiles(a["mla_w_kvb"][l], 256, CH)))
        slots.append(padded(tiles(a["w_o"][l], 512, CH)))
        first = 0
        for pairs in PAIRS:
            cols = slice(first * CH, (first + pairs) * CH)
            gate = tiles(a["w_gate_up"][l][:, :D_FF][:, cols], 512, CH)
            up = tiles(a["w_gate_up"][l][:, D_FF:][:, cols], 512, CH)
            slots.append(np.stack([gate, up], 1).reshape(-1, P, 4 * CH))
            slots.append(padded(tiles(a["w_down"][l][cols], 512, CH)))
            first += pairs
    stream = np.concatenate(slots, 0)
    assert stream.shape[0] == DEPTH * SLOTS_PER_LAYER

    def cols(z):
        return z.reshape(-1, P).T

    params, lora, rows, gains = [], [], [], []
    for l in range(DEPTH):
        qn, kn = a["mla_q_norm"][l], a["mla_k_norm"][l]
        par = dict(hg_lb=cols(a["hg_lower_bounds"][l]), q_a=cols(a["mla_q_a_norm"][l]), kv_a=cols(a["mla_kv_a_norm"][l]),
                   gq=cols(qn[:NOPE]), gk=cols(kn[:NOPE]), mu=cols(a["rw_mu"][l]), w0=cols(a["rw_w0"][l]),
                   a0=cols(a["rw_a0"][l]), v0=cols(a["rw_v0"][max(l - 1, 0)]), k_k=cols(a["rw_k_k"][l]),
                   k_a=cols(a["rw_k_a"][l]), r_k=cols(a["rw_r_k"][l].reshape(-1)), ln_w=cols(a["rw_ln_w"][l]),
                   ln_b=cols(a["rw_ln_b"][l]))
        params.append(np.concatenate([par[n] for n in PARAM_COLS], 1))
        v1 = a["rw_v1"][max(l - 1, 0)].reshape(4, P, 32).transpose(1, 0, 2).reshape(P, 128)
        v2 = a["rw_v2"][max(l - 1, 0)]
        lora.append(np.concatenate([np.concatenate([a["rw_w2"][l], a["rw_a2"][l]], 0), a["rw_g2"][l], v1,
                                    np.concatenate([v2] * 4, 0)], 1))
        rows.append(np.concatenate([a["hg_out_norm"][l]] + [qn[NOPE:]] * MLA_H + [kn[NOPE:]]))
        gains += [a["attn_norm"][l], a["ffn_norm"][l]]
    arrays = dict(
        stream=stream, x_in=a["x"].reshape(SEQ, D), positions=np.ascontiguousarray(a["positions"].reshape(TT, P).T),
        params=np.ascontiguousarray(np.concatenate(params, 1)), consts=shape_constants(),
        lora=np.stack(lora), gains=np.stack(gains), rows=np.stack(rows))
    nc = bacc.Bacc("TRN2", target_bir_lowering=False, num_devices=1)
    args = {n: nc.dram_tensor(n + "_dram", z.shape, mybir.dt.from_np(z.dtype), kind="ExternalInput").ap()
            for n, z in arrays.items()}
    out = nc.dram_tensor("out_dram", (SEQ, D), F32, kind="ExternalOutput").ap()
    build(nc, out=out, **args)
    r = run_bass_kernel_spmd(nc, [{n + "_dram": z for n, z in arrays.items()}], core_ids=[0])
    return r.results[0]["out_dram"].reshape(1, SEQ, D)
```

```python
from contextlib import ExitStack

import numpy as np

import concourse.bass as bass
from concourse import mybir

F32 = mybir.dt.float32
F32R = mybir.dt.float32r
U32 = mybir.dt.uint32
I32 = mybir.dt.int32
ALU = mybir.AluOpType
ACT = mybir.ActivationFunctionType
AX = mybir.AxisListType

P = 128
D = 2048
SEQ = 256
TT = SEQ // P
DEPTH = 2
KT = D // P
CH = 512

HG_H = 4
MLA_H = 8
NOPE = 128
ROPE = 64
QK = NOPE + ROPE
Q_RANK = 512
KV_RANK = 256
D_FF = 5632
RW_IN = 1792
RW_F = RW_IN // P
RC = 64
NC = SEQ // RC
JC = 4 * NC
IN_W = 4672
EPS = 1e-6
GN_EPS = 64e-5
C0 = float(np.exp(np.float32(-0.5)))
MAGIC = 12582912.0
TINY = float(2.0 ** -63)

IN_CHUNKS = [(c * CH, CH) for c in range(5)] + [(2560, 320)] + [(2880 + c * CH, CH) for c in range(3)] + [(4416, 256)]
PAIRS = [6, 5]
RAW_SLOTS = 4
HALF_RING = 4
N_IN = len(IN_CHUNKS) * 4
N_PLAIN = 8
N_O = 16
N_FFN = sum(8 * p + 4 * p for p in PAIRS)
SPLIT_PER_LAYER = N_IN + N_O + N_FFN
SLOTS_PER_LAYER = SPLIT_PER_LAYER + N_PLAIN
FFN_AT = N_IN + N_PLAIN + N_O
assert N_IN % 4 == N_PLAIN % 4 == N_O % 4 == N_FFN % 4 == 0

PARAM_COLS = dict(hg_lb=4, q_a=4, kv_a=2, gq=1, gk=1, mu=14, w0=4, a0=4, v0=4, k_k=4, k_a=4, r_k=4, ln_w=4, ln_b=4)
CONST_COLS = dict(ident=128, hg_masks=8 * 128, attn=384, reset=1024, ones2=128, idst=64, strict_lo=64,
                  strict_up=64, incl_up=64, pair_lo=64, pair_up=64, lev_lo=5 * 64, inv_freq=32)
LORA_COLS = dict(wa=512, g2=512, v1=128, v2=512)
HG_LEVELS = [0, 64, 32, 16, 8, 4, 2, 1]
RW_LEVELS = [2, 4, 8, 16, 32]

HG_LEVEL_SLOT = [14, 17, 20, 21, 23, 24, 26, 27]
HG_TURN, HG_GATES, HG_LOGF, HG_CROSS, HG_CROSS_OUT, HG_SILU, HG_GAIN, HG_OUT = 11, 14, 15, 18, 21, 24, 28, 30
HG_SQUARES, HG_STD, HG_NORMED = 33, 34, 35
MLA_SQUARES, MLA_STD, MLA_NORMED, MLA_TURN_Q, MLA_Q_OUT, MLA_TURN_KV, MLA_KV_OUT = 28, 29, 31, 32, 35, 36, 39


def offsets(cols):
    at, out = 0, {}
    for name, n in cols.items():
        out[name] = (at, at + n)
        at += n
    return out, at


PAR, N_PAR = offsets(PARAM_COLS)
CON, N_CON = offsets(CONST_COLS)
LOR, N_LOR = offsets(LORA_COLS)


def build(nc, stream, x_in, positions, params, consts, lora, gains, rows, out):
    with ExitStack() as ctx:
        def sb(name, shape, dt=F32, on=ctx):
            return on.enter_context(nc.sbuf_tensor(name, shape, dt))

        def sem(name):
            return ctx.enter_context(nc.semaphore(name))

        x = sb("x", [P, TT, D])
        hT_hi = sb("hT_hi", [P, KT, SEQ], F32R)
        hT_lo = sb("hT_lo", [P, KT, SEQ], F32R)
        raw = sb("raw", [P, RAW_SLOTS, 4 * CH])
        v_first = sb("v_first", [P, 4, SEQ])
        gain = sb("gain", [P, D])
        con = sb("con", [P, N_CON])
        par = sb("par", [P, DEPTH, N_PAR])
        lor = sb("lor", [P, N_LOR])
        row = sb("row", [P, 128 + 9 * ROPE])
        derived = sb("derived", [P, DEPTH, 12])
        rkb = sb("rkb", [P, 4, P])
        cs = sb("cs", [P, 2, TT, 32])
        small = sb("small", [P, 256])

        with ExitStack() as on:
            w_hi = sb("w_hi", [P, HALF_RING, 2 * CH], F32R, on)
            w_lo = sb("w_lo", [P, HALF_RING, 2 * CH], F32R, on)
            act_hi = sb("act_hi", [P, 4 * PAIRS[0], SEQ], F32R, on)
            act_lo = sb("act_lo", [P, 4 * PAIRS[0], SEQ], F32R, on)
            silu = sb("silu", [P, TT, CH], F32, on)
            act_row = sb("act_row", [P, TT, CH], F32, on)
        ARENA = 22528
        arena = sb("arena", [P, ARENA])

        def at(off, *shape):
            n = int(np.prod(shape))
            assert off + n <= ARENA
            v = arena[:, off:off + n]
            if len(shape) == 2:
                return v.rearrange("p (a b) -> p a b", b=shape[1])
            if len(shape) == 3:
                return v.rearrange("p (a b c) -> p a b c", b=shape[1], c=shape[2])
            return v

        RING_END = 8192
        xg_first = at(RING_END, TT, D)
        rstd = small[:, 220:222]
        p_rw = at(RING_END, TT, RW_IN)
        p_mla = at(RING_END + 3584, TT, 832)
        p_hg = at(RING_END + 5248, TT, 2048)
        HG_AT = RING_END + 5248 + 4096

        ring_gain = gain[:, :].rearrange("p (n h t) -> p n h t", n=2, h=4)
        hg_q = at(HG_AT, 4, SEQ)
        hg_sig = at(HG_AT + 1024, 4, SEQ)
        hg_b = hg_sig
        hg_k = at(HG_AT + 2048, 4, SEQ)
        hg_e = [ring_gain[:, 0], ring_gain[:, 1], at(HG_AT + 3072, 4, SEQ), at(RING_END + 5248 + 2048, 4, SEQ)]
        hg_kend, hg_qbeg, hg_logf = hg_e[0], hg_e[1], hg_e[2]
        hg_diag = at(RING_END + 5248, 8, P)
        hg_gate = p_hg[:, :, 1536:2048]
        hg_k128 = at(HG_AT + 4096, 4, P)
        hg_cross = hg_k128
        hg_q128 = rkb
        hg_o = hg_q.rearrange("p h t -> p (h t)").rearrange("p (t n) -> p t n", t=TT)
        hg_sq = hg_k

        qrow = at(0, TT, MLA_H * QK)
        kvrow = at(3072, TT, MLA_H * 2 * NOPE)
        MB = RING_END + 5248
        qaT = at(MB + 5632, 4, SEQ)
        kvaT = at(MB, 2, SEQ)
        mla_sq = at(MB + 512, 3072)
        scores = at(MB + 512, MLA_H, 384)
        qnT = at(MB + 3584, MLA_H, SEQ)
        knT = at(MB + 5632, MLA_H, SEQ)
        k_sq = at(MB + 5632, 2, TT * 4, NOPE)
        ro = at(MB + 7680, TT, 640)
        probsT = at(0, MLA_H, 384)
        rT = at(7168, 4, SEQ)
        rkT = kvaT[:, 0, :]
        rb = gain[:, 0:1280].rearrange("p (t n) -> p t n", t=TT)
        rtmp = gain[:, 1280:1280 + 576].rearrange("p (t h n) -> p t h n", t=TT, h=9)

        pT = at(0, RW_F, SEQ + 1)
        pm = at(3600, RW_F, SEQ)
        rw_r, rw_k, rw_v = pm[:, 0:4, :], pm[:, 4:8, :], pm[:, 8:12, :]
        rw_sig = at(7184, 256)
        RB = 11776
        rw_w = at(RB, 4, SEQ)
        rw_tmp = at(RB + 1024, 4, SEQ)
        rw_a = at(RB + 2048, 4, SEQ)
        rw_g = at(RB + 3072, 4, SEQ)
        rw_kk = at(RB + 4096, 4, SEQ)
        rw_kk_sq = rw_g
        rw_b = at(RB + 5120, 4, SEQ)
        rw_e = [at(RB + 6144, 4, SEQ), at(RB + 7168, 4, SEQ), at(RB + 8192, 4, SEQ)]
        rw_bonus = at(RB + 9216, 4, SEQ)
        rw_inv = rw_e[1].rearrange("p j t -> p (j t)").rearrange("p (n f) -> p n f", f=P)
        ar = at(RB, JC, 2, RC)
        diag_v = at(0, JC, P)
        diag_b = at(8192, JC, P)
        diag_k = at(RB + 5120, JC, P)
        diag_a = at(RB + 7168, JC, P)
        v_st = at(2048, JC, RC)
        k_st = at(3072, JC, RC)
        b_st = at(10240, JC, RC)
        mab = at(4096, JC, RC)
        mab_t = at(5120, JC, RC)
        mak_t = at(6144, JC, RC)
        mrk_t = at(7168, JC, RC)
        mrb_t = at(RB + 4096, JC, RC)
        inv = at(0, JC, RC)
        inv_t = at(1024, JC, RC)
        g_t = mab_t
        diag_x, diag_g, diag_l = diag_b, diag_k, diag_a
        rhs = at(RB + 2048, 4, RC)
        sa = at(RB + 2048 + 256, 4, RC)
        state = [at(RB + 2048 + 512, 4, RC), at(RB + 2048 + 768, 4, RC)]
        yc = at(RB + 512, JC, RC)
        ysq = at(RB + 8192, JC, RC)
        rw_gate = at(RB + 7168, 4, SEQ)
        y_out = at(RB + 6144, 4, SEQ)
        EVEN, ODD = slice(0, 64), slice(64, 128)
        UPPER = [slice(0, 32), slice(64, 96)]
        LOWER = [slice(32, 64), slice(96, 128)]

        psum = ctx.enter_context(nc.psum_tensor("psum", [P, 8, CH], F32))

        def bank(b, n=1):
            return psum[:, b:b + n, :].rearrange("p a b -> p (a b)")

        def C(name):
            return con[:, CON[name][0]:CON[name][1]]

        ident = C("ident")
        idst = C("idst")
        hg_masks = C("hg_masks").rearrange("p (l t) -> p l t", t=P)
        lev_lo = C("lev_lo").rearrange("p (l t) -> p l t", t=RC)

        def par_of(l, name):
            return par[:, l, PAR[name][0]:PAR[name][1]]

        def lora_of(name):
            return lor[:, LOR[name][0]:LOR[name][1]]

        def over(v, n, m):
            return v.unsqueeze(1).broadcast_to([P, n, m])

        def along(v, m):
            return v.unsqueeze(2).broadcast_to([P, v.shape[1], m])

        raw_in = [sem(f"raw_in{s}") for s in range(RAW_SLOTS)]
        x_in_sem = [sem(f"x_loaded{c}") for c in range(4)]
        ident_in, con_in, par_in, row_in, lora_in, pos_in = (sem(n) for n in (
            "ident_loaded", "consts_loaded", "params_loaded", "rows_loaded", "lora_loaded", "positions_loaded"))
        gain_in = sem("gain_loaded")
        out_done = sem("out_stored")
        hi_done, lo_done = sem("w_hi_written"), sem("w_lo_written")
        half_used = sem("half_used")
        plain_used = sem("plain_slot_used")
        acc_free = [sem("acc_even_free"), sem("acc_odd_free")]
        names = {}

        def S(name):
            if name not in names:
                names[name] = sem(name)
            return names[name]

        block = ctx.enter_context(nc.Block())

        def xg_tile(n, c):
            return act_row[:, :, :] if n else xg_first[:, :, c * CH:(c + 1) * CH]

        def x_turn_bank(n, c):
            return 6 if n or c == 3 else 2 * c

        def chunk_ends(s4, j):
            return s4 * 8 + (2 * j + HALF_RING)

        @block.sync
        def _(sp):
            for c in range(4):
                cols = slice(c * CH, (c + 1) * CH)
                sp.dma_start(x[:, :, cols], x_in.rearrange("(t p) d -> p t d", p=P)[:, :, cols]).then_inc(x_in_sem[c], 16)
            for l in range(DEPTH):
                g0, s0 = l * SLOTS_PER_LAYER, l * SPLIT_PER_LAYER
                for j in range(FFN_AT):
                    if j < N_IN + 4:
                        if l or j >= 4:
                            sp.wait_ge(lo_done, 2 * (s0 + j - 3))
                    elif j < N_IN + N_PLAIN + 4:
                        sp.wait_ge(plain_used, N_PLAIN * l + j - N_IN - 3)
                    else:
                        sp.wait_ge(lo_done, 2 * (s0 + j - N_PLAIN - 3))
                    n = 4 * (IN_CHUNKS[j // 4][1] if j < N_IN else 384 if j < N_IN + 4
                             else 256 if j < N_IN + N_PLAIN else CH)
                    sp.dma_start(raw[:, j % 4, 0:n], stream[g0 + j, :, 0:n]).then_inc(raw_in[j % 4], 16)
                with sp.Fori(0, N_FFN // 4) as i:
                    for j in range(4):
                        sp.wait_ge(lo_done, i * 8 + 2 * (s0 + N_IN + N_O + j - 3))
                        sp.dma_start(raw[:, j, :],
                                     stream[bass.ds(i * 4 + (g0 + FFN_AT + j), 1), :, :].rearrange(
                                         "o p n -> (o p) n")).then_inc(raw_in[j], 16)
            for c in range(4):
                cols = slice(c * CH, (c + 1) * CH)
                sp.wait_ge(S("x_added"), 12 * DEPTH - 3 + c)
                sp.dma_start(out.rearrange("(t p) d -> p t d", p=P)[:, :, cols], x[:, :, cols]).then_inc(out_done, 16)
            sp.wait_ge(out_done, 64)

        @block.gpsimd
        def _(pool):
            pool.dma_start(con[:, 0:P], consts[:, 0:P]).then_inc(ident_in, 16)
            pool.dma_start(gain[:, :], gains[0:1, :].broadcast_to([P, D])).then_inc(gain_in, 16)
            pool.wait_ge(raw_in[RAW_SLOTS - 1], 16)
            pool.dma_start(con[:, P:N_CON], consts[:, P:N_CON]).then_inc(con_in, 16)
            pool.dma_start(par[:, :, :], params.rearrange("p (l n) -> p l n", l=DEPTH)).then_inc(par_in, 16)
            pool.dma_start(small[:, 200:202].bitcast(I32), positions).then_inc(pos_in, 16)
            for l in range(DEPTH):
                if l:
                    pool.wait_ge(S("hg_gate_ready"), l)
                    pool.wait_ge(S("rw_mix_lo"), l)
                    pool.wait_ge(S("xg_ready"), 8 * l)
                    pool.dma_start(gain[:, :], gains[2 * l:2 * l + 1, :].broadcast_to([P, D])).then_inc(gain_in, 16)
                pool.dma_start(row[:, :], rows[l:l + 1, :].broadcast_to([P, 128 + 9 * ROPE])).then_inc(row_in, 16)
                pool.dma_start(lor[:, :], lora[l, :, :]).then_inc(lora_in, 16)
                pool.wait_ge(S("mla_rope_done"), l + 1)
                pool.dma_start(gain[:, :], gains[2 * l + 1:2 * l + 2, :].broadcast_to([P, D])).then_inc(gain_in, 16)
                for tile, free in ((diag_b, (("rw_pT_ready", 2),)), (diag_v, (("rw_shifted", 2),)),
                                   (diag_k, (("rw_exp", 3), ("rw_r_done", 1))), (diag_a, (("rw_ab_done", 1),))):
                    for name, n in free:
                        pool.wait_ge(S(name), n * (l + 1))
                    nc.gpsimd.memset(tile[EVEN, :, 64:128], 0.0).then_inc(S("rw_zeroed"), 1)
                    nc.gpsimd.memset(tile[ODD, :, 0:64], 0.0).then_inc(S("rw_zeroed"), 1)
                pool.wait_ge(S("rw_m_ready"), 5 * l + 1)
                for k in range(len(RW_LEVELS)):
                    if k:
                        pool.wait_ge(S("rw_gt_mm"), 10 * l + 2 * k)
                    for hp in (EVEN, ODD):
                        nc.gpsimd.tensor_tensor(diag_l[hp, :, hp], mab[hp, :, :],
                                                lev_lo[hp, k, :].unsqueeze(1).broadcast_to([64, JC, RC]),
                                                ALU.mult).then_inc(S("rw_level_ready"), 1)

        @block.scalar
        def _(act):
            def chained(ins, s, value):
                ins.then_inc(s, 1)
                act.wait_ge(s, value)

            def split_hi(g4, s4, j, w=CH):
                act.wait_ge(raw_in[j % 4], g4 * 16 + 16 * (j // 4 + 1))
                for hf in range(2):
                    q = 2 * j + hf
                    act.wait_ge(half_used, s4 * 8 + (q + 1))
                    nc.scalar.activation(w_hi[:, q % HALF_RING, 0:2 * w], raw[:, j % 4, hf * 2 * w:(hf + 1) * 2 * w],
                                         ACT.Copy).then_inc(hi_done, 1)

            def tables():
                for k in range(2):
                    act.wait_ge(S("angle_ready"), k + 1)
                    nc.scalar.activation(cs[:, k, :, :], small[:, 64 * k + 8:64 * k + 72].rearrange(
                        "p (t n) -> p t n", t=TT), ACT.Sin).then_inc(S("cs_ready"), 1)
                act.wait_ge(S("lb_shifted"), 1)
                nc.scalar.activation(small[:, 144:152], small[:, 144:152], ACT.Exp).then_inc(S("lb_exp"), 1)

            def x_hi(n, c):
                act.wait_ge(S("x_turned"), 4 * n + c + 1)
                nc.scalar.activation(hT_hi[:, 4 * c:4 * c + 4, :], bank(x_turn_bank(n, c), 2).rearrange(
                    "p (k t) -> p k t", k=4), ACT.Copy).then_inc(S("hT_hi_ready"), 1)

            def x_squares(n, c):
                if n:
                    act.wait_ge(S("x_added"), 12 * ((n - 1) // 2) + (4 if n % 2 else 12) - 3 + c)
                    if n > 1:
                        act.wait_ge(S("act_row_ready"), sum(PAIRS) * (n // 2))
                    act.wait_ge(S("x_squares"), 8 * n + 2 * c)
                for t in range(TT):
                    if n == 0:
                        act.wait_ge(x_in_sem[c], 16)
                        if c:
                            act.wait_ge(S("x_squares"), 2 * c + t - 1)
                    nc.scalar.activation(silu[:, t, :], x[:, t, c * CH:(c + 1) * CH], ACT.Square,
                                         accum_out=small[:, 208 + 4 * t + c:209 + 4 * t + c]).then_inc(
                                             S("x_squares"), 1)

            def x_std(n):
                act.wait_ge(S("x_var"), n + 1)
                nc.scalar.activation(small[:, 218:220], small[:, 216:218], ACT.Sqrt).then_inc(S("x_std"), 1)

            def norm_tail(n, j):
                if j == 3:
                    x_hi(n, 3)
                    for c in range(0 if n == 0 else 3, 4):
                        x_squares(n, c)
                if j == 5:
                    x_std(n)

            for l in range(DEPTH):
                ev = l + 1
                g4, s4 = l * SLOTS_PER_LAYER // 4, l * SPLIT_PER_LAYER // 4
                if l == 0:
                    for c in range(3):
                        x_hi(0, c)
                for j in range(N_IN):
                    if l == 0 and j == 8:
                        tables()
                    split_hi(g4, s4, j, IN_CHUNKS[j // 4][1])
                    norm_tail(2 * l, j)

                    if j == HG_GATES:
                        act.wait_ge(S("hg_turned"), 2 * l + 1)
                        nc.scalar.activation(hg_q.rearrange("p h t -> p (h t)"), bank(4, 2), ACT.Silu).then_inc(
                            S("hg_gates_ready"), 1)
                        act.wait_ge(S("hg_turned"), 2 * l + 2)
                        nc.scalar.activation(hg_sig.rearrange("p h t -> p (h t)"), bank(6, 2), ACT.Sigmoid).then_inc(
                            S("hg_gates_ready"), 1)
                        nc.scalar.activation(hg_k.rearrange("p h t -> p (h t)"), bank(6, 2), ACT.Sigmoid,
                                             scale=-1.0).then_inc(S("hg_gates_ready"), 1)
                    if j == HG_LOGF:
                        act.wait_ge(S("hg_sig_floor"), ev)
                        act.wait_ge(S("derived_ready"), 1)
                        for h in range(HG_H):
                            nc.scalar.activation(hg_logf[:, h, :], hg_sig[:, h, :], ACT.Ln, bias=derived[:, l, h:h + 1],
                                                 scale=derived[:, l, 4 + h:5 + h]).then_inc(S("hg_logf"), 1)
                    for k in range(1, 8):
                        if j != HG_LEVEL_SLOT[k] - 1:
                            continue
                        if k == 1:
                            act.wait_ge(S("hg_exponent"), 8 * l + 1)
                            nc.scalar.activation(hg_kend, hg_kend, ACT.Exp).then_inc(S("hg_exp"), 1)
                            nc.scalar.activation(small[:, 160:176].rearrange("p (h c) -> p h c", h=4),
                                                 hg_b.rearrange("p h (c i) -> p h c i", i=64)[:, :, :, 63], ACT.Exp)
                        act.wait_ge(S("hg_exponent"), 8 * l + k + 1)
                        nc.scalar.activation(hg_e[k % 4], hg_b if k == 1 else hg_e[k % 4], ACT.Exp).then_inc(
                            S("hg_exp"), 1)
                    if j == HG_CROSS_OUT:
                        act.wait_ge(S("hg_cross_mm"), ev)
                        nc.scalar.activation(hg_cross.rearrange("p h t -> p (h t)"), bank(4), ACT.Copy).then_inc(
                            S("hg_cross_ready"), 1)
                    if j == HG_SILU:
                        act.wait_ge(S("p_ready"), len(IN_CHUNKS) * l + 4)
                        nc.scalar.activation(hg_gate, hg_gate, ACT.Silu).then_inc(S("hg_gate_silu"), 1)
                    if j == HG_SQUARES:
                        act.wait_ge(S("hg_o_mm"), ev)
                        nc.scalar.activation(hg_sq.rearrange("p h t -> p (h t)"), bank(4, 2), ACT.Square).then_inc(
                            S("hg_squares"), 1)
                    if j == HG_STD:
                        act.wait_ge(S("hg_var"), ev)
                        nc.scalar.activation(small[:, 192:200], small[:, 184:192], ACT.Sqrt).then_inc(S("hg_std"), 1)

                    if j == MLA_SQUARES:
                        act.wait_ge(S("p_ready"), len(IN_CHUNKS) * l + 6)
                        act.wait_ge(S("hg_level_mm"), 8 * l + 5)
                        for k, (a, b) in enumerate(((0, 512), (512, 768), (768, 832))):
                            for t in range(TT):
                                nc.scalar.activation(hg_e[0].rearrange("p h t -> p (h t)")[:, 0:b - a], p_mla[:, t, a:b],
                                                     ACT.Square, accum_out=small[:, 8 + 2 * k + t:9 + 2 * k + t]).then_inc(
                                                         S("mla_in_squares"), 1)
                                act.wait_ge(S("mla_in_squares"), 6 * l + 2 * k + t + 1)
                    if j == MLA_STD:
                        act.wait_ge(S("mla_in_var"), ev)
                        nc.scalar.activation(small[:, 24:30], small[:, 16:22], ACT.Sqrt).then_inc(S("mla_in_std"), 1)
                    if j in (MLA_Q_OUT, MLA_KV_OUT):
                        act.wait_ge(S("mla_in_turned"), 2 * l + (1 if j == MLA_Q_OUT else 2))
                        for k in range(4) if j == MLA_Q_OUT else range(4, 6):
                            dst = qaT[:, k, :] if k < 4 else kvaT[:, k - 4, :]
                            g = par_of(l, "q_a")[:, k:k + 1] if k < 4 else par_of(l, "kv_a")[:, k - 4:k - 3]
                            src = bank(6, 2)[:, k * SEQ:(k + 1) * SEQ] if k < 4 else bank(4)[:, (k - 4) * SEQ:(k - 3) * SEQ]
                            nc.scalar.activation(dst, src, ACT.Copy, scale=g).then_inc(S("mla_inT_ready"), 1)
                act.wait_ge(S("hg_o_turned"), ev)
                nc.scalar.activation(hT_hi[:, 0:4, :], bank(6, 2).rearrange("p (h t) -> p h t", h=4),
                                     ACT.Copy).then_inc(S("hg_mix_hi"), 1)

                sq4 = mla_sq.rearrange("p (t n) -> p t n", t=TT)

                def k_std(hf):
                    act.wait_ge(S("mla_var"), 3 * l + hf + 2)
                    nc.scalar.activation(small[:, 112 + 8 * hf:120 + 8 * hf], small[:, 64 + 8 * hf:72 + 8 * hf],
                                         ACT.Sqrt).then_inc(S("mla_std"), 1)

                def k_out(hf):
                    act.wait_ge(S("mla_k_turned"), 2 * l + hf + 1)
                    nc.scalar.activation(knT[:, 4 * hf:4 * hf + 4, :].rearrange("p h t -> p (h t)"), bank(4 + 2 * hf, 2),
                                         ACT.Copy, scale=par_of(l, "gk")).then_inc(S("mla_kT_ready"), 1)

                for c in range(8):
                    act.wait_ge(S("mla_up_mm"), 8 * l + c + 1)
                    b0 = (4 + 2 * c) % 8
                    w = 384 if c < 4 else CH
                    if c < 4:
                        nc.scalar.activation(sq4[:, :, c * 384:(c + 1) * 384], psum[:, b0:b0 + 2, 0:w], ACT.Square).then_inc(
                            S("mla_q_squares"), 1)
                    else:
                        k_out4 = k_sq[:, (c - 4) // 2, :, :].rearrange("p (t h) n -> p t h n", t=TT)
                        nc.scalar.activation(k_out4[:, :, 2 * (c % 2):2 * (c % 2) + 2, :],
                                             psum[:, b0:b0 + 2, :].rearrange("p t (h n) -> p t h n", n=256)[:, :, :, 0:NOPE],
                                             ACT.Square).then_inc(S("mla_k_squares"), 1)
                    dst = qrow[:, :, c * 384:(c + 1) * 384] if c < 4 else kvrow[:, :, (c - 4) * CH:(c - 3) * CH]
                    nc.scalar.activation(dst, psum[:, b0:b0 + 2, 0:w], ACT.Copy).then_inc(S("mla_up_ready"), 1)
                    if c == 5:
                        act.wait_ge(S("mla_var"), 3 * l + 1)
                        nc.scalar.activation(small[:, 80:112], small[:, 32:64], ACT.Sqrt).then_inc(S("mla_std"), 1)
                    if c == 6:
                        k_std(0)
                act.wait_ge(S("mla_q_turned"), ev)
                nc.scalar.activation(qnT.rearrange("p h t -> p (h t)"), bank(0, 4), ACT.Copy,
                                     scale=par_of(l, "gq")).then_inc(S("mla_qT_ready"), 1)
                k_out(0)
                k_std(1)
                act.wait_ge(S("mla_r_turned"), ev)
                nc.scalar.activation(rT.rearrange("p h t -> p (h t)"), bank(0, 2), ACT.Copy).then_inc(S("mla_rT_ready"), 1)
                nc.scalar.activation(rkT, bank(2)[:, 0:SEQ], ACT.Copy).then_inc(S("mla_rT_ready"), 1)
                k_out(1)
                for j in range(4):
                    nc.scalar.activation(rkb[:, j, :], C("ones2"), ACT.Copy, scale=par_of(l, "r_k")[:, j:j + 1]).then_inc(
                        S("rkb_ready"), 1)
                for hf in range(2):
                    act.wait_ge(S("mla_max"), 2 * l + hf + 1)
                    for h in range(4 * hf, 4 * hf + 4):
                        for qt, cols in ((0, slice(0, 128)), (1, slice(128, 384))):
                            n = 8 * qt + h
                            nc.scalar.activation(scores[:, h, cols], scores[:, h, cols], ACT.Exp,
                                                 bias=small[:, 32 + n:33 + n],
                                                 accum_out=small[:, 48 + n:49 + n]).then_inc(S("mla_exp"), 1)
                for hf in range(2):
                    act.wait_ge(S("mla_p_turned"), 8 * l + 4 * hf + 4)
                    nc.scalar.activation(probsT[:, 4 * hf:4 * hf + 4, :], psum[:, 4 * hf:4 * hf + 4, 0:384],
                                         ACT.Copy).then_inc(S("mla_pT_ready"), 1)
                for hf in range(2):
                    act.wait_ge(S("mla_o_mm"), 2 * l + hf + 1)
                    nc.scalar.activation(hT_hi[:, 4 + 4 * hf:8 + 4 * hf, :], bank(2 * hf, 2).rearrange(
                        "p (h t) -> p h t", h=4), ACT.Copy).then_inc(S("mla_mix_hi"), 1)

                act.wait_ge(S("mla_mix_lo"), ev)
                act.wait_ge(S("rw_turned"), 2 * l + 1)
                nc.scalar.activation(pT[:, 8:14, 1:SEQ + 1], bank(4, 3).rearrange("p (f t) -> p f t", f=6),
                                     ACT.Copy).then_inc(S("rw_pT_ready"), 1)
                act.wait_ge(S("rw_turned"), 2 * l + 2)
                nc.scalar.activation(pT[:, 0:8, 1:SEQ + 1], bank(0, 4).rearrange("p (f t) -> p f t", f=8),
                                     ACT.Copy).then_inc(S("rw_pT_ready"), 1)
                act.wait_ge(S("rw_shifted"), 2 * l + 1)
                nc.scalar.activation(rw_sig[0:64, :], pm[0:64, 12, :], ACT.Tanh).then_inc(S("rw_lora_in"), 1)
                nc.scalar.activation(rw_tmp[:, 0, :], pm[:, 13, :], ACT.Sigmoid).then_inc(S("rw_lora_in"), 1)
                act.wait_ge(S("rw_lora_mm"), 3 * l + 1)
                for j in range(4):
                    nc.scalar.activation(rw_w[:, j, :], bank(4, 2)[:, j * SEQ:(j + 1) * SEQ], ACT.Sigmoid,
                                         bias=par_of(l, "w0")[:, j:j + 1]).then_inc(S("rw_w_ready"), 1)
                act.wait_ge(S("rw_lora_mm"), 3 * l + 2)
                for j in range(4):
                    nc.scalar.activation(rw_a[:, j, :], bank(6, 2)[:, j * SEQ:(j + 1) * SEQ], ACT.Sigmoid,
                                         bias=par_of(l, "a0")[:, j:j + 1]).then_inc(S("rw_a_ready"), 1)
                act.wait_ge(S("rw_kk_mm"), 2 * l + 1)
                nc.scalar.activation(small[:, 128:144], bank(2)[:, 0:16], ACT.Sqrt).then_inc(S("rw_kk_norm"), 1)
                act.wait_ge(S("rw_lora_mm"), 3 * l + 3)
                nc.scalar.activation(rw_g.rearrange("p j t -> p (j t)"), bank(0, 2), ACT.Copy).then_inc(S("rw_g_ready"), 1)
                if l:
                    act.wait_ge(S("rw_v1_mm"), l)
                    nc.scalar.activation(rw_bonus[0:32, 0, :], bank(6)[0:32, 0:SEQ], ACT.Copy).then_inc(S("rw_v1_ready"), 1)
                    act.wait_ge(S("rw_v2_mm"), l)
                    for j in range(4):
                        nc.scalar.activation(rw_e[0][:, j, :], bank(6, 2)[:, j * SEQ:(j + 1) * SEQ], ACT.Sigmoid,
                                             bias=par_of(l, "v0")[:, j:j + 1]).then_inc(S("rw_vmix_ready"), 1)
                v3, b3 = (z.rearrange("p j (c i) -> p (j c) i", i=RC) for z in (rw_v, rw_a))
                act.wait_ge(S("rw_v_ready"), ev)
                for hp in (EVEN, ODD):
                    nc.scalar.activation(diag_v[hp, :, hp], v3[hp, :, :], ACT.Copy).then_inc(S("rw_diag_act"), 1)

                def stacked(k, dst, b0):
                    act.wait_ge(S("rw_stack_mm"), 3 * l + k + 1)
                    turned = bank(b0, 4).rearrange("p (n f) -> p n f", f=P)
                    for hp in (EVEN, ODD):
                        nc.scalar.activation(dst[hp, :, :], turned[hp, :, hp], ACT.Copy).then_inc(S("rw_stacked"), 1)

                if l == 0:
                    nc.scalar.activation(v_first[:, :, :], rw_v, ACT.Copy)
                act.wait_ge(S("rw_exponent"), 3 * l + 1)
                act.wait_ge(S("rw_kk_mm"), 2 * ev)
                nc.scalar.activation(rw_e[0], rw_b, ACT.Exp, scale=-C0).then_inc(S("rw_exp"), 1)
                nc.scalar.activation(rw_e[1], rw_b, ACT.Exp, scale=C0).then_inc(S("rw_exp"), 1)
                act.wait_ge(S("rw_exponent"), 3 * l + 2)
                nc.scalar.activation(small[:, 48:64], small[:, 32:48], ACT.Exp, scale=-C0).then_inc(S("rw_half_decay"), 1)
                stacked(0, v_st, 4)
                act.wait_ge(S("rw_exponent"), 3 * l + 3)
                nc.scalar.activation(rw_e[2], rw_e[2], ACT.Exp, scale=-C0).then_inc(S("rw_exp"), 1)
                act.wait_ge(S("rw_b_done"), ev)
                nc.scalar.activation(diag_b[EVEN, :, EVEN], b3[EVEN, :, :], ACT.Copy).then_inc(S("rw_diag_act"), 1)
                act.wait_ge(S("rw_ab_done"), ev)
                nc.scalar.activation(diag_a[EVEN, :, EVEN], ar[EVEN, :, 0, :], ACT.Copy).then_inc(S("rw_diag_act"), 1)
                stacked(1, b_st, 4)
                stacked(2, k_st, 0)

                def spread_x(n):
                    act.wait_ge(S("rw_x"), 10 * l + n + 1)
                    h8 = slice(8 * (n % 2), 8 * (n % 2) + 8)
                    nc.scalar.activation(diag_x[EVEN, h8, EVEN], inv[EVEN, h8, :], ACT.Copy).then_inc(S("rw_diag_x_act"), 1)

                spread_x(0)
                spread_x(1)
                for k in range(len(RW_LEVELS)):
                    last = k == len(RW_LEVELS) - 1
                    for hf in range(2):
                        h8 = slice(8 * hf, 8 * hf + 8)
                        act.wait_ge(S("rw_gt_mm"), 10 * l + 2 * k + hf + 1)
                        if last:
                            g3 = bank(hf).rearrange("p (n t) -> p n t", n=8)
                            nc.scalar.activation(g_t[UPPER[0], h8, 32:64], g3[UPPER[0], :, 32:64], ACT.Copy)
                            nc.scalar.activation(g_t[UPPER[1], h8, 32:64], g3[UPPER[1], :, 32:64], ACT.Copy).then_inc(
                                S("rw_gt_ready"), 1)
                        else:
                            nc.scalar.activation(g_t[:, h8, :].rearrange("p a b -> p (a b)"), bank(hf),
                                                 ACT.Copy).then_inc(S("rw_gt_ready"), 1)
                            nc.scalar.activation(diag_g[EVEN, h8, EVEN], bank(hf)[EVEN, :].rearrange(
                                "p (n t) -> p n t", n=8), ACT.Copy).then_inc(S("rw_diag_g_act"), 1)
                    if k < len(RW_LEVELS) - 2:
                        spread_x(2 * k + 2)
                        spread_x(2 * k + 3)
                nc.scalar.activation(rw_gate, rw_g, ACT.Copy).then_inc(S("rw_g_ready"), 1)
                for c in range(NC):
                    act.wait_ge(S("rw_sa_mm"), NC * l + c + 1)
                    nc.scalar.activation(sa.rearrange("p a b -> p (a b)"), bank(1)[:, 0:256], ACT.Copy).then_inc(
                        S("rw_sa_ready"), 1)
                s4o, g4o = s4 + N_IN // 4, g4 + (N_IN + N_PLAIN) // 4
                act.wait_ge(S("rw_y_mm"), ev)
                for j in range(N_O):
                    split_hi(g4o, s4o, j)
                    if j == 0:
                        act.wait_ge(S("rw_y_centred"), ev)
                        nc.scalar.activation(ysq, yc, ACT.Square).then_inc(S("rw_y_squares"), 1)
                    if j == 1:
                        act.wait_ge(S("rw_y_var"), ev)
                        nc.scalar.activation(small[:, 112:128], small[:, 96:112], ACT.Sqrt).then_inc(S("rw_y_std"), 1)
                    if j == 3:
                        act.wait_ge(S("rw_out"), ev)
                        nc.scalar.activation(hT_hi[:, 12:16, :], y_out, ACT.Copy).then_inc(S("rw_mix_hi"), 1)
                        act.wait_ge(S("rw_mix_lo"), ev)
                    if 3 <= j < 7:
                        k4 = slice(4 * (j - 3), 4 * (j - 2))
                        nc.scalar.activation(act_hi[:, k4, :], hT_hi[:, k4, :].bitcast(F32), ACT.Copy).then_inc(
                            S("mix_hi_kept"), 1)
                    if j > 4 and j % 4 == 3:
                        x_hi(2 * l + 1, j // 4 - 1)
                        x_squares(2 * l + 1, j // 4 - 1)

                g4f, s4f = g4o + N_O // 4, s4o + N_O // 4
                pair0 = sum(PAIRS) * l
                norm_of_ffn = 2 * l + 1
                for part, pairs in enumerate(PAIRS):
                    fresh = part == 0
                    makes_norm = part == len(PAIRS) - 1 and l < DEPTH - 1

                    def pair(i, first):
                        gi, si = i * 2 + g4f, i * 2 + s4f
                        for j in range(8):
                            if j == 6:
                                act.wait_ge(half_used, chunk_ends(si, 4))
                                if not (first and pair0 == 0):
                                    act.wait_ge(S("act_row_ready"), i + pair0)
                                act.wait_ge(S("rstd_ready"), norm_of_ffn + 1)
                                nc.scalar.activation(silu[:, 0, :], psum[:, 0, :], ACT.Silu, scale=rstd[:, 0:1])
                                nc.scalar.activation(silu[:, 1, :], psum[:, 1, :], ACT.Silu, scale=rstd[:, 1:2]).then_inc(
                                    acc_free[0], 1)
                                if not first:
                                    turned_hi(i - 1, pair0)
                            split_hi(gi, si, j)
                            if first and fresh:
                                norm_tail(norm_of_ffn, j)

                    def turned_hi(i, p0):
                        act.wait_ge(S("act_turned"), i + (p0 + 1))
                        dst = act_hi[:, bass.ds(i * 4, 4), :] if not isinstance(i, int) else act_hi[:, 4 * i:4 * i + 4, :]
                        nc.scalar.activation(dst, bank(4, 2).rearrange("p (k t) -> p k t", k=4),
                                             ACT.Copy).then_inc(S("act_hi_ready"), 1)

                    pair(0, True)
                    with act.Fori(1, pairs) as i:
                        pair(i, False)
                    g4f, s4f = g4f + 2 * pairs, s4f + 2 * pairs
                    for j in range(4 * pairs):
                        split_hi(g4f, s4f, j)
                        if j == 3:
                            turned_hi(pairs - 1, pair0)
                        if makes_norm and j > pairs and j % pairs == 3:
                            x_hi(2 * l + 2, j // pairs - 1)
                            x_squares(2 * l + 2, j // pairs - 1)
                    g4f, s4f = g4f + pairs, s4f + pairs
                    pair0 += pairs

        @block.vector
        def _(dve):
            steps = [0]
            chain = sem("dve_steps")

            def v(ins):
                steps[0] += 1
                ins.then_inc(chain, 1)
                dve.wait_ge(chain, steps[0])

            def u(ins):
                steps[0] += 1
                ins.then_inc(chain, 1)

            def settle():
                dve.wait_ge(chain, steps[0])

            def vs(ins, name, value):
                ins.then_inc(S(name), 1)
                dve.wait_ge(S(name), value)

            tt, ts, stt = nc.vector.tensor_tensor, nc.vector.tensor_scalar, nc.vector.scalar_tensor_tensor
            red, rec, cp = nc.vector.tensor_reduce, nc.vector.reciprocal, nc.vector.tensor_copy
            ADD, SUB, MUL, MAX = ALU.add, ALU.subtract, ALU.mult, ALU.max

            def split_lo(s4, j, w=CH):
                for hf in range(2):
                    q = 2 * j + hf
                    dve.wait_ge(hi_done, s4 * 8 + (q + 1))
                    tt(w_lo[:, q % HALF_RING, 0:2 * w], raw[:, j % 4, hf * 2 * w:(hf + 1) * 2 * w],
                       w_hi[:, q % HALF_RING, 0:2 * w].bitcast(F32), SUB).then_inc(lo_done, 1)

            def x_gain(n, c):
                if n == 0:
                    dve.wait_ge(x_in_sem[c], 16)
                elif c == 0:
                    if n > 1:
                        dve.wait_ge(S("act_turned"), sum(PAIRS) * (n // 2))
                else:
                    dve.wait_ge(S("x_turned"), 4 * n + c)
                dve.wait_ge(gain_in, 16 * (n + 1))
                vs(tt(xg_tile(n, c), x[:, :, c * CH:(c + 1) * CH], over(gain[:, c * CH:(c + 1) * CH], TT, CH), MUL),
                   "xg_ready", 4 * n + c + 1)

            def x_lo(n, c):
                dve.wait_ge(S("hT_hi_ready"), 4 * n + c + 1)
                tt(hT_lo[:, 4 * c:4 * c + 4, :], bank(x_turn_bank(n, c), 2).rearrange("p (k t) -> p k t", k=4),
                   hT_hi[:, 4 * c:4 * c + 4, :].bitcast(F32), SUB).then_inc(S("hT_ready"), 1)

            def norm_tail(n, j):
                if j == 3:
                    x_lo(n, 3)
                if j == 4:
                    dve.wait_ge(S("x_squares"), 8 * (n + 1))
                    v(red(small[:, 222:224], small[:, 208:216].rearrange("p (t c) -> p t c", t=TT), AX.X, ADD))
                    vs(ts(small[:, 216:218], small[:, 222:224], 1.0 / D, EPS, MUL, ADD), "x_var", n + 1)
                if j == 5:
                    dve.wait_ge(S("x_std"), n + 1)
                    vs(rec(rstd, small[:, 218:220]), "rstd_ready", n + 1)

            def add_x(s, j, c, n_added):
                b0 = 2 * (c % 2)
                dve.wait_ge(half_used, chunk_ends(s, j))
                xs = x[:, :, c * CH:(c + 1) * CH]
                vs(tt(xs, xs, psum[:, b0:b0 + 2, :], ADD), "x_added", n_added)
                dve.sem_inc(acc_free[b0 // 2], 1)

            def tables():
                dve.wait_ge(pos_in, 16)
                dve.wait_ge(con_in, 16)
                v(cp(small[:, 202:204], small[:, 200:202].bitcast(I32)))
                ang = small[:, 72:136].rearrange("p (t n) -> p t n", t=TT)
                co = small[:, 8:72]
                turns = arena[:, HG_AT:HG_AT + 64]
                for t in range(TT):
                    v(ts(ang[:, t, :], C("inv_freq"), small[:, 202 + t:203 + t], None, MUL))
                ang = small[:, 72:136]
                v(ts(turns, ang, 1.0 / (2 * np.pi), MAGIC, MUL, ADD))
                v(ts(turns, turns, MAGIC, None, SUB))
                for part in (6.28125, 0.0019340515136718750, 1.2556659146e-06):
                    v(stt(ang, turns, -part, ang, MUL, ADD))
                v(ts(ang, ang, 3.1415925, -3.1415925, ALU.min, MAX))
                v(stt(co, ang, -1.0, ang, MUL, MAX))
                vs(ts(co, co, -1.0, float(np.pi / 2), MUL, ADD), "angle_ready", 1)
                dve.sem_inc(S("angle_ready"), 1)
                dve.wait_ge(par_in, 16)
                lb0, lb1 = par_of(0, "hg_lb"), par_of(1, "hg_lb")
                v(tt(small[:, 136:140], lb0, lb1, MAX))
                v(tt(small[:, 144:148], lb0, small[:, 136:140], SUB))
                vs(tt(small[:, 148:152], lb1, small[:, 136:140], SUB), "lb_shifted", 1)
                dve.wait_ge(S("lb_exp"), 1)
                v(tt(small[:, 136:140], small[:, 144:148], small[:, 148:152], ADD))
                v(rec(small[:, 140:144], small[:, 136:140]))
                v(tt(small[:, 144:148], small[:, 144:148], small[:, 140:144], MUL))
                v(tt(small[:, 148:152], small[:, 148:152], small[:, 140:144], MUL))
                v(tt(derived[:, 0, 0:4], small[:, 144:148], small[:, 144:148], SUB))
                v(tt(derived[:, 1, 0:4], small[:, 144:148], small[:, 148:152], ADD))
                v(tt(derived[:, 1, 0:4], derived[:, 1, 0:4], small[:, 144:148], SUB))
                for l in range(DEPTH):
                    v(ts(derived[:, l, 4:8], derived[:, l, 0:4], -1.0, 1.0, MUL, ADD))
                    v(ts(derived[:, l, 8:12], par_of(l, "k_a"), -1.0, 1.0, MUL, ADD))
                dve.sem_inc(S("derived_ready"), 1)

            for l in range(DEPTH):
                ev = l + 1
                s4 = l * SPLIT_PER_LAYER // 4

                def store_p(c):
                    w = IN_CHUNKS[c][1]
                    dst = (p_hg[:, :, c * CH:(c + 1) * CH] if c < 4 else p_mla[:, :, 0:512] if c == 4
                           else p_mla[:, :, 512:832] if c == 5
                           else p_rw[:, :, (c - 6) * CH:(c - 6) * CH + w])
                    dve.wait_ge(half_used, chunk_ends(s4, 4 * c + 4))
                    for t in range(TT):
                        u(ts(dst[:, t, :], psum[:, 2 * (c % 2) + t, 0:w], rstd[:, t:t + 1], None, MUL))
                    settle()
                    dve.sem_inc(acc_free[c % 2], 1)
                    dve.sem_inc(S("p_ready"), 1)

                def acc_base(layer):
                    return layer * (len(IN_CHUNKS) // 2 + 2 + sum(PAIRS) + 4)

                def exponent(k):
                    m = HG_LEVELS[k]
                    if k >= 4:
                        dve.wait_ge(S("hg_level_mm"), 8 * l + max(2, k - 3))
                    e = hg_e[k % 4].rearrange("p h (n two m) -> p (h n) two m", two=2, m=m)
                    b = hg_b.rearrange("p h (n two m) -> p (h n) two m", two=2, m=m)
                    n = 1024 // (2 * m)
                    r = b[:, :, 0, m - 1:m].broadcast_to([P, n, m])
                    v(tt(e[:, :, 0, :], r, b[:, :, 0, :], SUB))
                    vs(tt(e[:, :, 1, :], b[:, :, 1, :], r, SUB), "hg_exponent", 8 * l + k + 1)

                def factors(k):
                    m = HG_LEVELS[k]
                    dve.wait_ge(S("hg_exp"), 8 * l + k + 1)
                    if k < 2:
                        dst, src = ((hg_kend, hg_k), (hg_qbeg, hg_q))[k]
                        v(tt(dst, dst, src, MUL))
                        if k == 1:
                            dve.sem_inc(S("hg_factors"), 1)
                        return
                    e, kk, qq = (z.rearrange("p h (n two m) -> p (h n) two m", two=2, m=m)
                                 for z in (hg_e[k % 4], hg_k, hg_q))
                    v(tt(e[:, :, 0, :], e[:, :, 0, :], kk[:, :, 0, :], MUL))
                    vs(tt(e[:, :, 1, :], e[:, :, 1, :], qq[:, :, 1, :], MUL), "hg_factors", 7 * l + k)

                def masked(k):
                    dve.wait_ge(S("hg_level_mm"), 8 * l + k + 1)
                    vs(nc.vector.copy_predicated(hg_diag[:, :, :], over(hg_masks[:, k, :], 8, P).bitcast(U32),
                                                 bank(4 + 2 * (k % 2), 2).rearrange("p (n t) -> p n t", n=8)),
                       "hg_masked", 8 * l + k + 1)

                flat = "p h t -> p (h t)"
                if l == 0:
                    for c in range(3):
                        x_gain(0, c)
                    for c in range(3):
                        x_lo(0, c)
                for j in range(N_IN):
                    if j == 2:
                        if l:
                            add_x(s4, 0, 3, 12 * l)
                        x_gain(2 * l, 3)
                    elif j % 4 == 2:
                        store_p(j // 4 - 1)
                    if l == 0 and j == 8:
                        tables()
                    split_lo(s4, j, IN_CHUNKS[j // 4][1])
                    norm_tail(2 * l, j)

                    if j == HG_GATES:
                        dve.wait_ge(S("hg_turned"), 2 * ev)
                        v(nc.vector.memset(hg_diag[:, :, :], 0.0))
                        dve.wait_ge(S("hg_gates_ready"), 3 * l + 2)
                        vs(ts(hg_sig[:, :, :], hg_sig[:, :, :], TINY, None, MAX), "hg_sig_floor", ev)
                        dve.wait_ge(S("hg_gates_ready"), 3 * ev)
                        dve.wait_ge(S("derived_ready"), 1)
                        v(tt(hg_k, hg_k, along(derived[:, l, 4:8], SEQ), MUL))
                        dve.sem_inc(S("hg_qk_ready"), 1)
                    if j == HG_LOGF:
                        dve.wait_ge(S("hg_logf"), 4 * ev)
                        v(nc.vector.tensor_tensor_scan(hg_b.rearrange(flat), C("reset"), hg_logf.rearrange(flat), 0.0,
                                                       MUL, ADD))
                        b4 = hg_b.rearrange("p h (c i) -> p (h c) i", i=64)
                        v(tt(hg_kend.rearrange("p h (c i) -> p (h c) i", i=64),
                             b4[:, :, 63:64].broadcast_to([P, JC, 64]), b4, SUB))
                        dve.sem_inc(S("hg_exponent"), 2)
                    for k in range(8):
                        if j == HG_LEVEL_SLOT[k] + 3:
                            masked(k)
                        if k and j == HG_LEVEL_SLOT[k]:
                            if k == 1:
                                factors(0)
                            factors(k)
                        if k >= 2 and j == HG_LEVEL_SLOT[k] - 2:
                            exponent(k)
                    if j == HG_CROSS:
                        dve.wait_ge(S("hg_exp"), 8 * l + 2)
                        tot = small[:, 160:176].rearrange("p (h c) -> p h c", h=4)
                        v(tt(hg_k128[:, :, 0:64], hg_kend[:, :, 0:64], tot[:, :, 1:2].broadcast_to([P, 4, 64]), MUL))
                        v(cp(hg_k128[:, :, 64:128], hg_kend[:, :, 64:128]))
                        v(cp(hg_q128[:, :, 0:64], hg_qbeg[:, :, 128:192]))
                        v(tt(hg_q128[:, :, 64:128], hg_qbeg[:, :, 192:256], tot[:, :, 2:3].broadcast_to([P, 4, 64]), MUL))
                        dve.sem_inc(S("hg_cross_factors"), 1)
                    if j == HG_GAIN:
                        dve.wait_ge(row_in, 16 * ev)
                        dve.wait_ge(S("hg_gate_silu"), ev)
                        for t in range(TT):
                            g3 = hg_gate[:, t, :].rearrange("p (h n) -> p h n", n=P)
                            u(tt(g3, g3, over(row[:, 0:128], 4, P), MUL))
                        settle()
                        dve.sem_inc(S("hg_gate_ready"), 1)
                    if j == HG_SQUARES:
                        dve.wait_ge(S("hg_squares"), ev)
                        v(red(small[:, 176:184], hg_sq.rearrange("p h (d n) -> p (h d) n", n=P), AX.X, ADD))
                        vs(ts(small[:, 184:192], small[:, 176:184], 1.0 / P, EPS, MUL, ADD), "hg_var", ev)
                    if j == HG_NORMED:
                        dve.wait_ge(S("hg_std"), ev)
                        v(rec(small[:, 176:184], small[:, 192:200]))
                        o3 = hg_o.rearrange("p t (h n) -> p (t h) n", n=P)
                        v(tt(o3, bank(4, 2).rearrange("p (n v) -> p n v", n=8), along(small[:, 176:184], P), MUL))
                        vs(tt(hg_o, hg_o, hg_gate, MUL), "hg_o_ready", ev)

                    if j == MLA_SQUARES:
                        dve.wait_ge(S("mla_in_squares"), 6 * ev)
                        for k, n in enumerate((Q_RANK, KV_RANK, ROPE)):
                            u(ts(small[:, 16 + 2 * k:18 + 2 * k], small[:, 8 + 2 * k:10 + 2 * k], 1.0 / n, EPS, MUL, ADD))
                        settle()
                        dve.sem_inc(S("mla_in_var"), 1)
                    if j == MLA_NORMED:
                        dve.wait_ge(S("mla_in_std"), ev)
                        v(rec(small[:, 8:14], small[:, 24:30]))
                        for t in range(TT):
                            u(ts(p_mla[:, t, 0:512], p_mla[:, t, 0:512], small[:, 8 + t:9 + t], None, MUL))
                            u(ts(p_mla[:, t, 512:768], p_mla[:, t, 512:768], small[:, 10 + t:11 + t], None, MUL))
                            u(ts(rb[:, t, 512:576], p_mla[:, t, 768:832], small[:, 12 + t:13 + t], None, MUL))
                        settle()
                        dve.sem_inc(S("mla_in_normed"), 1)
                store_p(len(IN_CHUNKS) - 1)
                dve.wait_ge(S("hg_mix_hi"), ev)
                vs(tt(hT_lo[:, 0:4, :], bank(6, 2).rearrange("p (h t) -> p h t", h=4), hT_hi[:, 0:4, :].bitcast(F32), SUB),
                   "hg_o_used", ev)

                dve.wait_ge(S("mla_q_squares"), 4 * ev)
                sq3 = mla_sq.rearrange("p (n d) -> p n d", d=QK)
                u(red(small[:, 32:48], sq3[:, :, 0:NOPE], AX.X, ADD))
                u(red(small[:, 48:64], sq3[:, :, NOPE:QK], AX.X, ADD))
                settle()
                u(ts(small[:, 32:48], small[:, 32:48], 1.0 / NOPE, EPS, MUL, ADD))
                u(ts(small[:, 48:64], small[:, 48:64], 1.0 / ROPE, EPS, MUL, ADD))
                settle()
                dve.sem_inc(S("mla_var"), 1)

                def k_var(hf):
                    dve.wait_ge(S("mla_k_squares"), 4 * l + 2 * hf + 2)
                    z = small[:, 64 + 8 * hf:72 + 8 * hf]
                    v(red(z, k_sq[:, hf, :, :], AX.X, ADD))
                    vs(ts(z, z, 1.0 / NOPE, EPS, MUL, ADD), "mla_var", 3 * l + hf + 2)

                kv4 = kvrow.rearrange("p t (h d) -> p t h d", d=256)

                def k_norm(hf):
                    dve.wait_ge(S("mla_std"), 3 * l + hf + 2)
                    dve.wait_ge(S("mla_up_ready"), 8 * l + 6 + 2 * hf)
                    v(rec(small[:, 64 + 8 * hf:72 + 8 * hf], small[:, 112 + 8 * hf:120 + 8 * hf]))
                    for t in range(TT):
                        z = kv4[:, t, 4 * hf:4 * hf + 4, 0:NOPE]
                        u(tt(z, z, along(small[:, 64 + 8 * hf + 4 * t:68 + 8 * hf + 4 * t], NOPE), MUL))
                    settle()
                    dve.sem_inc(S("mla_k_normed"), 1)

                q4 = qrow.rearrange("p t (h d) -> p t h d", d=QK)
                rb4 = rb.rearrange("p t (h d) -> p t h d", d=ROPE)
                ro4 = ro.rearrange("p t (h d) -> p t h d", d=ROPE)

                def rope(t):
                    x1, x2 = rb4[:, t, 0:9, 0:32], rb4[:, t, 0:9, 32:64]
                    co_, si_ = over(cs[:, 0, t, :], 9, 32), over(cs[:, 1, t, :], 9, 32)
                    v(tt(rb4[:, t, 0:8, :], q4[:, t, :, NOPE:QK], along(small[:, 48 + 8 * t:56 + 8 * t], ROPE), MUL))
                    v(tt(rb[:, t, 0:576], rb[:, t, 0:576], row[:, 128:704], MUL))
                    u(tt(ro4[:, t, 0:9, 0:32], x1, co_, MUL))
                    u(tt(rtmp[:, t, :, :], x2, si_, MUL))
                    u(tt(ro4[:, t, 0:9, 32:64], x2, co_, MUL))
                    settle()
                    v(tt(ro4[:, t, 0:9, 0:32], ro4[:, t, 0:9, 0:32], rtmp[:, t, :, :], SUB))
                    v(tt(rtmp[:, t, :, :], x1, si_, MUL))
                    v(tt(ro4[:, t, 0:9, 32:64], ro4[:, t, 0:9, 32:64], rtmp[:, t, :, :], ADD))
                    v(cp(ro4[:, t, 9, :], ro4[:, t, 8, :]))

                dve.wait_ge(S("mla_std"), 3 * l + 1)
                v(rec(small[:, 32:64], small[:, 80:112]))
                dve.wait_ge(S("mla_up_ready"), 8 * l + 4)
                q3 = qrow.rearrange("p t (h d) -> p (t h) d", d=QK)
                v(tt(q3[:, :, 0:NOPE], q3[:, :, 0:NOPE], along(small[:, 32:48], NOPE), MUL))
                dve.sem_inc(S("mla_q_normed"), 1)
                k_var(0)
                dve.wait_ge(S("cs_ready"), 2)
                rope(0)
                k_norm(0)
                rope(1)
                dve.sem_inc(S("mla_rope_done"), 1)
                k_var(1)
                k_norm(1)

                parts = ((0, slice(0, 128), 128), (8, slice(128, 384), 256))
                for hf in range(2):
                    h4 = slice(4 * hf, 4 * hf + 4)
                    dve.wait_ge(S("mla_s_mm"), 8 * l + 4 * hf + 4)
                    v(stt(scores[:, h4, :], psum[:, h4, 0:384], float(QK ** -0.5), over(C("attn"), 4, 384), MUL, ADD))
                    for off, cols, n in parts:
                        u(red(small[:, 32 + off + 4 * hf:36 + off + 4 * hf], scores[:, h4, cols], AX.X, MAX))
                    settle()
                    for off, cols, n in parts:
                        z = small[:, 32 + off + 4 * hf:36 + off + 4 * hf]
                        u(ts(z, z, -1.0, None, MUL))
                    settle()
                    dve.sem_inc(S("mla_max"), 1)
                for hf in range(2):
                    h4 = slice(4 * hf, 4 * hf + 4)
                    dve.wait_ge(S("mla_exp"), 16 * l + 8 * hf + 8)
                    for off, cols, n in parts:
                        u(rec(small[:, 64 + off + 4 * hf:68 + off + 4 * hf], small[:, 48 + off + 4 * hf:52 + off + 4 * hf]))
                    settle()
                    for off, cols, n in parts:
                        z = scores[:, h4, cols]
                        u(tt(z, z, along(small[:, 64 + off + 4 * hf:68 + off + 4 * hf], n), MUL))
                    settle()
                    dve.sem_inc(S("mla_probs"), 1)
                for hf in range(2):
                    k4 = slice(4 + 4 * hf, 8 + 4 * hf)
                    dve.wait_ge(S("mla_mix_hi"), 2 * l + hf + 1)
                    u(tt(hT_lo[:, k4, :], bank(2 * hf, 2).rearrange("p (h t) -> p h t", h=4), hT_hi[:, k4, :].bitcast(F32),
                         SUB))
                settle()
                dve.sem_inc(S("mla_mix_lo"), 1)

                v(nc.vector.memset(pT[:, :, 0:1], 0.0))
                for half, (a, b) in enumerate(((8, 14), (0, 8))):
                    dve.wait_ge(S("rw_pT_ready"), 2 * l + half + 1)
                    v(tt(pm[:, a:b, :], pT[:, a:b, 0:SEQ], pT[:, a:b, 1:SEQ + 1], SUB))
                    for f in range(b - 1, a - 1, -1):
                        u(stt(pm[:, f, :], pm[:, f, :], par_of(l, "mu")[:, f:f + 1], pT[:, f, 1:SEQ + 1], MUL, ADD))
                        if f == 12:
                            settle()
                            dve.sem_inc(S("rw_shifted"), 1)
                settle()
                dve.sem_inc(S("rw_shifted"), 1)
                v(tt(rw_kk, rw_k, along(par_of(l, "k_k"), SEQ), MUL))
                v(tt(rw_kk_sq, rw_kk, rw_kk, MUL))
                dve.sem_inc(S("rw_kk_squares"), 1)
                dve.wait_ge(S("rw_w_ready"), 4 * ev)
                v(nc.vector.tensor_tensor_scan(rw_b.rearrange(flat), C("reset"), rw_w.rearrange(flat), 0.0, MUL, ADD))
                b3 = rw_b.rearrange("p j (c i) -> p (j c) i", i=RC)
                v(ts(small[:, 32:48], b3[:, :, RC - 1], 0.5, None, MUL))
                v(tt(b3, b3, along(small[:, 32:48], RC), SUB))
                dve.sem_inc(S("rw_exponent"), 2)
                if l:
                    dve.wait_ge(S("rw_vmix_ready"), 4 * l)
                    v(tt(rw_e[2], v_first[:, :, :], rw_v, SUB))
                    v(tt(rw_e[2], rw_e[2], rw_e[0], MUL))
                    v(tt(rw_v, rw_v, rw_e[2], ADD))
                dve.sem_inc(S("rw_v_ready"), 1)
                dve.wait_ge(S("rw_kk_norm"), ev)
                v(ts(small[:, 128:144], small[:, 128:144], 1e-12, None, MAX))
                v(rec(small[:, 144:160], small[:, 128:144]))
                v(cp(rw_inv.rearrange("p n (h i) -> p n h i", i=64), small[:, 144:160].rearrange(
                    "p (n h) -> p n h", h=2).unsqueeze(3).broadcast_to([P, 8, 2, 64])))
                dve.sem_inc(S("rw_kk_scale"), 1)
                dve.wait_ge(S("rw_a_ready"), 4 * ev)
                for j in range(4):
                    v(ts(rw_e[2][:, j, :], rw_a[:, j, :], par_of(l, "k_a")[:, j:j + 1], derived[:, l, 8 + j:9 + j], MUL, ADD))
                v(tt(rw_k, rw_k, rw_e[2], MUL))
                v(tt(rw_e[2], rw_r, rw_k, MUL))
                dve.sem_inc(S("rw_rk"), 1)
                dve.wait_ge(S("rw_kk_mm"), 2 * ev)
                v(tt(rw_kk.rearrange(flat), rw_kk.rearrange(flat), bank(2, 2), MUL))
                v(tt(rw_a, rw_a, rw_kk, MUL))
                dve.wait_ge(S("rw_bonus_mm"), ev)
                v(tt(rw_e[2], rw_b, rw_w, SUB))
                dve.sem_inc(S("rw_exponent"), 1)
                v(tt(rw_bonus.rearrange(flat), bank(0, 2), rw_v.rearrange(flat), MUL))
                dve.wait_ge(S("rw_exp"), 3 * l + 1)
                r3, k3r, kk3, b3r, e0, e1, e2 = (z.rearrange("p j (c i) -> p (j c) i", i=RC) for z in (
                    rw_r, rw_k, rw_kk, rw_a, rw_e[0], rw_e[1], rw_e[2]))
                vs(tt(ar[:, :, 1, :], r3, e0, MUL), "rw_r_done", ev)
                dve.wait_ge(S("rw_exp"), 3 * l + 2)
                vs(tt(rw_a, rw_a, rw_e[1], MUL), "rw_b_done", ev)
                cp(diag_b[ODD, :, ODD], b3r[ODD, :, :]).then_inc(S("rw_diag_dve"), 1)
                dve.wait_ge(S("rw_exp"), 3 * l + 3)
                for hp in (EVEN, ODD):
                    tt(diag_k[hp, :, hp], k3r[hp, :, :], e1[hp, :, :], MUL).then_inc(S("rw_diag_dve"), 1)
                dve.wait_ge(S("rw_diag_dve"), 4 * l + 3)
                vs(tt(ar[:, :, 0, :], kk3, e2, MUL), "rw_ab_done", ev)
                cp(diag_a[ODD, :, ODD], ar[ODD, :, 0, :]).then_inc(S("rw_diag_dve"), 1)
                dve.wait_ge(S("rw_half_decay"), ev)
                hd = small[:, 48:64].rearrange("p (j c) -> p j c", j=4)
                md = small[:, 64:80].rearrange("p (j c) -> p j c", j=4)
                v(tt(md[:, :, 0:3], hd[:, :, 0:3], hd[:, :, 1:4], MUL))
                left4, right4 = (bank(b0, 4).rearrange("p (n two t) -> p n two t", n=JC, two=2) for b0 in (0, 4))
                for k, (dst, src, mask, product) in enumerate((
                        (mab, bank(6, 2).rearrange("p (n t) -> p n t", n=JC), "strict_lo", 1),
                        (mab_t, left4[:, :, 0, :], "strict_up", 2), (mrb_t, left4[:, :, 1, :], "incl_up", 2),
                        (mak_t, right4[:, :, 0, :], "strict_up", 3), (mrk_t, right4[:, :, 1, :], "incl_up", 3))):
                    dve.wait_ge(S("rw_m_mm"), 3 * l + product)
                    vs(tt(dst, src, over(C(mask), JC, RC), MUL), "rw_m_ready", 5 * l + k + 1)
                    if k == 2:
                        v(tt(inv_t, mab_t, over(C("pair_up"), JC, RC), MUL))
                        v(stt(inv_t, inv_t, -1.0, over(idst, JC, RC), MUL, ADD))
                        dve.sem_inc(S("rw_xt"), 2)
                        v(tt(inv, mab, over(C("pair_lo"), JC, RC), MUL))
                        v(stt(inv, inv, -1.0, over(idst, JC, RC), MUL, ADD))
                        dve.sem_inc(S("rw_x"), 2)
                        for hf in range(2):
                            h8 = slice(8 * hf, 8 * hf + 8)
                            cp(diag_x[ODD, h8, ODD], inv[ODD, h8, :]).then_inc(S("rw_diag_x_dve"), 1)
                for k in range(len(RW_LEVELS)):
                    last = k == len(RW_LEVELS) - 1
                    for hf in range(2):
                        if not last:
                            h8 = slice(8 * hf, 8 * hf + 8)
                            dve.wait_ge(S("rw_gt_ready"), 10 * l + 2 * k + hf + 1)
                            cp(diag_g[ODD, h8, ODD], g_t[ODD, h8, :]).then_inc(S("rw_diag_g_dve"), 1)
                    for hf in range(2):
                        h8 = slice(8 * hf, 8 * hf + 8)
                        dve.wait_ge(S("rw_dinv_mm"), 10 * l + 2 * k + hf + 1)
                        if not last:
                            vs(tt(inv[:, h8, :], inv[:, h8, :], bank(2 + hf).rearrange("p (n t) -> p n t", n=8), SUB),
                               "rw_x", 10 * l + 2 * k + hf + 3)
                            if k < len(RW_LEVELS) - 2:
                                cp(diag_x[ODD, h8, ODD], inv[ODD, h8, :]).then_inc(S("rw_diag_x_dve"), 1)
                            tt(inv_t[:, h8, :], inv_t[:, h8, :], bank(4 + hf).rearrange("p (n t) -> p n t", n=8),
                               SUB).then_inc(S("rw_xt"), 1)
                        else:
                            d3 = bank(4 + hf).rearrange("p (n t) -> p n t", n=8)
                            for up in UPPER:
                                z = inv_t[up, h8, 32:64]
                                u(tt(z, z, d3[up, :, 32:64], SUB))
                            settle()
                            dve.sem_inc(S("rw_xt"), 1)
                dve.wait_ge(S("rw_xt"), 12 * ev)
                for c in range(NC):
                    dve.wait_ge(S("rw_rhs_mm"), NC * l + c + 1)
                    vs(ts(rhs.rearrange("p a b -> p (a b)"), bank(0)[:, 0:256], -1.0, None, MUL), "rw_rhs_ready", NC * l + c + 1)
                    if c < NC - 1:
                        dve.wait_ge(S("rw_state_mm"), 3 * l + c + 1)
                        st = bank(2)[:, 0:256].rearrange("p (j n) -> p j n", j=4)
                        if c == 0:
                            v(tt(state[1], st, md[:, :, 0:1].broadcast_to([P, 4, RC]), MUL))
                        else:
                            v(tt(rhs, state[c % 2], st, ADD))
                            v(tt(state[(c + 1) % 2], rhs, md[:, :, c:c + 1].broadcast_to([P, 4, RC]), MUL))
                        dve.sem_inc(S("rw_state_ready"), 1)
                dve.wait_ge(S("rw_y_mm"), ev)
                y3 = bank(6, 2).rearrange("p (n v) -> p n v", n=JC)
                v(red(small[:, 80:96], y3, AX.X, ADD))
                v(ts(small[:, 80:96], small[:, 80:96], 1.0 / RC, None, MUL))
                v(tt(yc, y3, along(small[:, 80:96], RC), SUB))
                dve.sem_inc(S("rw_y_centred"), 1)

                s4o = s4 + N_IN // 4
                for c in range(4):
                    for j in range(4):
                        if j == 2 and c:
                            add_x(s4o, 4 * c, c - 1, 12 * l + c)
                            x_gain(2 * l + 1, c - 1)
                        if c == 0 and j == 3:
                            dve.wait_ge(S("rw_y_turned"), ev)
                            for i in range(4):
                                u(ts(y_out[:, i, :], bank(4, 2)[:, i * SEQ:(i + 1) * SEQ], par_of(l, "ln_w")[:, i:i + 1],
                                     par_of(l, "ln_b")[:, i:i + 1], MUL, ADD))
                            settle()
                            v(tt(y_out, y_out, rw_bonus, ADD))
                            dve.wait_ge(S("rw_g_ready"), 2 * ev)
                            v(tt(y_out, y_out, rw_gate, MUL))
                            dve.sem_inc(S("rw_out"), 1)
                        split_lo(s4o, 4 * c + j)
                        if c == 0 and j == 0:
                            dve.wait_ge(S("rw_y_squares"), ev)
                            v(red(small[:, 80:96], ysq, AX.X, ADD))
                            vs(ts(small[:, 96:112], small[:, 80:96], 1.0 / RC, GN_EPS, MUL, ADD), "rw_y_var", ev)
                        if c == 0 and j == 1:
                            dve.wait_ge(S("rw_y_std"), ev)
                            v(rec(small[:, 80:96], small[:, 112:128]))
                            v(tt(yc, yc, along(small[:, 80:96], RC), MUL))
                            dve.sem_inc(S("rw_y_normed"), 1)
                        if c == 0 and j == 3:
                            dve.wait_ge(S("rw_mix_hi"), ev)
                            vs(tt(hT_lo[:, 12:16, :], y_out, hT_hi[:, 12:16, :].bitcast(F32), SUB), "rw_mix_lo", ev)
                        if 3 <= 4 * c + j < 7:
                            n = 4 * c + j - 3
                            cp(act_lo[:, 4 * n:4 * n + 4, :], hT_lo[:, 4 * n:4 * n + 4, :].bitcast(F32)).then_inc(
                                S("mix_lo_kept"), 1)
                        if c and j == 3:
                            x_lo(2 * l + 1, c - 1)

                s4f = s4o + N_O // 4
                pair0 = sum(PAIRS) * l
                odd0 = acc_base(l) + len(IN_CHUNKS) // 2 + 2

                for n, pairs in enumerate(PAIRS):
                    def act_rows(i, si, p0):
                        dve.wait_ge(half_used, chunk_ends(si, 8))
                        dve.wait_ge(acc_free[0], i + (gate_base + 2))
                        if not isinstance(i, int) or i + p0 > 0:
                            dve.wait_ge(S("act_turned"), i + p0)
                        stt(act_row[:, 0, :], psum[:, 2, :], rstd[:, 0:1], silu[:, 0, :], MUL, MUL)
                        stt(act_row[:, 1, :], psum[:, 3, :], rstd[:, 1:2], silu[:, 1, :], MUL, MUL).then_inc(acc_free[1], 1)
                        dve.wait_ge(acc_free[1], i + (gate_base + 2))
                        dve.sem_inc(S("act_row_ready"), 1)

                    def turned_lo(i, p0):
                        dve.wait_ge(S("act_hi_ready"), i + (p0 + 1))
                        k = bass.ds(i * 4, 4) if not isinstance(i, int) else slice(4 * i, 4 * i + 4)
                        tt(act_lo[:, k, :], bank(4, 2).rearrange("p (k t) -> p k t", k=4), act_hi[:, k, :].bitcast(F32),
                           SUB).then_inc(S("act_lo_ready"), 1)

                    gate_base = odd0 + sum(PAIRS[:n]) + 4 * n // 2

                    def pair(i, first):
                        si = i * 2 + s4f
                        for j in range(8):
                            if j == 2 and not first:
                                act_rows(i - 1, si - 2, pair0)
                            if j == 2 and first:
                                add_x(s4f, 0, 3, 12 * l + 4 * (n + 1))
                                if n == 0:
                                    x_gain(2 * l + 1, 3)
                            if j == 6 and not first:
                                turned_lo(i - 1, pair0)
                            split_lo(si, j)
                            if n == 0 and first:
                                norm_tail(2 * l + 1, j)

                    pair(0, True)
                    with dve.Fori(1, pairs) as i:
                        pair(i, False)
                    last_si = s4f + 2 * (pairs - 1)
                    s4f = s4f + 2 * pairs
                    for c in range(4):
                        for j in range(pairs):
                            if j == 2 and c == 0:
                                act_rows(pairs - 1, last_si, pair0)
                            makes_norm = n == len(PAIRS) - 1 and l < DEPTH - 1
                            if j == 2 and c:
                                add_x(s4f, pairs * c, c - 1, 12 * l + 4 * (n + 1) + c)
                                if makes_norm:
                                    x_gain(2 * l + 2, c - 1)
                            split_lo(s4f, pairs * c + j)
                            if j == 3 and c == 0:
                                turned_lo(pairs - 1, pair0)
                            if j == 3 and c and makes_norm:
                                x_lo(2 * l + 2, c - 1)
                    s4f = s4f + pairs
                    pair0 += pairs
                if l == DEPTH - 1:
                    add_x(s4f, 0, 3, 12 * DEPTH)

        @block.tensor
        def _(pe):
            mm, tr = nc.tensor.matmul, nc.tensor.transpose
            pe.sem_inc(half_used, HALF_RING)
            pe.sem_inc(acc_free[0], 1)
            pe.sem_inc(acc_free[1], 1)

            def slots(s4, js, k0, n_k, b0, lhi, llo, w=CH):
                for n, j in enumerate(js):
                    for hf in range(2):
                        q = 2 * j + hf
                        pe.wait_ge(lo_done, s4 * 8 + (q + 1))
                        r = q % HALF_RING
                        for k2 in range(2):
                            k = k0 + 4 * n + 2 * hf + k2
                            cols = slice(k2 * w, (k2 + 1) * w)
                            for t in range(TT):
                                o = psum[:, b0 + t, 0:w]
                                a_hi, a_lo = lhi[:, k, t * P:(t + 1) * P], llo[:, k, t * P:(t + 1) * P]
                                mm(o, a_hi, w_hi[:, r, cols], start=(k == 0), stop=False)
                                mm(o, a_hi, w_lo[:, r, cols], start=False, stop=False)
                                last = mm(o, a_lo, w_hi[:, r, cols], start=False, stop=(k == n_k - 1))
                        last.then_inc(half_used, 1)

            def x_turn(n, c):
                pe.wait_ge(S("xg_ready"), 4 * n + c + 1)
                if n:
                    pe.wait_ge(S("hT_ready"), 4 * n + c)
                for k in range(4):
                    for t in range(TT):
                        last = tr(bank(x_turn_bank(n, c), 2)[:, k * SEQ + t * P:k * SEQ + (t + 1) * P],
                                  xg_tile(n, c)[:, t, k * P:(k + 1) * P], ident)
                last.then_inc(S("x_turned"), 1)

            def first_slot(n, s4, j, b0, w=CH):
                pe.wait_ge(S("hT_ready"), 4 * n + j + 1)
                slots(s4, [j], 4 * j, KT, b0, hT_hi, hT_lo, w)
                if j == 1:
                    x_turn(n, 3)

            def heads(fn):
                last = None
                for p0 in (0, 64):
                    last = fn(slice(p0, p0 + 64))
                return last

            pe.wait_ge(ident_in, 16)
            for l in range(DEPTH):
                ev = l + 1
                s4 = l * SPLIT_PER_LAYER // 4
                acc0 = l * (len(IN_CHUNKS) // 2 + 2 + sum(PAIRS) + 4)
                if l == 0:
                    for c in range(3):
                        x_turn(0, c)

                def level(k):
                    if k >= 2:
                        pe.wait_ge(S("hg_masked"), 8 * l + k - 1)
                    if k == 2:
                        pe.wait_ge(S("hg_cross_ready"), ev)
                    if k == 0:
                        pe.wait_ge(S("hg_qk_ready"), ev)
                    else:
                        pe.wait_ge(S("hg_factors"), 7 * l + k)
                    left, right = ((hg_k, hg_q) if k == 0 else (hg_kend, hg_qbeg) if k == 1 else (hg_e[k % 4],) * 2)
                    for h in range(HG_H):
                        for d in range(TT):
                            n = h * TT + d
                            last = mm(bank(4 + 2 * (k % 2), 2)[:, n * P:(n + 1) * P], left[:, h, d * P:(d + 1) * P],
                                      right[:, h, d * P:(d + 1) * P], start=True, stop=True)
                    last.then_inc(S("hg_level_mm"), 1)

                for j in range(N_IN):
                    c = j // 4
                    if j % 4 == 0:
                        pe.wait_ge(acc_free[c % 2], acc0 + c // 2 + 1)
                    if c == 0:
                        first_slot(2 * l, s4, j, 0)
                    else:
                        slots(s4, [j], 4 * (j % 4), KT, 2 * (c % 2), hT_hi, hT_lo, IN_CHUNKS[c][1])

                    if j == MLA_TURN_Q:
                        pe.wait_ge(S("mla_in_normed"), ev)
                        pe.wait_ge(S("hg_masked"), 8 * ev)
                        for k in range(4):
                            for t in range(TT):
                                last = tr(bank(6, 2)[:, k * SEQ + t * P:k * SEQ + (t + 1) * P],
                                          p_mla[:, t, k * P:(k + 1) * P], ident)
                        last.then_inc(S("mla_in_turned"), 1)
                    if j == MLA_TURN_KV:
                        pe.wait_ge(S("hg_o_ready"), ev)
                        for k in range(2):
                            for t in range(TT):
                                last = tr(bank(4)[:, k * SEQ + t * P:k * SEQ + (t + 1) * P],
                                          p_mla[:, t, (4 + k) * P:(5 + k) * P], ident)
                        last.then_inc(S("mla_in_turned"), 1)

                    if j == HG_TURN:
                        pe.wait_ge(S("p_ready"), len(IN_CHUNKS) * l + 2)
                        for k in range(2):
                            for h in range(HG_H):
                                for t in range(TT):
                                    last = tr(bank(4 + 2 * k, 2)[:, h * SEQ + t * P:h * SEQ + (t + 1) * P],
                                              p_hg[:, t, k * CH + h * P:k * CH + (h + 1) * P], ident)
                            last.then_inc(S("hg_turned"), 1)
                    for k in range(8):
                        if j == HG_LEVEL_SLOT[k]:
                            level(k)
                    if j == HG_CROSS:
                        pe.wait_ge(S("hg_cross_factors"), ev)
                        pe.wait_ge(S("hg_masked"), 8 * l + 1)
                        for h in range(HG_H):
                            last = mm(bank(4)[:, h * P:(h + 1) * P], hg_k128[:, h, :], hg_q128[:, h, :],
                                      start=True, stop=True)
                        last.then_inc(S("hg_cross_mm"), 1)
                    if j == HG_OUT:
                        pe.wait_ge(S("hg_masked"), 8 * ev)
                        pe.wait_ge(S("p_ready"), len(IN_CHUNKS) * l + 3)
                        for d in range(TT):
                            for h in range(HG_H):
                                o = psum[:, 4 + d, h * P:(h + 1) * P]
                                vv = [p_hg[:, t, 1024 + h * P:1024 + (h + 1) * P] for t in range(TT)]
                                if d:
                                    mm(o, hg_cross[:, h, :], vv[0], start=True, stop=False)
                                last = mm(o, hg_diag[:, h * TT + d, :], vv[d], start=(d == 0), stop=True)
                        last.then_inc(S("hg_o_mm"), 1)
                pe.wait_ge(S("hg_o_ready"), ev)
                pe.wait_ge(S("mla_inT_ready"), 6 * l + 4)
                for h in range(HG_H):
                    for t in range(TT):
                        last = tr(bank(6, 2)[:, h * SEQ + t * P:h * SEQ + (t + 1) * P], hg_o[:, t, h * P:(h + 1) * P], ident)
                last.then_inc(S("hg_o_turned"), 1)

                pe.wait_ge(S("mla_inT_ready"), 6 * ev)
                g4 = (l * SLOTS_PER_LAYER + N_IN) // 4
                for c in range(8):
                    if c == 1:
                        pe.wait_ge(S("hg_o_used"), ev)
                    if c == 2:
                        pe.wait_ge(S("p_ready"), len(IN_CHUNKS) * ev)
                    if c >= 4:
                        pe.wait_ge(S("mla_up_ready"), 8 * l + c - 3)
                    pe.wait_ge(raw_in[c % 4], 16 * (g4 + c // 4 + 1))
                    w, nk, src = (384, 4, qaT) if c < 4 else (CH, 2, kvaT)
                    for t in range(TT):
                        for k in range(nk):
                            last = mm(psum[:, (4 + 2 * c) % 8 + t, 0:w], src[:, k, t * P:(t + 1) * P],
                                      raw[:, c % 4, k * w:(k + 1) * w], start=(k == 0), stop=(k == nk - 1))
                    last.then_inc(S("mla_up_mm"), 1)
                    pe.wait_ge(S("mla_up_mm"), 8 * l + c + 1)
                    pe.sem_inc(plain_used, 1)
                pe.wait_ge(S("mla_up_ready"), 8 * ev)
                pe.wait_ge(S("mla_q_normed"), ev)
                for h in range(MLA_H):
                    for t in range(TT):
                        last = tr(bank(0, 4)[:, h * SEQ + t * P:h * SEQ + (t + 1) * P],
                                  qrow[:, t, h * QK:h * QK + NOPE], ident)
                last.then_inc(S("mla_q_turned"), 1)

                def k_turn(hf):
                    pe.wait_ge(S("mla_k_normed"), 2 * l + hf + 1)
                    for h in range(4):
                        for t in range(TT):
                            last = tr(bank(4 + 2 * hf, 2)[:, h * SEQ + t * P:h * SEQ + (t + 1) * P],
                                      kvrow[:, t, (4 * hf + h) * 256:(4 * hf + h) * 256 + NOPE], ident)
                    last.then_inc(S("mla_k_turned"), 1)

                def attend(hf):
                    pe.wait_ge(S("mla_kT_ready"), 2 * l + hf + 1)
                    for h in range(4 * hf, 4 * hf + 4):
                        hp = slice(64 * (h % 2), 64 * (h % 2) + 64)
                        for qt, cols, keys in ((0, slice(0, 128), 128), (1, slice(128, 384), 256)):
                            o = psum[:, h, cols]
                            tq = slice(qt * P, (qt + 1) * P)
                            mm(o, qnT[:, h, tq], knT[:, h, 0:keys], start=True, stop=False)
                            last = mm(o, rT[hp, h // 2, tq], rkT[hp, 0:keys], start=False, stop=True)
                        last.then_inc(S("mla_s_mm"), 1)

                k_turn(0)
                pe.wait_ge(S("mla_rope_done"), ev)
                pe.wait_ge(S("mla_qT_ready"), ev)
                for k in range(5):
                    for t in range(TT):
                        last = tr(bank(0, 3)[:, k * SEQ + t * P:k * SEQ + (t + 1) * P], ro[:, t, k * P:(k + 1) * P], ident)
                last.then_inc(S("mla_r_turned"), 1)
                pe.wait_ge(S("mla_rT_ready"), 2 * ev)
                attend(0)
                k_turn(1)
                attend(1)
                for hf in range(2):
                    pe.wait_ge(S("mla_probs"), 2 * l + hf + 1)
                    for h in range(4 * hf, 4 * hf + 4):
                        for n in range(3):
                            last = tr(psum[:, h, n * P:(n + 1) * P], scores[:, h, n * P:(n + 1) * P], ident)
                        last.then_inc(S("mla_p_turned"), 1)
                for hf in range(2):
                    pe.wait_ge(S("mla_pT_ready"), 2 * l + hf + 1)
                    for h in range(4 * hf, 4 * hf + 4):
                        o = bank(0, 4)[:, h * SEQ:(h + 1) * SEQ]
                        vv = [kvrow[:, t, h * 256 + NOPE:(h + 1) * 256] for t in range(TT)]
                        mm(o, vv[0], probsT[:, h, 0:256], start=True, stop=False)
                        last = mm(o[:, 128:256], vv[1], probsT[:, h, 256:384], start=False, stop=True)
                    last.then_inc(S("mla_o_mm"), 1)

                for f in [*range(8, RW_F), *range(8)]:
                    if f == 0:
                        pe.wait_ge(S("mla_mix_lo"), ev)
                    b0 = 0 if f < 8 else 4
                    for t in range(TT):
                        last = tr(bank(b0, 4)[:, (f % 8) * SEQ + t * P:(f % 8) * SEQ + (t + 1) * P],
                                  p_rw[:, t, f * P:(f + 1) * P], ident)
                    if f in (7, 13):
                        last.then_inc(S("rw_turned"), 1)
                pe.wait_ge(lora_in, 16 * ev)
                pe.wait_ge(S("rw_lora_in"), 2 * ev)
                for k, (b0, w, src, hp) in enumerate(((4, lora_of("wa"), rw_sig, slice(0, 64)),
                                                      (6, lora_of("wa"), pm[:, 12, :], slice(64, 128)),
                                                      (0, lora_of("g2"), rw_tmp[:, 0, :], slice(0, 128)))):
                    if k == 2:
                        pe.wait_ge(S("rw_kk_squares"), ev)
                        for t in range(TT):
                            for j in range(4):
                                n = 4 * t + j
                                last = mm(bank(2)[:, 2 * n:2 * n + 2], rw_kk_sq[:, j, t * P:(t + 1) * P], C("ones2")[:, 0:P:64],
                                          start=True, stop=True)
                        last.then_inc(S("rw_kk_mm"), 1)
                    if k != 1:
                        pe.wait_ge(S("rw_pT_ready"), 2 * l + (2 if k else 1))
                    for j in range(4):
                        last = mm(bank(b0, 2)[:, j * SEQ:(j + 1) * SEQ], w[hp, j * P:(j + 1) * P], src[hp, :],
                                  start=True, stop=True)
                    last.then_inc(S("rw_lora_mm"), 1)
                if l:
                    v1 = lora_of("v1")
                    pe.wait_ge(S("rw_shifted"), 2 * ev)
                    pe.wait_ge(S("rw_a_ready"), 4 * ev)
                    for k in range(4):
                        last = mm(bank(6)[0:32, 0:SEQ], v1[:, k * 32:(k + 1) * 32], rw_v[:, k, :], start=(k == 0), stop=(k == 3))
                    last.then_inc(S("rw_v1_mm"), 1)
                    pe.wait_ge(S("rw_v1_ready"), l)
                    for j in range(4):
                        last = mm(bank(6, 2)[:, j * SEQ:(j + 1) * SEQ], lora_of("v2")[0:32, j * P:(j + 1) * P],
                                  rw_bonus[0:32, 0, :], start=True, stop=True)
                    last.then_inc(S("rw_v2_mm"), 1)
                pe.wait_ge(S("rw_kk_scale"), ev)
                for t in range(TT):
                    for j in range(4):
                        last = tr(bank(2, 2)[:, j * SEQ + t * P:j * SEQ + (t + 1) * P], rw_inv[:, 4 * t + j, :], ident)
                last.then_inc(S("rw_kk_mm"), 1)

                def both_heads(b0, ns, left, right, w):
                    last = None
                    for m, n in enumerate(ns):
                        last = mm(bank(b0, 8 - b0)[:, m * w:(m + 1) * w], left[:, n, :], right(n), start=True, stop=True)
                    return last

                def quarters(b0, ns, left, right):
                    last = None
                    for m, n in enumerate(ns):
                        for h in range(2):
                            last = mm(bank(b0)[UPPER[h], m * RC + 32:(m + 1) * RC], left(h, n), right(h, n),
                                      start=True, stop=True)
                    return last

                def b_of(n):
                    return rw_a[:, n // NC, (n % NC) * RC:(n % NC + 1) * RC]

                def ar_of(n):
                    return ar[:, n, :, :].rearrange("p two i -> p (two i)")

                def turned_tiles(b0, tiles):
                    last = None
                    for n in range(JC):
                        last = tr(bank(b0, 4)[:, n * P:(n + 1) * P], tiles[:, n, :], ident)
                    return last

                pe.wait_ge(S("rw_rk"), ev)
                pe.wait_ge(S("rkb_ready"), 4 * ev)
                pe.wait_ge(S("rw_g_ready"), 2 * l + 1)
                for j in range(4):
                    last = mm(bank(0, 2)[:, j * SEQ:(j + 1) * SEQ], rkb[:, j, :], rw_e[2][:, j, :], start=True, stop=True)
                last.then_inc(S("rw_bonus_mm"), 1)
                pe.wait_ge(S("rw_zeroed"), 8 * l + 4)
                pe.wait_ge(S("rw_diag_act"), 4 * l + 2)
                pe.wait_ge(S("rw_a_ready"), 4 * ev)
                turned_tiles(4, diag_v).then_inc(S("rw_stack_mm"), 1)
                pe.wait_ge(S("rw_diag_act"), 4 * l + 3)
                pe.wait_ge(S("rw_diag_dve"), 4 * l + 1)
                pe.wait_ge(S("rw_stacked"), 6 * l + 2)
                turned_tiles(4, diag_b).then_inc(S("rw_stack_mm"), 1)
                pe.wait_ge(S("rw_zeroed"), 8 * l + 6)
                pe.wait_ge(S("rw_diag_dve"), 4 * l + 3)
                pe.wait_ge(S("rw_g_ready"), 2 * l + 1)
                turned_tiles(0, diag_k).then_inc(S("rw_stack_mm"), 1)
                pe.wait_ge(S("rw_zeroed"), 8 * ev)
                pe.wait_ge(S("rw_diag_act"), 4 * ev)
                pe.wait_ge(S("rw_diag_dve"), 4 * ev)
                pe.wait_ge(S("rw_stacked"), 6 * l + 4)
                both_heads(6, range(JC), diag_a, b_of, RC).then_inc(S("rw_m_mm"), 1)
                pe.wait_ge(S("rw_stacked"), 6 * ev)
                both_heads(0, range(JC), diag_b, ar_of, 2 * RC).then_inc(S("rw_m_mm"), 1)
                pe.wait_ge(S("rw_m_ready"), 5 * l + 1)
                both_heads(4, range(JC), diag_k, ar_of, 2 * RC).then_inc(S("rw_m_mm"), 1)
                for k in range(len(RW_LEVELS)):
                    last = k == len(RW_LEVELS) - 1
                    pe.wait_ge(S("rw_level_ready"), 10 * l + 2 * k + 2)
                    for hf in range(2):
                        ns = range(8 * hf, 8 * hf + 8)
                        pe.wait_ge(S("rw_xt"), 12 * l + 2 * k + hf + 1)
                        if last:
                            quarters(hf, ns, lambda h, n: diag_l[LOWER[h], n, 64 * h:64 * h + 32],
                                     lambda h, n: inv_t[LOWER[h], n, 32:64]).then_inc(S("rw_gt_mm"), 1)
                        else:
                            both_heads(hf, ns, diag_l, lambda n: inv_t[:, n, :], RC).then_inc(S("rw_gt_mm"), 1)
                    if k == 0:
                        pe.wait_ge(S("rw_m_ready"), 5 * ev)
                    for hf in range(2):
                        ns = range(8 * hf, 8 * hf + 8)
                        pe.wait_ge(S("rw_gt_ready"), 10 * l + 2 * k + hf + 1)
                        if not last:
                            pe.wait_ge(S("rw_diag_g_act"), 8 * l + 2 * k + hf + 1)
                            pe.wait_ge(S("rw_diag_g_dve"), 8 * l + 2 * k + hf + 1)
                            both_heads(2 + hf, ns, diag_g, lambda n: inv[:, n, :], RC)
                            pe.wait_ge(S("rw_diag_x_act"), 8 * l + 2 * k + hf + 1)
                            pe.wait_ge(S("rw_diag_x_dve"), 8 * l + 2 * k + hf + 1)
                            both_heads(4 + hf, ns, diag_x, lambda n: g_t[:, n, :], RC).then_inc(S("rw_dinv_mm"), 1)
                        else:
                            quarters(4 + hf, ns, lambda h, n: inv[UPPER[h], n, 0:32],
                                     lambda h, n: g_t[UPPER[h], n, 32:64]).then_inc(S("rw_dinv_mm"), 1)
                pe.wait_ge(S("rw_xt"), 12 * ev)
                for c in range(NC):
                    def each(b0, off, terms):
                        last = None
                        for j in range(4):
                            for hp in (slice(0, 64), slice(64, 128)):
                                for n, (left, right) in enumerate(terms):
                                    last = mm(bank(b0, 2)[hp, off + j * RC:off + (j + 1) * RC], left(hp, j), right(hp, j),
                                              start=(n == 0), stop=(n == len(terms) - 1))
                        return last

                    def in_ar(which):
                        return lambda hp, j: ar[hp, NC * j + c, which, :]

                    def stacked(z):
                        return lambda hp, j: z[hp, NC * j + c, :]

                    def pair_of(z):
                        return lambda hp, j: z[hp, j, :]

                    if c:
                        pe.wait_ge(S("rw_state_ready"), 3 * l + c)
                    carried = [(in_ar(0), pair_of(state[c % 2]))] if c else []
                    each(0, 0, carried + [(stacked(mak_t), stacked(v_st))]).then_inc(S("rw_rhs_mm"), 1)
                    pe.wait_ge(S("rw_rhs_ready"), NC * l + c + 1)
                    each(1, 0, [(stacked(inv_t), pair_of(rhs))]).then_inc(S("rw_sa_mm"), 1)
                    pe.wait_ge(S("rw_sa_ready"), NC * l + c + 1)
                    if c < NC - 1:
                        each(2, 0, [(stacked(b_st), pair_of(sa)), (stacked(k_st), stacked(v_st))]).then_inc(S("rw_state_mm"), 1)
                    carried = [(in_ar(1), pair_of(state[c % 2]))] if c else []
                    last = each(6, 256 * c, carried + [(stacked(mrb_t), pair_of(sa)), (stacked(mrk_t), stacked(v_st))])
                last.then_inc(S("rw_y_mm"), 1)
                s4o = s4 + N_IN // 4
                acc = acc0 + len(IN_CHUNKS) // 2
                for c in range(4):
                    pe.wait_ge(acc_free[c % 2], acc + c // 2 + 1)
                    for j in range(4):
                        if c == 0 and j == 3:
                            pe.wait_ge(S("rw_mix_lo"), ev)
                        if c == 1:
                            pe.wait_ge(S("mix_hi_kept"), 4 * l + j + 1)
                            pe.wait_ge(S("mix_lo_kept"), 4 * l + j + 1)
                        slots(s4o, [4 * c + j], 4 * j, KT, 2 * (c % 2), *((act_hi, act_lo) if c else (hT_hi, hT_lo)))
                        if c == 0 and j == 1:
                            pe.wait_ge(S("rw_y_normed"), ev)
                            for n in range(JC):
                                i, k = n % 4, n // 4
                                last = heads(lambda hp: mm(bank(4, 2)[hp, i * SEQ + k * RC:i * SEQ + (k + 1) * RC],
                                                           yc[hp, n, :], idst[hp, :], start=True, stop=True))
                            last.then_inc(S("rw_y_turned"), 1)
                        if c and j == 1:
                            x_turn(2 * l + 1, c - 1)
                acc += 2

                s4f = s4o + N_O // 4
                pair0 = sum(PAIRS) * l
                for part, pairs in enumerate(PAIRS):
                    makes_norm = part == len(PAIRS) - 1 and l < DEPTH - 1

                    def turn(i, p0):
                        pe.wait_ge(S("act_row_ready"), i + (p0 + 1))
                        if not isinstance(i, int) or i + p0 > 0:
                            pe.wait_ge(S("act_lo_ready"), i + p0)
                        for k in range(4):
                            for t in range(TT):
                                last = tr(bank(4, 2)[:, k * SEQ + t * P:k * SEQ + (t + 1) * P],
                                          act_row[:, t, k * P:(k + 1) * P], ident)
                        last.then_inc(S("act_turned"), 1)

                    def pair(i, first):
                        si = i * 2 + s4f
                        for u in range(2):
                            pe.wait_ge(acc_free[u], i + (acc + 1))
                            if part == 0 and first and u == 0:
                                for j in range(4):
                                    first_slot(2 * l + 1, si, j, 0)
                            else:
                                slots(si, range(4 * u, 4 * u + 4), 0, KT, 2 * u, hT_hi, hT_lo)
                            if u == 0 and not first:
                                turn(i - 1, pair0)

                    pair(0, True)
                    with pe.Fori(1, pairs) as i:
                        pair(i, False)
                    s4f, acc = s4f + 2 * pairs, acc + pairs
                    for c in range(4):
                        pe.wait_ge(acc_free[c % 2], acc + c // 2 + 1)
                        for j in range(pairs):
                            if c == 0 and j == 3:
                                turn(pairs - 1, pair0)
                            if c == 0 and j == pairs - 1:
                                pe.wait_ge(S("act_lo_ready"), pair0 + pairs)
                            slots(s4f, [pairs * c + j], 4 * j, 4 * pairs, 2 * (c % 2), act_hi, act_lo)
                            if makes_norm and c and j == 1:
                                x_turn(2 * l + 2, c - 1)
                    s4f, acc = s4f + pairs, acc + 2
                    pair0 += pairs


def shape_constants():
    i, j = np.arange(P)[:, None], np.arange(P)[None, :]
    out = {"ident": (i == j)}
    masks = []
    for m in HG_LEVELS:
        masks.append((i == j) if m == 0 else
                     (i // (2 * m) == j // (2 * m)) & (i // m % 2 == 0) & (j // m % 2 == 1))
    out["hg_masks"] = np.concatenate(masks, 1)
    low = np.where(j <= i, 0.0, -1e30)
    out["attn"] = np.concatenate([low, np.zeros((P, P)), low], 1)
    out["reset"] = np.broadcast_to((np.arange(1024) % 64 != 0)[None, :], (P, 1024))
    out["ones2"] = (i // 64 == j // 64)
    a, b = (np.arange(P) % RC)[:, None], np.arange(RC)[None, :]
    out["idst"] = a == b
    out["strict_lo"] = a > b
    out["strict_up"] = a < b
    out["incl_up"] = a <= b
    out["pair_lo"] = (a // 2 == b // 2) & (a > b)
    out["pair_up"] = (a // 2 == b // 2) & (a < b)
    out["lev_lo"] = np.concatenate([(a // (2 * m) == b // (2 * m)) & (a // m % 2 == 1) & (b // m % 2 == 0)
                                    for m in RW_LEVELS], 1)
    half = ROPE // 2
    freq = np.float32(10000.0) ** (-np.arange(half, dtype=np.float32) / np.float32(half))
    out["inv_freq"] = np.broadcast_to(freq[None, :], (P, half))
    return np.ascontiguousarray(np.concatenate([np.asarray(out[n], np.float32) for n in CONST_COLS], 1))


def kernel(**inputs):
    import concourse.bacc as bacc
    from concourse.bass_utils import run_bass_kernel_spmd

    a = {k: np.asarray(z) for k, z in inputs.items()}

    def tiles(w, k_rows, cols):
        K, N = w.shape
        t = w.reshape(K // k_rows, k_rows // P, P, N // cols, cols).transpose(3, 0, 2, 1, 4)
        return t.reshape(N // cols, K // k_rows, P, (k_rows // P) * cols)

    def padded(t):
        full = np.zeros(t.shape[:-1] + (4 * CH,), np.float32)
        full[..., :t.shape[-1]] = t
        return full.reshape(-1, P, 4 * CH)

    slots = []
    for l in range(DEPTH):
        for c, w in IN_CHUNKS:
            slots.append(padded(tiles(a["w_in"][l][:, c:c + w], 512, w)))
        slots.append(padded(tiles(a["mla_w_qb"][l], 512, 384)))
        slots.append(padded(tiles(a["mla_w_kvb"][l], 256, CH)))
        slots.append(padded(tiles(a["w_o"][l], 512, CH)))
        first = 0
        for pairs in PAIRS:
            cols = slice(first * CH, (first + pairs) * CH)
            gate = tiles(a["w_gate_up"][l][:, :D_FF][:, cols], 512, CH)
            up = tiles(a["w_gate_up"][l][:, D_FF:][:, cols], 512, CH)
            slots.append(np.stack([gate, up], 1).reshape(-1, P, 4 * CH))
            slots.append(padded(tiles(a["w_down"][l][cols], 512, CH)))
            first += pairs
    stream = np.concatenate(slots, 0)
    assert stream.shape[0] == DEPTH * SLOTS_PER_LAYER

    def cols(z):
        return z.reshape(-1, P).T

    params, lora, rows, gains = [], [], [], []
    for l in range(DEPTH):
        qn, kn = a["mla_q_norm"][l], a["mla_k_norm"][l]
        par = dict(hg_lb=cols(a["hg_lower_bounds"][l]), q_a=cols(a["mla_q_a_norm"][l]), kv_a=cols(a["mla_kv_a_norm"][l]),
                   gq=cols(qn[:NOPE]), gk=cols(kn[:NOPE]), mu=cols(a["rw_mu"][l]), w0=cols(a["rw_w0"][l]),
                   a0=cols(a["rw_a0"][l]), v0=cols(a["rw_v0"][max(l - 1, 0)]), k_k=cols(a["rw_k_k"][l]),
                   k_a=cols(a["rw_k_a"][l]), r_k=cols(a["rw_r_k"][l].reshape(-1)), ln_w=cols(a["rw_ln_w"][l]),
                   ln_b=cols(a["rw_ln_b"][l]))
        params.append(np.concatenate([par[n] for n in PARAM_COLS], 1))
        v1 = a["rw_v1"][max(l - 1, 0)].reshape(4, P, 32).transpose(1, 0, 2).reshape(P, 128)
        v2 = a["rw_v2"][max(l - 1, 0)]
        lora.append(np.concatenate([np.concatenate([a["rw_w2"][l], a["rw_a2"][l]], 0), a["rw_g2"][l], v1,
                                    np.concatenate([v2] * 4, 0)], 1))
        rows.append(np.concatenate([a["hg_out_norm"][l]] + [qn[NOPE:]] * MLA_H + [kn[NOPE:]]))
        gains += [a["attn_norm"][l], a["ffn_norm"][l]]
    arrays = dict(
        stream=stream, x_in=a["x"].reshape(SEQ, D), positions=np.ascontiguousarray(a["positions"].reshape(TT, P).T),
        params=np.ascontiguousarray(np.concatenate(params, 1)), consts=shape_constants(),
        lora=np.stack(lora), gains=np.stack(gains), rows=np.stack(rows))
    nc = bacc.Bacc("TRN2", target_bir_lowering=False, num_devices=1)
    args = {n: nc.dram_tensor(n + "_dram", z.shape, mybir.dt.from_np(z.dtype), kind="ExternalInput").ap()
            for n, z in arrays.items()}
    out = nc.dram_tensor("out_dram", (SEQ, D), F32, kind="ExternalOutput").ap()
    build(nc, out=out, **args)
    r = run_bass_kernel_spmd(nc, [{n + "_dram": z for n, z in arrays.items()}], core_ids=[0])
    return r.results[0]["out_dram"].reshape(1, SEQ, D)
```
